# Optimizing a Trainium2 kernel written in Bass

```python
import jax, jax.numpy as jnp
from jax import lax
import numpy as np
import jax
import jax.numpy as jnp

D_MODEL = 1024
BATCH = 1
SEQ = 512
DEPTH = 1

N_Q_HEADS = 8
N_KV_HEADS = 2
HEAD_DIM = 64
Q_GROUP = N_Q_HEADS // N_KV_HEADS
ATT_WIDTH = N_Q_HEADS * HEAD_DIM
KV_WIDTH = N_KV_HEADS * HEAD_DIM
WINDOW = 128
ATT_BLOCK = 128
SGU_WIDTH = D_MODEL // 2
SGU_GROUPS = 8
SGU_GROUP_DIM = SGU_WIDTH // SGU_GROUPS
SGU_CHUNK = 128
N_BRANCHES = 2
IN_WIDTH = ATT_WIDTH + 2 * KV_WIDTH + 2 * SGU_WIDTH + N_BRANCHES * D_MODEL
D_FF = 256 * ((8 * D_MODEL // 3 + 255) // 256)
CONV_WIDTH = 3
NORM_EPS = 1e-6
NEG_INF = -1e30


def rmsnorm(x, gain):
    xf = x.astype(jnp.float32)
    y = xf * lax.rsqrt(jnp.mean(xf * xf, axis=-1, keepdims=True) + NORM_EPS)
    return (y * gain.astype(jnp.float32)).astype(x.dtype)

def alibi_slopes():
    return jnp.exp2(-8.0 * (jnp.arange(N_Q_HEADS, dtype=jnp.float32) + 1.0) / N_Q_HEADS)

def sliding_window_attention(q, k, v, q_gain, k_gain, sinks):
    B, S, _ = q.shape
    nb = S // ATT_BLOCK
    q = rmsnorm(q.reshape(B, S, N_Q_HEADS, HEAD_DIM), q_gain)
    k = rmsnorm(k.reshape(B, S, N_KV_HEADS, HEAD_DIM), k_gain)
    v = v.reshape(B, S, N_KV_HEADS, HEAD_DIM)
    qb = q.reshape(B, nb, ATT_BLOCK, N_KV_HEADS, Q_GROUP, HEAD_DIM)

    def band(t):
        tp = jnp.pad(t, ((0, 0), (ATT_BLOCK, 0), (0, 0), (0, 0)))
        tp = tp.reshape(B, nb + 1, ATT_BLOCK, N_KV_HEADS, HEAD_DIM)
        return jnp.concatenate([tp[:, :-1], tp[:, 1:]], axis=2)

    kb, vb = band(k), band(v)
    scores = jnp.einsum('bnqhgd,bnkhd->bnhgqk', qb, kb,
                        preferred_element_type=jnp.float32) * (HEAD_DIM ** -0.5)
    qi = jnp.arange(ATT_BLOCK)[:, None]
    kj = jnp.arange(2 * ATT_BLOCK)[None, :]
    dist = qi + ATT_BLOCK - kj
    key_pos = jnp.arange(nb)[:, None] * ATT_BLOCK - ATT_BLOCK + kj
    valid = ((dist >= 0) & (dist < WINDOW))[None] & (key_pos >= 0)[:, None, :]
    slopes = alibi_slopes().reshape(N_KV_HEADS, Q_GROUP)
    alibi = -slopes[:, :, None, None] * dist.astype(jnp.float32)[None, None]
    scores = jnp.where(valid[None, :, None, None], scores + alibi[None, None], NEG_INF)
    sink = jnp.broadcast_to(
        sinks.astype(jnp.float32).reshape(1, 1, N_KV_HEADS, Q_GROUP, 1, 1),
        scores.shape[:-1] + (1,))
    probs = jax.nn.softmax(jnp.concatenate([scores, sink], axis=-1), axis=-1)[..., :-1]
    out = jnp.einsum('bnhgqk,bnkhd->bnqhgd', probs.astype(v.dtype), vb)
    return out.reshape(B, S, ATT_WIDTH)

def chunked_spatial_gating(u, v, sgu_gain, w_s, b_s):
    B, S, _ = u.shape
    nc = S // SGU_CHUNK
    u = jax.nn.gelu(u)
    v = rmsnorm(jax.nn.gelu(v), sgu_gain)
    vc = v.reshape(B, nc, SGU_CHUNK, SGU_GROUPS, SGU_GROUP_DIM)
    causal = jnp.tril(jnp.ones((SGU_CHUNK, SGU_CHUNK), dtype=bool))
    w = jnp.where(causal[None], w_s, 0)
    mixed = jnp.einsum('gij,bcjgd->bcigd', w, vc) + b_s.T[:, :, None]
    return u * mixed.reshape(B, S, SGU_WIDTH)

def conv_gated_mlp(h, w_up, conv_w, conv_b, w_down):
    S = h.shape[1]
    z = h @ w_up
    zp = jnp.pad(z, ((0, 0), (CONV_WIDTH - 1, 0), (0, 0)))
    zc = conv_b
    for tap in range(CONV_WIDTH):
        zc = zc + conv_w[tap] * zp[:, tap:tap + S]
    gate, val = jnp.split(zc, 2, axis=-1)
    return (jax.nn.silu(gate) * val) @ w_down

def first_inputs(seed: int = 0) -> dict:
    key = jax.random.key(seed)
    ks = jax.random.split(key, 20)
    f32 = jnp.float32

    def nrm(k, shape, scale):
        return jax.random.normal(k, shape, f32) * scale

    return {
        "x": nrm(ks[0], (BATCH, SEQ, D_MODEL), 1.0),
        "mix_norm": 1.0 + nrm(ks[1], (DEPTH, D_MODEL), 0.05),
        "w_in": nrm(ks[2], (DEPTH, D_MODEL, IN_WIDTH), D_MODEL ** -0.5),
        "q_norm": 1.0 + nrm(ks[3], (DEPTH, HEAD_DIM), 0.05),
        "k_norm": 1.0 + nrm(ks[4], (DEPTH, HEAD_DIM), 0.05),
        "sinks": nrm(ks[5], (DEPTH, N_Q_HEADS), 0.5),
        "sgu_norm": 1.0 + nrm(ks[6], (DEPTH, SGU_WIDTH), 0.05),
        "w_s": nrm(ks[7], (DEPTH, SGU_GROUPS, SGU_CHUNK, SGU_CHUNK), SGU_CHUNK ** -0.5),
        "b_s": 1.0 + nrm(ks[8], (DEPTH, SGU_GROUPS, SGU_CHUNK), 0.1),
        "w_oa": nrm(ks[9], (DEPTH, ATT_WIDTH, D_MODEL), ATT_WIDTH ** -0.5),
        "w_ob": nrm(ks[10], (DEPTH, SGU_WIDTH, D_MODEL), SGU_WIDTH ** -0.5),
        "w_out": nrm(ks[11], (DEPTH, D_MODEL, D_MODEL), D_MODEL ** -0.5),
        "ffn_norm": 1.0 + nrm(ks[12], (DEPTH, D_MODEL), 0.05),
        "w_up": nrm(ks[13], (DEPTH, D_MODEL, 2 * D_FF), D_MODEL ** -0.5),
        "conv_w": nrm(ks[14], (DEPTH, CONV_WIDTH, 2 * D_FF), CONV_WIDTH ** -0.5),
        "conv_b": nrm(ks[15], (DEPTH, 2 * D_FF), 0.02),
        "w_down": nrm(ks[16], (DEPTH, D_FF, D_MODEL), D_FF ** -0.5),
    }

def first_block(x, mix_norm, w_in, q_norm, k_norm, sinks, sgu_norm, w_s, b_s,
              w_oa, w_ob, w_out, ffn_norm, w_up, conv_w, conv_b, w_down):
    splits = (ATT_WIDTH,
              ATT_WIDTH + KV_WIDTH,
              ATT_WIDTH + 2 * KV_WIDTH,
              ATT_WIDTH + 2 * KV_WIDTH + SGU_WIDTH,
              ATT_WIDTH + 2 * KV_WIDTH + 2 * SGU_WIDTH,
              ATT_WIDTH + 2 * KV_WIDTH + 2 * SGU_WIDTH + D_MODEL)
    for l in range(DEPTH):
        h = rmsnorm(x, mix_norm[l])
        proj = h @ w_in[l]
        q, k, v, su, sv, g_a, g_b = jnp.split(proj, splits, axis=-1)
        y_att = sliding_window_attention(q, k, v, q_norm[l], k_norm[l], sinks[l])
        y_sgu = chunked_spatial_gating(su, sv, sgu_norm[l], w_s[l], b_s[l])
        merged = (jax.nn.sigmoid(g_a) * (y_att @ w_oa[l])
                  + jax.nn.sigmoid(g_b) * (y_sgu @ w_ob[l]))
        x = x + merged @ w_out[l]
        x = x + conv_gated_mlp(rmsnorm(x, ffn_norm[l]), w_up[l], conv_w[l], conv_b[l], w_down[l])
    return x


N_META = 16
GRID_W = 64
EPS = 1e-6

MLA_HEADS = 8
MLA_NOPE = 128
MLA_ROPE = 64
MLA_V = 128
MLA_Q_RANK = 256
MLA_KV_RANK = 256
MLA_WIDTH = MLA_HEADS * MLA_V
ROPE_BASE = 10000.0
Q_BLOCK = 128

NA_HEADS = 16
NA_HEAD_DIM = 64
NA_WIDTH = NA_HEADS * NA_HEAD_DIM
NA_WIN_R = 8
NA_WIN_C = 16

D_INNER = MLA_WIDTH + NA_WIDTH
IN_SIZES = (MLA_Q_RANK, MLA_KV_RANK, MLA_ROPE, MLA_WIDTH, NA_WIDTH, NA_WIDTH, NA_WIDTH, NA_WIDTH)
D_IN_PROJ = sum(IN_SIZES)


def _rmsnorm(x, w):
    xf = x.astype(jnp.float32)
    y = xf * lax.rsqrt(jnp.mean(xf * xf, axis=-1, keepdims=True) + EPS)
    return (y * w.astype(jnp.float32)).astype(x.dtype)

def _rope(x, cos, sin):
    x1, x2 = jnp.split(x.astype(jnp.float32), 2, axis=-1)
    return jnp.concatenate([x1 * cos - x2 * sin, x2 * cos + x1 * sin], axis=-1).astype(x.dtype)

def _mla(q_lat, kv_lat, k_pe, w_uq, w_ukv, q_lat_w, kv_lat_w, qn_w, qpe_w, kn_w, kpe_w):
    B, L, _ = q_lat.shape
    q = (_rmsnorm(q_lat, q_lat_w) @ w_uq).reshape(B, L, MLA_HEADS, MLA_NOPE + MLA_ROPE)
    kv = (_rmsnorm(kv_lat, kv_lat_w) @ w_ukv).reshape(B, L, MLA_HEADS, MLA_NOPE + MLA_V)
    q_nope, q_pe = q[..., :MLA_NOPE], q[..., MLA_NOPE:]
    k_nope, v = kv[..., :MLA_NOPE], kv[..., MLA_NOPE:]
    q_nope = _rmsnorm(q_nope, qn_w)
    k_nope = _rmsnorm(k_nope, kn_w)
    pos = jnp.arange(L, dtype=jnp.float32)
    inv_freq = ROPE_BASE ** (-(jnp.arange(0, MLA_ROPE, 2, dtype=jnp.float32) / MLA_ROPE))
    ang = pos[:, None] * inv_freq[None, :]
    cos, sin = jnp.cos(ang), jnp.sin(ang)
    q_pe = _rope(_rmsnorm(q_pe, qpe_w), cos[None, :, None, :], sin[None, :, None, :])
    k_pe = _rope(_rmsnorm(k_pe, kpe_w), cos[None], sin[None])
    scale = (MLA_NOPE + MLA_ROPE) ** -0.5

    n_blk = -(-L // Q_BLOCK)
    pad = n_blk * Q_BLOCK - L
    qn = jnp.pad(q_nope, ((0, 0), (0, pad), (0, 0), (0, 0)))
    qn = qn.reshape(B, n_blk, Q_BLOCK, MLA_HEADS, MLA_NOPE).transpose(1, 0, 2, 3, 4)
    qp = jnp.pad(q_pe, ((0, 0), (0, pad), (0, 0), (0, 0)))
    qp = qp.reshape(B, n_blk, Q_BLOCK, MLA_HEADS, MLA_ROPE).transpose(1, 0, 2, 3, 4)

    def block(args):
        qn_b, qp_b = args
        s = (jnp.einsum('bqhd,bkhd->bhqk', qn_b, k_nope)
             + jnp.einsum('bqhr,bkr->bhqk', qp_b, k_pe))
        p = jax.nn.softmax(s.astype(jnp.float32) * scale, axis=-1).astype(v.dtype)
        return jnp.einsum('bhqk,bkhd->bqhd', p, v)

    o = lax.map(block, (qn, qp))
    o = o.transpose(1, 0, 2, 3, 4).reshape(B, n_blk * Q_BLOCK, MLA_WIDTH)
    return o[:, :L]

def _na(q, k, v, q_w, k_w, rel_bias, meta_bias):
    B, L, _ = q.shape
    n_real = L - N_META
    rows = n_real // GRID_W
    win_r = min(NA_WIN_R, rows)
    n_win = win_r * NA_WIN_C
    scale = NA_HEAD_DIM ** -0.5
    q = _rmsnorm(q.reshape(B, L, NA_HEADS, NA_HEAD_DIM), q_w)
    k = _rmsnorm(k.reshape(B, L, NA_HEADS, NA_HEAD_DIM), k_w)
    v = v.reshape(B, L, NA_HEADS, NA_HEAD_DIM)
    q_meta, k_meta, v_meta = q[:, :N_META], k[:, :N_META], v[:, :N_META]
    q_grid = q[:, N_META:].reshape(B, rows, GRID_W, NA_HEADS, NA_HEAD_DIM)
    k_grid = k[:, N_META:].reshape(B, rows, GRID_W, NA_HEADS, NA_HEAD_DIM)
    v_grid = v[:, N_META:].reshape(B, rows, GRID_W, NA_HEADS, NA_HEAD_DIM)

    cols = np.arange(GRID_W)
    c0 = np.clip(cols - NA_WIN_C // 2, 0, GRID_W - NA_WIN_C)
    col_idx_np = c0[:, None] + np.arange(NA_WIN_C)[None, :]
    col_idx = jnp.asarray(col_idx_np, dtype=jnp.int32)
    dc_idx = jnp.asarray(col_idx_np - cols[:, None] + (NA_WIN_C - 1), dtype=jnp.int32)
    meta_b = meta_bias.astype(jnp.float32)[None, :, None, :]

    def row_block(args):
        r, q_row = args
        r0 = jnp.clip(r - win_r // 2, 0, rows - win_r)
        k_rows = lax.dynamic_slice_in_dim(k_grid, r0, win_r, axis=1)
        v_rows = lax.dynamic_slice_in_dim(v_grid, r0, win_r, axis=1)
        k_win = k_rows[:, :, col_idx]
        v_win = v_rows[:, :, col_idx]
        dr_idx = r0 + jnp.arange(win_r, dtype=jnp.int32) - r + (NA_WIN_R - 1)
        bias = rel_bias[:, dr_idx[None, :, None], dc_idx[:, None, :]]
        s_win = (jnp.einsum('bqhd,brqchd->bhqrc', q_row, k_win).astype(jnp.float32) * scale
                 + bias.astype(jnp.float32)[None])
        s_meta = jnp.einsum('bqhd,bmhd->bhqm', q_row, k_meta).astype(jnp.float32) * scale + meta_b
        s = jnp.concatenate([s_win.reshape(B, NA_HEADS, GRID_W, n_win), s_meta], axis=-1)
        p = jax.nn.softmax(s, axis=-1).astype(v.dtype)
        p_win = p[..., :n_win].reshape(B, NA_HEADS, GRID_W, win_r, NA_WIN_C)
        p_meta = p[..., n_win:]
        return (jnp.einsum('bhqrc,brqchd->bqhd', p_win, v_win)
                + jnp.einsum('bhqm,bmhd->bqhd', p_meta, v_meta))

    o_grid = lax.map(row_block, (jnp.arange(rows, dtype=jnp.int32), q_grid.transpose(1, 0, 2, 3, 4)))
    o_real = o_grid.transpose(1, 0, 2, 3, 4).reshape(B, n_real, NA_WIDTH)

    s_mm = jnp.einsum('bqhd,bmhd->bhqm', q_meta, k_meta).astype(jnp.float32) * scale + meta_b
    p_mm = jax.nn.softmax(s_mm, axis=-1).astype(v.dtype)
    o_meta = jnp.einsum('bhqm,bmhd->bqhd', p_mm, v_meta).reshape(B, N_META, NA_WIDTH)
    return jnp.concatenate([o_meta, o_real], axis=1)

def second_inputs(seed: int = 0) -> dict:
    key = jax.random.key(seed)
    ks = jax.random.split(key, 20)
    f32 = jnp.float32

    def nrm(k, shape, scale):
        return jax.random.normal(k, shape, f32) * scale

    def gain(k, shape):
        return 1.0 + 0.05 * jax.random.normal(k, shape, f32)

    return {
        "x": jax.random.normal(ks[0], (BATCH, SEQ, D_MODEL), f32),
        "meta_tokens": nrm(ks[1], (N_META, D_MODEL), 1.0),
        "norm_w": gain(ks[2], (DEPTH, D_MODEL)),
        "w_in": nrm(ks[3], (DEPTH, D_MODEL, D_IN_PROJ), D_MODEL ** -0.5),
        "q_lat_norm_w": gain(ks[4], (DEPTH, MLA_Q_RANK)),
        "kv_lat_norm_w": gain(ks[5], (DEPTH, MLA_KV_RANK)),
        "w_uq": nrm(ks[6], (DEPTH, MLA_Q_RANK, MLA_HEADS * (MLA_NOPE + MLA_ROPE)), MLA_Q_RANK ** -0.5),
        "w_ukv": nrm(ks[7], (DEPTH, MLA_KV_RANK, MLA_HEADS * (MLA_NOPE + MLA_V)), MLA_KV_RANK ** -0.5),
        "mla_qn_w": gain(ks[8], (DEPTH, MLA_NOPE)),
        "mla_qpe_w": gain(ks[9], (DEPTH, MLA_ROPE)),
        "mla_kn_w": gain(ks[10], (DEPTH, MLA_NOPE)),
        "mla_kpe_w": gain(ks[11], (DEPTH, MLA_ROPE)),
        "na_q_norm_w": gain(ks[12], (DEPTH, NA_HEAD_DIM)),
        "na_k_norm_w": gain(ks[13], (DEPTH, NA_HEAD_DIM)),
        "na_rel_bias": nrm(ks[14], (DEPTH, NA_HEADS, 2 * NA_WIN_R - 1, 2 * NA_WIN_C - 1), 0.5),
        "na_meta_bias": nrm(ks[15], (DEPTH, NA_HEADS, N_META), 0.5),
        "w_out": nrm(ks[16], (DEPTH, D_INNER, D_MODEL), D_INNER ** -0.5),
    }

def second_block(x, meta_tokens, norm_w, w_in, q_lat_norm_w, kv_lat_norm_w, w_uq, w_ukv,
              mla_qn_w, mla_qpe_w, mla_kn_w, mla_kpe_w, na_q_norm_w, na_k_norm_w,
              na_rel_bias, na_meta_bias, w_out):
    B = x.shape[0]
    meta = jnp.broadcast_to(meta_tokens.astype(x.dtype)[None], (B, N_META, D_MODEL))
    h_res = jnp.concatenate([meta, x], axis=1)
    split_at = [int(s) for s in np.cumsum(IN_SIZES)[:-1]]
    for l in range(DEPTH):
        h = _rmsnorm(h_res, norm_w[l])
        proj = h @ w_in[l]
        q_lat, kv_lat, k_pe, g_mla, na_q, na_k, na_v, g_na = jnp.split(proj, split_at, axis=-1)
        y_mla = _mla(q_lat, kv_lat, k_pe, w_uq[l], w_ukv[l], q_lat_norm_w[l], kv_lat_norm_w[l],
                     mla_qn_w[l], mla_qpe_w[l], mla_kn_w[l], mla_kpe_w[l]) * jax.nn.silu(g_mla)
        y_na = _na(na_q, na_k, na_v, na_q_norm_w[l], na_k_norm_w[l],
                   na_rel_bias[l], na_meta_bias[l]) * jax.nn.silu(g_na)
        h_res = h_res + jnp.concatenate([y_mla, y_na], axis=-1) @ w_out[l]
    return h_res[:, N_META:]


def setup_inputs(seed=0):
    out = dict(first_inputs(seed))
    for name, value in second_inputs(seed + 1).items():
        if name != "x":
            out[name + "_2"] = value
    return out


def reference(
    x, mix_norm, w_in, q_norm, k_norm, sinks, sgu_norm, w_s, b_s, w_oa, w_ob, w_out, ffn_norm,
    w_up, conv_w, conv_b, w_down, meta_tokens_2, norm_w_2, w_in_2, q_lat_norm_w_2,
    kv_lat_norm_w_2, w_uq_2, w_ukv_2, mla_qn_w_2, mla_qpe_w_2, mla_kn_w_2, mla_kpe_w_2,
    na_q_norm_w_2, na_k_norm_w_2, na_rel_bias_2, na_meta_bias_2, w_out_2,
):
    x = first_block(
        x, mix_norm, w_in, q_norm, k_norm, sinks, sgu_norm, w_s, b_s, w_oa, w_ob, w_out,
        ffn_norm, w_up, conv_w, conv_b, w_down,
    )
    return second_block(
        x, meta_tokens_2, norm_w_2, w_in_2, q_lat_norm_w_2, kv_lat_norm_w_2, w_uq_2, w_ukv_2,
        mla_qn_w_2, mla_qpe_w_2, mla_kn_w_2, mla_kpe_w_2, na_q_norm_w_2, na_k_norm_w_2,
        na_rel_bias_2, na_meta_bias_2, w_out_2,
    )


_drawn_inputs = setup_inputs


def setup_inputs(seed=0):
    import zlib

    import numpy as np

    out = dict(_drawn_inputs(seed))
    spreads = {}
    factors = {'q_norm': 7.686,
     'k_norm': 8.0,
     'sinks': 22.154,
     'sgu_norm': 4.438,
     'conv_b': 4.075,
     'meta_tokens_2': 3.235,
     'norm_w_2': 8.0,
     'q_lat_norm_w_2': 8.0,
     'kv_lat_norm_w_2': 8.0,
     'mla_qn_w_2': 8.0,
     'mla_qpe_w_2': 8.0,
     'mla_kn_w_2': 8.0,
     'mla_kpe_w_2': 8.0,
     'na_q_norm_w_2': 8.0,
     'na_k_norm_w_2': 8.0,
     'na_meta_bias_2': 7.627}
    for name, (base, spread) in spreads.items():
        noise = np.random.default_rng([zlib.crc32(name.encode()), seed]).standard_normal(out[name].shape)
        drawn = base * np.exp(spread * noise) if base else spread * noise
        out[name] = jnp.asarray(drawn.astype(out[name].dtype))
    for name, factor in factors.items():
        out[name] = (out[name] * factor).astype(out[name].dtype)
    return out
```

```python
from contextlib import ExitStack

import numpy as np

import concourse.bass as bass
from concourse import mybir

ACT = mybir.ActivationFunctionType
ALU = mybir.AluOpType
AX = mybir.AxisListType
F32 = mybir.dt.float32
F32R = mybir.dt.float32r

P = 128
D = 1024
KT = D // P
S = 512
META = 16
L = S + META
HALF = L // 2
EPS = 1e-6
ATT_H, KV_H, HD = 8, 2, 64
SGU = 512
FF = 2816
FT = FF // P
MH = 8
MLA_SCALE = 192.0 ** -0.5
NH = 16
GW = 64
CG = 4

N_SGU = 0
N_QKV = N_SGU + 8
N_GATE = N_QKV + 6
N_MERGE = N_GATE + 16
N_OUT = N_MERGE + 8
N_UP = N_OUT + 8
N_DOWN = N_UP + 2 * FT
N_GM = N_DOWN + 3 * KT
N_LAT = N_GM + 8
N_MLA = N_LAT + 5
N_OM = N_MLA + 16
N_NA = N_OM + 8
N_ON = N_NA + 32
N_END = N_ON + 8
RAW = 2
RING = 4

V_MIX, V_FFN, V_N2, V_QL, V_KL, V_QN, V_KN, V_SGU = 0, 8, 16, 24, 26, 28, 29, 30
V_AQ, V_AK, V_NQ, V_NK, V_QPE, V_KPE, V_ROWS = 34, 35, 36, 37, 38, 39, 40
C_CONV, C_CONVB = 0, 3 * 2 * FT
C_V = C_CONVB + 2 * FT

NA_W = [2 * P, 3 * P, 3 * P, 2 * P]
NA_G = [0, 0, 1, 2]
NA_OFF = [META + 3 * P, 0, 0, 2 * META + 5 * P]
NA_COLS = 3 * META + 7 * P
MASK_OFF = [3 * P, 0, 0, 5 * P]
MASK_COLS = 7 * P


def program(nc, x, mix_norm, w_in, q_norm, k_norm, sinks, sgu_norm, w_s, b_s, w_oa, w_ob, w_out,
            ffn_norm, w_up, conv_w, conv_b, w_down, meta_tokens_2, norm_w_2, w_in_2,
            q_lat_norm_w_2, kv_lat_norm_w_2, w_uq_2, w_ukv_2, mla_qn_w_2, mla_qpe_w_2, mla_kn_w_2,
            mla_kpe_w_2, na_q_norm_w_2, na_k_norm_w_2, na_meta_bias_2, w_out_2, rel_bias,
            c_ident, c_blocks, c_rot, c_cos, c_sin, c_dist, c_slope, c_mask, out):
    with ExitStack() as ctx:
        def sb(name, shape, dt=F32, at=ctx):
            return at.enter_context(nc.sbuf_tensor(name, shape, dt))

        def sem(name):
            return ctx.enter_context(nc.semaphore(name))

        ident = sb("ident", [P, P])
        ones = sb("ones", [P, P])
        blocks = sb("blocks", [P, P])
        rot = sb("rot", [P, P])
        eps = sb("eps", [P, 1])
        cv = sb("cv", [P, C_V + V_ROWS])
        aq_gain = sb("aq_gain", [P, 1])
        nq_gain = sb("nq_gain", [P, 1])
        x_t = sb("x_t", [P, KT, S])
        h_high = sb("h_high", [P, KT, L], F32R)
        h_low = sb("h_low", [P, KT, L], F32R)
        w_raw = sb("w_raw", [P, RAW, KT * P])
        w_high = sb("w_high", [P, RING, KT * P], F32R)
        w_low = sb("w_low", [P, RING, KT * P], F32R)
        with ExitStack() as one:
            sq = sb("sq", [P, 2, L], F32, one)
            root = sb("root", [P, 2, L], F32, one)
            scaled = sb("scaled", [P, 2, S], F32, one)
            a_high = sb("a_high", [P, 8, S], F32R, one)
            a_low = sb("a_low", [P, 8, S], F32R, one)
            bias_s = sb("bias_s", [P, 4, P], F32, one)
            dist = sb("dist", [P, 2 * P], F32, one)
            slope = sb("slope", [P, ATT_H], F32, one)
            sink = sb("sink", [P, ATT_H], F32, one)
            k_t = sb("k_t", [P, S], F32, one)
            q_t = sb("q_t", [P, 4, S], F32, one)
            v_f = sb("v_f", [P, S], F32, one)
            v_tok = sb("v_tok", [P, 4, P], F32, one)
            with ExitStack() as a:
                x_tok = sb("x_tok", [P, 4, D], F32, a)
                meta_tok = sb("meta_tok", [META, D], F32, a)
                meta_t = sb("meta_t", [P, KT, META], F32, a)
                rows_a = sb("rows_a", [4 * FT, P], F32, a)
                rows_b = sb("rows_b", [4 * FT, P], F32, a)
                rows_v = sb("rows_v", [V_ROWS, P], F32, a)
            with ExitStack() as a:
                uv = sb("uv", [P, 8, S], F32, a)
                uv_tok = sb("uv_tok", [P, 4, SGU], F32, a)
            with ExitStack() as a:
                gates = sb("gates", [P, 16, S], F32, a)
                ws_raw = sb("ws_raw", [P, 8, P], F32, a)
                ws_t = sb("ws_t", [P, 8, P], F32, a)
            with ExitStack() as a:
                a.enter_context(nc.sbuf_tensor("gates_", [P, 16, S], F32))
                q_st = sb("q_st", [P, S], F32, a)
                bias_h = sb("bias_h", [P, 2, 2 * P], F32, a)
                att_e = sb("att_e", [P, 2, 2 * P], F32, a)
                att_p = sb("att_p", [P, 4, P], F32, a)
                att_m = sb("att_m", [P, 6, 2], F32, a)
                att_y = sb("att_y", [P, S], F32, a)
            merge = scaled
        with ExitStack() as two:
            m_high = sb("m_high", [P, FT, S], F32R, two)
            m_low = sb("m_low", [P, FT, S], F32R, two)
            z = sb("z", [P, 4, S], F32, two)
            zg = sb("zg", [P, 2, S], F32, two)
        with ExitStack() as three:
            sq2 = sb("sq2", [P, 2, L], F32, three)
            root2 = sb("root2", [P, 2, L], F32, three)
            scaled2 = sb("scaled2", [P, 2, L], F32, three)
            y_high = sb("y_high", [P, 8, S], F32R, three)
            y_low = sb("y_low", [P, 8, S], F32R, three)
            y_f = sb("y_f", [P, S], F32, three)
            with ExitStack() as a:
                cos = sb("cos", [P, L], F32, a)
                sin = sb("sin", [P, L], F32, a)
                gm = sb("gm", [P, MH, S], F32, a)
                ql_high = sb("ql_high", [P, 2, S], F32R, a)
                ql_low = sb("ql_low", [P, 2, S], F32R, a)
                kl_high = sb("kl_high", [P, 2, L], F32R, a)
                kl_low = sb("kl_low", [P, 2, L], F32R, a)
                k_pe = sb("k_pe", [P, L], F32, a)
                q_pe = sb("q_pe", [P, S], F32, a)
                kn = sb("kn", [P, 2, L], F32, a)
                qn = sb("qn", [P, 2, S], F32, a)
                me = sb("me", [P, 2, L], F32, a)
                mv = sb("mv", [P, 5, 2 * P], F32, a)
                mp = sb("mp", [P, 5 * P], F32, a)
                mm_ = sb("mm_", [P, 2, 4], F32, a)
                mvf = sq2
            with ExitStack() as a:
                mask = sb("mask", [P, MASK_COLS], F32, a)
                meta_b = sb("meta_b", [P, NH * META], F32, a)
                rel = sb("rel", [P, 2, 3 * P], F32, a)
                nb = sb("nb", [P, 2, NA_COLS], F32, a)
                nk = sb("nk", [P, L], F32, a)
                nq = sb("nq", [P, S], F32, a)
                nvf = sb("nvf", [P, L], F32, a)
                nv = sb("nv", [P, 5, P], F32, a)
                ng = sb("ng", [P, 2, S], F32, a)
                ne = sb("ne", [P, 2, 2, META + 3 * P], F32, a)
                npt = sb("npt", [P, 4, 2 * P], F32, a)
                nm = sb("nm", [P, 2, 3, 2], F32, a)
            with ExitStack() as a:
                y_tok = sb("y_tok", [P, 4, D], F32, a)
        ps = ctx.enter_context(nc.psum_tensor("ps", [P, 8, 512], F32))

        def wide(bank):
            return ps[:, bank:bank + 2, 0:HALF]

        def halves(ap):
            return ap.rearrange("p (h c) -> p h c", h=2)

        landed = [sem(f"strip_landed_{i}") for i in range(RAW)]
        high_made = sem("high_made")
        low_made = sem("low_made")
        strip_used = sem("strip_used")

        def strip_sources(n, i):
            def cols(w, c, k0=0, kn=KT):
                v = w[0].rearrange("(k p) c -> p k c", p=P)
                h = (kn + 1) // 2
                return [(slice(0, P), (a, b), P, v[:, k0 + a:k0 + b, bass.ds(c, P)])
                        for a, b in ((0, h), (h, kn))]
            if n < N_QKV:
                return cols(w_in, (n - N_SGU + i) * P + 768)
            if n < N_GATE:
                m = n - N_QKV
                if m < 2:
                    return cols(w_in, 512 + m * P)
                v = w_in[0].rearrange("(k p) c -> p k c", p=P)
                return [("c", g * HD, HD, v[:, :, g * 256 + (m - 2) * HD:g * 256 + (m - 1) * HD])
                        for g in range(2)]
            if n < N_MERGE:
                return cols(w_in, (n - N_GATE + i) * P + 1792)
            if n < N_OUT:
                m = n - N_MERGE
                c = i * P + ((m - m % 4) * P + (m % 4) // 2 * 256)
                if m % 2 == 0:
                    v = w_oa[0].rearrange("(g j d) c -> g d j c", g=2, d=HD)
                    return [(slice(g * HD, g * HD + HD), (0, 4), 256, v[g][:, :, bass.ds(c, 256)])
                            for g in range(2)]
                v = w_ob[0].rearrange("(k p) c -> p k c", p=P)
                return [(slice(0, P), (a, a + 2), 256, v[:, a:a + 2, bass.ds(c, 256)]) for a in (0, 2)]
            if n < N_UP:
                return cols(w_out, (n - N_OUT + i) * P)
            if n < N_DOWN:
                m = n - N_UP
                c = ((m - m % 4) // 2 + m % 2) * P + (m % 4) // 2 * FF
                return cols(w_up, i * (P // 2) + c)
            if n < N_GM:
                m, part = divmod(n - N_DOWN, 3)
                return cols(w_down, i * P + m * P, 8 * part, 8 if part < 2 else 6)
            if n < N_LAT:
                return cols(w_in_2, (n - N_GM + i) * P + 576)
            if n < N_MLA:
                m = n - N_LAT
                if m < 4:
                    return cols(w_in_2, m * P)
                v = w_in_2[0].rearrange("(k p) c -> p k c", p=P)
                return [("c", g * 64, 64, v[:, :, 512:576]) for g in range(2)]
            if n < N_OM:
                m = n - N_MLA
                pair = (m - m % 4) // 4
                s = m % 4
                w, head, off, width = ((w_ukv_2, 256, 0, P), (w_uq_2, 192, 0, P), (w_uq_2, 192, P, 64),
                                       (w_ukv_2, 256, P, P))[s]
                v = w[0].rearrange("(k p) c -> p k c", p=P)
                base = i * (head // 2) + pair * 2 * head + off
                return [("h", h * width, (2, 2 * width), v[:, :, bass.ds(base + h * head, width)])
                        for h in range(2)]
            if n < N_NA:
                return cols(w_out_2, (n - N_OM + i) * P)
            if n < N_ON:
                m = n - N_NA
                pair, s = (m - m % 4) // 4, m % 4
                c = (2624, 1600, 3648, 4672)[s]
                return cols(w_in_2, i * (P // 4) + pair * P + c)
            return cols(w_out_2, (n - N_ON + i) * P, KT)

        def load_strip(sp, n, i=0):
            if n >= RAW:
                sp.wait_ge(low_made, i + (n - RAW + 1))
            slot = w_raw[:, n % RAW, :]
            for load in strip_sources(n, i):
                if load[0] == "c":
                    _, c, width, src = load
                    dst = slot.rearrange("p (k c) -> p k c", c=P)[:, :, c:c + width]
                elif load[0] == "h":
                    _, c, (k, row), src = load
                    dst = slot[:, 0:k * row].rearrange("p (k c) -> p k c", k=k)[:, :, c:c + row // 2]
                else:
                    rows, (a, b), width, src = load
                    dst = slot.rearrange("p (k c) -> p k c", c=width)[rows, a:b, :]
                sp.dma_start(dst, src).then_inc(landed[n % RAW], 16)

        def make_high(dve, n, i=0):
            if isinstance(i, int) and n + i >= N_END:
                return
            dve.wait_ge(landed[n % RAW], i * 16 + 32 * (n // RAW + 1))
            if n >= RING:
                dve.wait_ge(strip_used, i + (n - RING + 1))
            dve.tensor_copy(w_high[:, n % RING, :], w_raw[:, n % RAW, :]).then_inc(high_made, 1)

        def make_low(pool, n, i=0):
            pool.wait_ge(high_made, i + (n + 1))
            pool.tensor_tensor(w_low[:, n % RING, :], w_raw[:, n % RAW, :],
                               w_high[:, n % RING, :].bitcast(F32), ALU.subtract).then_inc(low_made, 1)

        def product(pe, acc, n, col, step, tiles, moving, first=True, last=True):
            for k in range(tiles):
                c = col + k * step
                wh, wl = w_high[:, n % RING, c:c + P], w_low[:, n % RING, c:c + P]
                mh, ml = moving(k)
                pe.matmul(acc, wh, mh, start=first and k == 0, stop=False)
                pe.matmul(acc, wh, ml, start=False, stop=False)
                done = pe.matmul(acc, wl, mh, start=False, stop=last and k == tiles - 1)
            return done

        def product_wide(pe, bank, n, col, step, tiles, high, low):
            for k in range(tiles):
                c = col + k * step
                wh, wl = w_high[:, n % RING, c:c + P], w_low[:, n % RING, c:c + P]
                for wt, mt, one_, end in ((wh, high, k == 0, False), (wh, low, False, False),
                                          (wl, high, False, k == tiles - 1)):
                    for h in range(2):
                        done = pe.matmul(ps[:, bank + h, 0:HALF], wt, mt[:, k, h * HALF:h * HALF + HALF],
                                         start=one_, stop=end)
            return done

        def hx(k):
            return h_high[:, k, META:L], h_low[:, k, META:L]

        names = """consts_in x_in meta_in ones_set x_turned x_ready rows_turned cols_ready gain_ready meta_turned
            meta_ready ws_cut ws_turned ws_ready
            norm_sq norm_sum norm_root norm_scaled norm_high norm_low
            gelu_done sv_sq sv_sum sv_root  sv_normed sv_turned sv_tok_ready mixed mix_biased mix_gated
            mix_high mix_low
            i1_sq i1_sum i1_ln i1_root i1_normed v_copied v_turned v_ready
            j_staged j_bias a_scored a_masked a_part   a_exp a_sink_exp   a_probs a_turned
            a_copied a_summed a_y a_high a_low gate_kept
            g_sig m_part m_whole m_high_ m_low_ o_added
            z_first z_mid z_done z_silu z_gated z_high z_low d_added d_placed
            gm_done lat_sq lat_sum lat_root  lat_scaled lat_high lat_low pe_root_part pe_sum  
            pe_part  pe_turned    tables_in
            p_sq p_kept p_sum p_ln p_root p_normed qr_turned  qr_part  mv_kept mv_turned mv_ready
            s_scored s_top s_neg s_exp s_inv s_probs s_turned s_copied_a s_copied_b s_summed s_y s_high s_low
            om_added rel_in nb_ready
            q_sq q_kept q_sum q_root  q_normed nv_kept nv_turned nv_ready g_exp g_part   
            t_scored t_masked t_neg t_exp t_inv t_probs t_turned t_copied_a t_copied_b t_summed t_y t_high t_low
            on_added out_turned out_left out_right out_stored""".split()
        s = {name: sem(name) for name in names}
        N_CONST = 33

        ends = {
            "setup": [("x_ready", 8), ("gain_ready", 2), ("meta_ready", 1), ("norm_low", 16)],
            "sgu": [("gelu_done", 8)],
            "qkv": [("i1_normed", 5), ("v_ready", 1), ("sv_normed", 4)],
            "mix": [("mix_low", 4), ("sv_tok_ready", 4), ("mixed", 4)],
            "att": [("a_low", 4), ("gate_kept", 16)],
            "merge": [("m_low_", 8)],
            "out": [("o_added", 8)],
            "norm2": [("norm_low", 24)],
            "up": [("z_low", FT)],
            "down": [("d_placed", 8)],
            "norm3": [("norm_low", 32)],
            "gm": [("gm_done", 8)],
            "lat": [("lat_low", 4), ("pe_part", 5)],
            "mla": [("s_low", 8)],
            "om": [("om_added", 8)],
            "na": [("t_low", 8)],
            "on": [("on_added", 8)],
        }

        def after(eng, stage):
            for name, value in ends[stage]:
                eng.wait_ge(s[name], value)

        def col(c):
            return cv[:, C_V + c:C_V + c + 1]

        def norm_pe(pe, t, acc, sq_, n):
            for k in range(KT):
                pe.wait_ge(s["norm_sq"], 8 * t + k + 1)
                pe.matmul(acc, ones[:], sq_[:, k % 2, 0:n], start=k == 0, stop=k == KT - 1)\
                    .then_inc(s["norm_sum"], 1)

        def norm_act(act, t, acc, src, sq_, root_, scaled_, n, high, ready=None):
            for k in range(KT):
                if ready:
                    act.wait_ge(s[ready], k + 1)
                if k >= 2:
                    act.wait_ge(s["norm_sum"], 8 * t + k - 1)
                act.activation(sq_[:, k % 2, 0:n], src(k), ACT.Square).then_inc(s["norm_sq"], 1)
            act.wait_ge(s["norm_sum"], 8 * t + KT)
            act.activation(root_[:, 0, 0:n], acc, ACT.Ln, bias=eps[:, 0:1], scale=1.0 / D).then_inc(s["norm_root"], 1)
            act.wait_ge(s["norm_root"], 2 * t + 1)
            act.activation(root_[:, 0, 0:n], root_[:, 0, 0:n], ACT.Exp, scale=-0.5).then_inc(s["norm_root"], 1)
            for k in range(KT):
                act.wait_ge(s["norm_scaled"], 8 * t + k + 1)
                act.activation(high(k), scaled_[:, k % 2, 0:n], ACT.Copy).then_inc(s["norm_high"], 1)

        def norm_dve(dve, t, src, gain, root_, scaled_, n, high, low):
            dve.wait_ge(s["norm_root"], 2 * t + 2)
            for k in range(KT + 1):
                if k < KT:
                    if k >= 2:
                        dve.wait_ge(s["norm_low"], 8 * t + k - 1)
                    dve.scalar_tensor_tensor(scaled_[:, k % 2, 0:n], src(k), col(gain + k), root_[:, 0, 0:n],
                                             ALU.mult, ALU.mult).then_inc(s["norm_scaled"], 1)
                if k >= 1:
                    dve.wait_ge(s["norm_high"], 8 * t + k)
                    dve.tensor_tensor(low(k - 1), scaled_[:, (k - 1) % 2, 0:n], high(k - 1).bitcast(F32),
                                      ALU.subtract).then_inc(s["norm_low"], 1)

        def xs(k):
            return x_t[:, k, :]

        def hh(k):
            return h_high[:, k, META:L]

        def hl(k):
            return h_low[:, k, META:L]

        block = ctx.enter_context(nc.Block())

        @block.sync
        def _(sp):
            for t in range(4):
                sp.dma_start(x_tok[:, t, :], x[0, t * P:(t + 1) * P, :]).then_inc(s["x_in"], 16)
            for n in range(RAW):
                load_strip(sp, n)
            sp.dma_start(ws_raw[:], w_s[0].rearrange("g i j -> i g j")).then_inc(s["meta_in"], 16)
            for n in range(RAW, 4):
                load_strip(sp, n)
            for n in range(4, N_GATE):
                load_strip(sp, n)
            for n0, n1, step in ((N_GATE, N_MERGE, 4), (N_MERGE, N_OUT, 4), (N_OUT, N_UP, 4), (N_UP, N_DOWN, 4)):
                with sp.Fori(0, (n1 - n0) // step) as turn:
                    i = turn * step
                    for n in range(n0, n0 + step):
                        load_strip(sp, n, i)
            with sp.Fori(0, 2) as i:
                for n in range(N_DOWN, N_DOWN + 12):
                    sp.wait_ge(low_made, i * 12 + (n - RAW + 1))
                    slot = w_raw[:, n % RAW, :].rearrange("p (k c) -> p k c", c=P)
                    for rows, (a, b), width, src in strip_sources(n, i * 4):
                        sp.dma_start(slot[:, a:b, :], src).then_inc(landed[n % RAW], 16)
            with sp.Fori(0, 2) as turn:
                i = turn * 4
                for n in range(N_GM, N_GM + 4):
                    load_strip(sp, n, i)
            after(sp, "down")
            sp.dma_start(cos[:], c_cos).then_inc(s["tables_in"], 16)
            sp.dma_start(sin[:], c_sin).then_inc(s["tables_in"], 16)
            for n in range(N_LAT, N_MLA):
                load_strip(sp, n)
            for n0, n1 in ((N_MLA, N_OM), (N_OM, N_NA)):
                with sp.Fori(0, (n1 - n0) // 4) as turn:
                    i = turn * 4
                    for n in range(n0, n0 + 4):
                        load_strip(sp, n, i)
            after(sp, "mla")
            sp.dma_start(mask[:], c_mask).then_inc(s["tables_in"], 16)
            sp.dma_start(meta_b[:], na_meta_bias_2[0].rearrange("h m -> (h m)").partition_broadcast(P))\
                .then_inc(s["tables_in"], 16)
            with sp.Fori(0, 8) as p:
                for n in range(N_NA, N_NA + 4):
                    load_strip(sp, n, p * 4)
                    if n == N_NA + 2:
                        sp.dma_start(rel[:], rel_bias[bass.ds(p * 2, 2)].rearrange("h q k -> q h k"))\
                            .then_inc(s["rel_in"], 16)
            for n in range(N_ON, N_END):
                load_strip(sp, n)
            for t in range(4):
                sp.wait_ge(s["out_left"], t + 1)
                sp.wait_ge(s["out_right"], t + 1)
                dst = out[0].rearrange("(r g c) d -> g r c d", g=CG, c=16)[t]
                for r in range(8):
                    sp.dma_start(dst[r], y_tok[r * 16:(r + 1) * 16, t, :]).then_inc(s["out_stored"], 16)
            sp.wait_ge(s["out_stored"], 16 * 32)

        @block.gpsimd
        def _(pool):
            nc.gpsimd.memset(ones[:], 1.0).then_inc(s["ones_set"], 1)
            nc.gpsimd.memset(eps[:], EPS).then_inc(s["ones_set"], 1)
            for n in range(0, N_GATE):
                make_low(pool, n)
                if n == 3:
                    pool.wait_ge(s["meta_in"], 16)
                    pool.affine_select(out=ws_raw[:], in_=ws_raw[:], compare_op=ALU.is_ge, fill=0.0, base=0,
                                       pattern=[[0, 8], [-1, P]], channel_multiplier=1).then_inc(s["ws_cut"], 1)
            for n0, n1, step in ((N_GATE, N_MERGE, 4), (N_MERGE, N_OUT, 4), (N_OUT, N_UP, 4), (N_UP, N_DOWN, 4),
                                 (N_DOWN, N_GM, 12), (N_GM, N_LAT, 4)):
                with pool.Fori(0, (n1 - n0) // step) as turn:
                    i = turn * step
                    for n in range(n0, n0 + step):
                        make_low(pool, n, i)
            for n in range(N_LAT, N_MLA):
                make_low(pool, n)
            for n0, n1 in ((N_MLA, N_OM), (N_OM, N_NA)):
                with pool.Fori(0, (n1 - n0) // 4) as turn:
                    i = turn * 4
                    for n in range(n0, n0 + 4):
                        make_low(pool, n, i)
            pool.wait_ge(s["tables_in"], 64)
            with pool.Fori(0, 8) as p:
                for n in range(N_NA, N_NA + 4):
                    make_low(pool, n, p * 4)
                    if n == N_NA + 3:
                        pool.wait_ge(s["rel_in"], p * 16 + 16)
                        pool.wait_ge(s["q_kept"], p * 2 + 1)
                        pool.wait_ge(s["ones_set"], 2)
                        for h in range(2):
                            for o, m, r in ((0, 0, 0), (META + 3 * P, 3 * P, P), (2 * META + 5 * P, 5 * P, 0)):
                                w = 3 * P if o == 0 else 2 * P
                                pool.tensor_tensor(nb[:, h, o + META:o + META + w], rel[:, h, r:r + w],
                                                   mask[:, m:m + w], ALU.add).then_inc(s["nb_ready"], 1)
                        for o in (0, META + 3 * P, 2 * META + 5 * P):
                            pool.tensor_copy(nb[:, :, o:o + META],
                                             meta_b[:, bass.ds(p * 32, 32)].rearrange("p (h m) -> p h m", h=2))\
                                .then_inc(s["nb_ready"], 1)
            for n in range(N_ON, N_END):
                make_low(pool, n)

        @block.tensor
        def _(pe):
            pe.wait_ge(s["consts_in"], 16 * N_CONST)
            pe.transpose(ps[:, 7, 0:88], rows_a[:], ident[0:88, 0:88])
            pe.transpose(ps[:, 7, 88:176], rows_b[:], ident[0:88, 0:88])
            pe.transpose(ps[:, 7, 176:176 + V_ROWS], rows_v[:], ident[0:V_ROWS, 0:V_ROWS])\
                .then_inc(s["rows_turned"], 1)
            for k in range(KT):
                t = pe.transpose(ps[:, 2, k * META:(k + 1) * META], meta_tok[:, k * P:(k + 1) * P],
                                 ident[0:META, 0:META])
            t.then_inc(s["meta_turned"], 1)
            pe.wait_ge(s["x_in"], 64)
            for k in range(KT):
                if k >= 2:
                    pe.wait_ge(s["x_ready"], k - 1)
                for t in range(4):
                    mm = pe.transpose(ps[:, k % 2, t * P:(t + 1) * P], x_tok[:, t, k * P:(k + 1) * P], ident[:])
                mm.then_inc(s["x_turned"], 1)
            pe.wait_ge(s["ones_set"], 2)
            norm_pe(pe, 0, ps[:, 4, 0:META], sq, META)
            norm_pe(pe, 1, ps[:, 3, :], sq, S)

            for n in range(N_SGU, N_QKV):
                pe.wait_ge(low_made, n + 1)
                if n == 0:
                    after(pe, "setup")
                if n >= 4:
                    pe.wait_ge(s["gelu_done"], n - 3)
                product(pe, ps[:, n % 4, :], n, 0, P, KT, hx).then_inc(strip_used, 1)

            bank = [4, 5, 6, 7, 4, 5]
            item = [0, None, 1, 2, 3, 4]

            def qkv_sum(m):
                j = item[m]
                pe.wait_ge(s["i1_sq"], j + 1)
                if m in (0, 2, 3):
                    pass
                if j >= 2:
                    pe.wait_ge(s["i1_root"], j - 1)
                pe.matmul(ps[:, j % 2, :], blocks[:], sq[:, j % 2, 0:S], start=True, stop=True)\
                    .then_inc(s["i1_sum"], 1)

            def sv_sum(k):
                pe.wait_ge(s["sv_sq"], k + 1)
                pe.matmul(ps[:, 2, :], ones[:], sq[:, k % 2, 0:S], start=k == 0, stop=k == 3).then_inc(s["sv_sum"], 1)

            for m in range(6):
                n = N_QKV + m
                pe.wait_ge(low_made, n + 1)
                if m >= 4:
                    pe.wait_ge(s["i1_normed"], 1) if m == 4 else pe.wait_ge(s["v_copied"], 1)
                product(pe, ps[:, bank[m], :], n, 0, P, KT, hx).then_inc(strip_used, 1)
                if m == 0:
                    pe.wait_ge(s["gelu_done"], 8)
                    for k in range(4):
                        sv_sum(k)
                    qkv_sum(0)
                elif m == 2:
                    pe.wait_ge(s["v_copied"], 1)
                    for t in range(4):
                        mm = pe.transpose(ps[:, 3, t * P:(t + 1) * P], v_f[:, t * P:(t + 1) * P], ident[:])
                    mm.then_inc(s["v_turned"], 1)
                    qkv_sum(2)
                elif m > 2:
                    qkv_sum(m)

            after(pe, "qkv")
            pe.wait_ge(s["ws_cut"], 1)
            for g in range(8):
                mm = pe.transpose(ps[:, 6 + g // 4, (g % 4) * P:(g % 4 + 1) * P], ws_raw[:, g, :], ident[:])
            mm.then_inc(s["ws_turned"], 1)
            for c in range(4):
                if c >= 2:
                    pe.wait_ge(s["sv_tok_ready"], c - 1)
                for k in range(4):
                    mm = pe.transpose(ps[:, c % 2, k * P:(k + 1) * P], uv[:, 4 + k, c * P:(c + 1) * P], ident[:])
                mm.then_inc(s["sv_turned"], 1)
            pe.wait_ge(s["ws_ready"], 1)
            pe.wait_ge(s["sv_tok_ready"], 4)
            for q in range(4):
                if q >= 2:
                    pe.wait_ge(s["mix_biased"], 2 * (q - 1))
                for c in range(4):
                    mm = pe.matmul(ps[:, 2 + 2 * (q % 2) + c // 2, (c % 2) * 256:(c % 2) * 256 + 256],
                                   uv_tok[:, c, q * P:(q + 1) * P],
                                   ws_t[:, 2 * q:2 * q + 2, :].rearrange("p g i -> p (g i)"), start=True, stop=True)
                mm.then_inc(s["mixed"], 1)

            after(pe, "mix")
            with pe.Fori(0, 4) as j:
                def scores(t):
                    w = 2 * P if t else P
                    pe.wait_ge(s["j_staged"], j + 1)
                    if t:
                        pe.wait_ge(s["a_masked"], j * 8 + 2 * t)
                    for h in range(2):
                        mm = pe.matmul(ps[:, h, 0:w], q_st[h * HD:(h + 1) * HD, t * P:(t + 1) * P],
                                       k_t[h * HD:(h + 1) * HD, (t + 1) * P - w:(t + 1) * P], start=True, stop=True)
                    mm.then_inc(s["a_scored"], 1)

                def turn(t):
                    pe.wait_ge(s["a_probs"], j * 8 + (2 * t + 2))
                    for a in range(2 if t else 1):
                        for h in range(2):
                            mm = pe.transpose(ps[:, 2, (2 * a + h) * P:(2 * a + h + 1) * P],
                                              att_e[:, h, a * P:(a + 1) * P], ident[:])
                    mm.then_inc(s["a_turned"], 1)

                def weigh(t):
                    pe.wait_ge(s["a_copied"], j * 4 + (t + 1))
                    if t:
                        pe.wait_ge(s["a_y"], j * 8 + 2 * t)
                    ks = [t - 1, t] if t else [0]
                    for a, kt in enumerate(ks):
                        mm = pe.matmul(ps[:, 3, 0:2 * P], v_tok[:, kt, :],
                                       att_p[:, 2 * a:2 * a + 2, :].rearrange("p h q -> p (h q)"),
                                       start=a == 0, stop=a == len(ks) - 1)
                    mm.then_inc(s["a_summed"], 1)

                scores(0)
                for t in range(4):
                    pe.wait_ge(low_made, j * 4 + (N_GATE + t + 1))
                    if t >= 2:
                        pe.wait_ge(s["gate_kept"], j * 4 + (t - 1))
                    product(pe, ps[:, 4 + t, :], N_GATE + t, 0, P, KT, hx).then_inc(strip_used, 1)
                    turn(t)
                    if t < 3:
                        scores(t + 1)
                    weigh(t)
                pe.wait_ge(s["gate_kept"], j * 4 + 3)

            after(pe, "att")
            with pe.Fori(0, 2) as i:
                for u in range(2):
                    for b in range(2):
                        n = N_MERGE + 2 * u + b
                        pe.wait_ge(low_made, i * 4 + (n + 1))
                        for m in range(2):
                            mm = product(pe, ps[:, 4 * b + 2 * u + m, :], n, m * P, 2 * P, 4,
                                         lambda k: (a_high[:, 4 * b + k, :], a_low[:, 4 * b + k, :]))
                        mm.then_inc(strip_used, 1)
                pe.wait_ge(s["m_part"], i * 8 + 8)

            after(pe, "merge")
            with pe.Fori(0, 2) as i:
                for m in range(4):
                    pe.wait_ge(low_made, i * 4 + (N_OUT + m + 1))
                    if m >= 2:
                        pe.wait_ge(s["o_added"], i * 4 + (m - 1))
                    product(pe, ps[:, m, :], N_OUT + m, 0, P, KT, hx).then_inc(strip_used, 1)
                pe.wait_ge(s["o_added"], i * 4 + 3)

            after(pe, "out")
            norm_pe(pe, 2, ps[:, 7, :], sq, S)

            after(pe, "norm2")
            with pe.Fori(0, 11) as i:
                for m in range(4):
                    pe.wait_ge(low_made, i * 4 + (N_UP + m + 1))
                    if m >= 2:
                        pe.wait_ge(s["z_done"], i * 4 + (m - 1))
                    product(pe, ps[:, m, :], N_UP + m, 0, P, KT, hx).then_inc(strip_used, 1)
                pe.wait_ge(s["z_done"], i * 4 + 3)

            after(pe, "up")
            with pe.Fori(0, 2) as i:
                for m in range(4):
                    for part in range(3):
                        n = N_DOWN + 3 * m + part
                        pe.wait_ge(low_made, i * 12 + (n + 1))
                        if part == 0 and m >= 2:
                            pe.wait_ge(s["d_added"], i * 4 + (m - 1))
                        product(pe, ps[:, 4 + m, :], n, 0, P, 8 if part < 2 else 6,
                                lambda k: (m_high[:, 8 * part + k, :], m_low[:, 8 * part + k, :]),
                                part == 0, part == 2).then_inc(strip_used, 1)
                pe.wait_ge(s["d_added"], i * 4 + 3)

            after(pe, "down")
            norm_pe(pe, 3, ps[:, 0, :], sq2, S)

            after(pe, "norm3")
            with pe.Fori(0, 2) as i:
                for m in range(4):
                    pe.wait_ge(low_made, i * 4 + (N_GM + m + 1))
                    if m >= 2:
                        pe.wait_ge(s["gm_done"], i * 4 + (m - 1))
                    product(pe, ps[:, m, :], N_GM + m, 0, P, KT, hx).then_inc(strip_used, 1)
                pe.wait_ge(s["gm_done"], i * 4 + 3)

            after(pe, "gm")
            for m in range(5):
                n = N_LAT + m
                pe.wait_ge(low_made, n + 1)
                if m < 2:
                    mm = product(pe, ps[:, m, :], n, 0, P, KT, hx)
                else:
                    mm = product_wide(pe, 2 * m - 2, n, 0, P, KT, h_high, h_low)
                mm.then_inc(strip_used, 1)
            pe.wait_ge(s["pe_root_part"], 1)
            pe.wait_ge(s["pe_part"], 1)
            for h in range(2):
                mm = pe.matmul(ps[:, 6 + h, 0:HALF], blocks[:], sq2[:, 0, h * HALF:(h + 1) * HALF],
                               start=True, stop=True)
            mm.then_inc(s["pe_sum"], 1)
            pe.wait_ge(s["pe_root_part"], 3)
            for k in range(2):
                pe.wait_ge(s["lat_sq"], k + 1)
                pe.matmul(ps[:, 6, :], ones[:], sq2[:, k % 2, 0:S], start=k == 0, stop=k == 1)\
                    .then_inc(s["lat_sum"], 1)
            pe.wait_ge(s["lat_root"], 2)
            for k in range(2):
                pe.wait_ge(s["lat_sq"], k + 3)
                for h in range(2):
                    mm = pe.matmul(ps[:, 6 + h, 0:HALF], ones[:], sq2[:, k % 2, h * HALF:(h + 1) * HALF],
                                   start=k == 0, stop=k == 1)
                mm.then_inc(s["lat_sum"], 1)
            pe.wait_ge(s["pe_part"], 2)
            pe.wait_ge(s["lat_scaled"], 2)
            for h in range(2):
                mm = pe.matmul(ps[:, h, 0:HALF], rot[:], k_pe[:, h * HALF:(h + 1) * HALF], start=True, stop=True)
            mm.then_inc(s["pe_turned"], 1)

            after(pe, "lat")
            with pe.Fori(0, 4) as p:
                pe.wait_ge(low_made, p * 4 + (N_MLA + 1))
                for h in range(2):
                    mm = product_wide(pe, 2 * h, N_MLA, h * P, 2 * P, 2, kl_high, kl_low)
                mm.then_inc(strip_used, 1)
                pe.wait_ge(low_made, p * 4 + (N_MLA + 2))
                for h in range(2):
                    mm = product(pe, ps[:, 4 + h, :], N_MLA + 1, h * P, 2 * P, 2,
                                 lambda k: (ql_high[:, k, :], ql_low[:, k, :]))
                mm.then_inc(strip_used, 1)
                pe.wait_ge(low_made, p * 4 + (N_MLA + 3))
                product(pe, ps[:, 6, :], N_MLA + 2, 0, P, 2,
                        lambda k: (ql_high[:, k, :], ql_low[:, k, :])).then_inc(strip_used, 1)
                for m in range(5):
                    pe.wait_ge(s["p_sq"], p * 5 + (m + 1))
                    pe.wait_ge(s["p_kept"], p * 5 + (m + 1))
                    if m < 2:
                        for h in range(2):
                            mm = pe.matmul(ps[:, 2 * m + h, 0:HALF], ones[:],
                                           sq2[:, m % 2, h * HALF:(h + 1) * HALF], start=True, stop=True)
                    else:
                        mm = pe.matmul(ps[:, 2 + m, :], ones[:] if m < 4 else blocks[:], sq2[:, m % 2, 0:S],
                                       start=True, stop=True)
                    mm.then_inc(s["p_sum"], 1)
                pe.wait_ge(low_made, p * 4 + (N_MLA + 4))
                for h in range(2):
                    pe.wait_ge(s["p_ln"], p * 5 + (h + 1))
                    mm = product_wide(pe, 2 * h, N_MLA + 3, h * P, 2 * P, 2, kl_high, kl_low)
                mm.then_inc(strip_used, 1)
                pe.wait_ge(s["p_normed"], p * 5 + 5)
                pe.matmul(ps[:, 7, :], rot[:], q_pe[:], start=True, stop=True).then_inc(s["qr_turned"], 1)
                for h in range(2):
                    pe.wait_ge(s["mv_kept"], p * 2 + (h + 1))
                    if h:
                        pe.wait_ge(s["mv_ready"], p * 4 + 2)
                    for a in range(4):
                        pe.transpose(ps[:, 4, a * P:(a + 1) * P], mvf[:, h, a * P:(a + 1) * P], ident[:])
                    pe.transpose(ps[0:META, 5, 0:P], mvf[:, h, 4 * P:L], ident[:]).then_inc(s["mv_turned"], 1)

                def scores(u):
                    h, t = divmod(u, 4)
                    b = 2 * (u % 2)
                    if u == 0:
                        pe.wait_ge(s["qr_part"], p * 3 + 3)
                        pe.wait_ge(s["mv_kept"], p * 2 + 2)
                    if u >= 2:
                        pe.wait_ge(s["s_exp"], p * 8 + (u - 1))
                    for c in range(2):
                        pe.matmul(ps[:, b + c, 0:HALF], qn[:, h, t * P:(t + 1) * P],
                                  kn[:, h, c * HALF:(c + 1) * HALF], start=True, stop=False)
                        mm = pe.matmul(ps[:, b + c, 0:HALF], q_pe[h * 64:(h + 1) * 64, t * P:(t + 1) * P],
                                       k_pe[h * 64:(h + 1) * 64, c * HALF:(c + 1) * HALF], start=False, stop=True)
                    mm.then_inc(s["s_scored"], 1)

                def turn(u):
                    pe.wait_ge(s["s_probs"], p * 8 + (u + 1))
                    if u:
                        pe.wait_ge(s["s_copied_a"], p * 8 + u)
                        pe.wait_ge(s["s_copied_b"], p * 8 + u)
                    else:
                        pe.wait_ge(s["mv_ready"], p * 4 + 4)
                    for a in range(4):
                        pe.transpose(ps[:, 4, a * P:(a + 1) * P], me[:, u % 2, a * P:(a + 1) * P], ident[:])
                    pe.transpose(ps[0:META, 5, 0:P], me[:, u % 2, 4 * P:L], ident[:]).then_inc(s["s_turned"], 1)

                def weigh(u):
                    h, t = divmod(u, 4)
                    pe.wait_ge(s["s_copied_a"], p * 8 + (u + 1))
                    pe.wait_ge(s["s_copied_b"], p * 8 + (u + 1))
                    if u == 4:
                        pe.wait_ge(s["qr_part"], p * 3 + 1)
                    for a in range(5):
                        r = P if a < 4 else META
                        mm = pe.matmul(ps[:, 6 + h, t * P:(t + 1) * P], mv[0:r, a, h * P:(h + 1) * P],
                                       mp[0:r, a * P:(a + 1) * P], start=a == 0, stop=a == 4)
                    mm.then_inc(s["s_summed"], 1)

                scores(0)
                for u in range(9):
                    if u < 7:
                        scores(u + 1)
                    if u < 8:
                        turn(u)
                    if u >= 1:
                        weigh(u - 1)
                pe.wait_ge(s["s_y"], p * 2 + 2)

            after(pe, "mla")
            with pe.Fori(0, 2) as i:
                for m in range(4):
                    pe.wait_ge(low_made, i * 4 + (N_OM + m + 1))
                    if m >= 2:
                        pe.wait_ge(s["om_added"], i * 4 + (m - 1))
                    product(pe, ps[:, m, :], N_OM + m, 0, P, KT,
                            lambda k: (y_high[:, k, :], y_low[:, k, :])).then_inc(strip_used, 1)
                pe.wait_ge(s["om_added"], i * 4 + 3)

            after(pe, "om")
            with pe.Fori(0, 8) as p:
                pe.wait_ge(low_made, p * 4 + (N_NA + 1))
                product_wide(pe, 0, N_NA, 0, P, KT, h_high, h_low).then_inc(strip_used, 1)
                pe.wait_ge(low_made, p * 4 + (N_NA + 2))
                product(pe, ps[:, 2, :], N_NA + 1, 0, P, KT, hx).then_inc(strip_used, 1)
                pe.wait_ge(s["q_sq"], p * 2 + 1)
                pe.wait_ge(s["q_kept"], p * 2 + 1)
                for h in range(2):
                    mm = pe.matmul(ps[:, h, 0:HALF], blocks[:], sq2[:, 0, h * HALF:(h + 1) * HALF],
                                   start=True, stop=True)
                mm.then_inc(s["q_sum"], 1)
                pe.wait_ge(low_made, p * 4 + (N_NA + 3))
                product_wide(pe, 4, N_NA + 2, 0, P, KT, h_high, h_low).then_inc(strip_used, 1)
                pe.wait_ge(s["q_sq"], p * 2 + 2)
                pe.wait_ge(s["q_kept"], p * 2 + 2)
                pe.matmul(ps[:, 2, :], blocks[:], sq2[:, 1, 0:S], start=True, stop=True).then_inc(s["q_sum"], 1)
                pe.wait_ge(low_made, p * 4 + (N_NA + 4))
                product(pe, ps[:, 7, :], N_NA + 3, 0, P, KT, hx).then_inc(strip_used, 1)

                def scores(t):
                    w, g = NA_W[t], NA_G[t]
                    if t < 2:
                        pe.wait_ge(s["q_normed"], p * 2 + 2)
                    else:
                        pe.wait_ge(s["t_masked"], p * 8 + 2 * (t - 1))
                    for h in range(2):
                        b = 2 * (t % 2) + h
                        q = nq[h * HD:(h + 1) * HD, t * P:(t + 1) * P]
                        pe.matmul(ps[:, b, 0:META], q, nk[h * HD:(h + 1) * HD, 0:META], start=True, stop=True)
                        mm = pe.matmul(ps[:, b, META:META + w], q,
                                       nk[h * HD:(h + 1) * HD, META + g * P:META + g * P + w],
                                       start=True, stop=True)
                    mm.then_inc(s["t_scored"], 1)

                def turn(t):
                    pe.wait_ge(s["t_probs"], p * 8 + (2 * t + 2))
                    if t:
                        pe.wait_ge(s["t_copied_a"], p * 4 + t)
                        pe.wait_ge(s["t_copied_b"], p * 4 + t)
                    else:
                        pe.wait_ge(s["nv_ready"], p * 2 + 2)
                    for a in range(NA_W[t] // P):
                        for h in range(2):
                            o = (2 * a + h) % 4 * P
                            pe.transpose(ps[:, 4 + a // 2, o:o + P], ne[:, t % 2, h, META + a * P:META + (a + 1) * P],
                                         ident[:])
                    for h in range(2):
                        mm = pe.transpose(ps[0:META, 5, (2 + h) * P:(3 + h) * P], ne[:, t % 2, h, 0:META], ident[:])
                    mm.then_inc(s["t_turned"], 1)

                def weigh(t):
                    n = NA_W[t] // P
                    pe.wait_ge(s["t_copied_a"], p * 4 + (t + 1))
                    pe.wait_ge(s["t_copied_b"], p * 4 + (t + 1))
                    if t:
                        pe.wait_ge(s["t_y"], p * 8 + 2 * t)
                    for a in range(n):
                        pe.matmul(ps[:, 6, 0:2 * P], nv[:, NA_G[t] + a, :], npt[:, a, :], start=a == 0, stop=False)
                    pe.matmul(ps[:, 6, 0:2 * P], nv[0:META, 4, :], npt[0:META, 3, :], start=False, stop=True)\
                        .then_inc(s["t_summed"], 1)

                scores(0)
                pe.wait_ge(s["nv_kept"], p + 1)
                for a in range(4):
                    pe.transpose(ps[:, 4, a * P:(a + 1) * P], nvf[:, META + a * P:META + (a + 1) * P], ident[:])
                pe.transpose(ps[0:META, 5, 0:P], nvf[:, 0:META], ident[:]).then_inc(s["nv_turned"], 1)
                for t in range(5):
                    if t < 3:
                        scores(t + 1)
                    if t < 4:
                        turn(t)
                    if t >= 1:
                        weigh(t - 1)
                pe.wait_ge(s["g_exp"], p + 1)
                pe.wait_ge(s["g_part"], p * 4 + 4)

            after(pe, "na")
            for m in range(8):
                pe.wait_ge(low_made, N_ON + m + 1)
                product(pe, ps[:, m, :], N_ON + m, 0, P, KT,
                        lambda k: (y_high[:, k, :], y_low[:, k, :])).then_inc(strip_used, 1)

            after(pe, "on")
            for t in range(4):
                for h in range(2):
                    for k in range(4):
                        mm = pe.transpose(ps[:, 2 * t + h, k * P:(k + 1) * P],
                                          x_t[:, 4 * h + k, t * P:(t + 1) * P], ident[:])
                    mm.then_inc(s["out_turned"], 1)

        @block.scalar
        def _(act):
            c = 0

            def const(dst, src):
                nonlocal c
                c += 1
                act.dma_start(dst, src).then_inc(s["consts_in"], 16)

            const(ident[:], c_ident)
            taps = conv_w[0].rearrange("t (c p) -> t c p", p=P)
            const(rows_a[0:44, :], taps[0])
            const(rows_a[44:88, :], taps[1])
            const(rows_b[0:44, :], taps[2])
            const(rows_b[44:88, :], conv_b[0].rearrange("(c p) -> c p", p=P))
            for r, k, v in ((V_MIX, 8, mix_norm), (V_FFN, 8, ffn_norm), (V_N2, 8, norm_w_2),
                            (V_QL, 2, q_lat_norm_w_2), (V_KL, 2, kv_lat_norm_w_2), (V_QN, 1, mla_qn_w_2),
                            (V_KN, 1, mla_kn_w_2), (V_SGU, 4, sgu_norm)):
                const(rows_v[r:r + k, :], v[0].rearrange("(c p) -> c p", p=P))
            for r, v in ((V_AQ, q_norm), (V_AK, k_norm), (V_NQ, na_q_norm_w_2), (V_NK, na_k_norm_w_2),
                         (V_QPE, mla_qpe_w_2), (V_KPE, mla_kpe_w_2)):
                for h in range(2):
                    const(rows_v[r:r + 1, h * 64:(h + 1) * 64], v)
            const(meta_tok[:], meta_tokens_2)
            const(blocks[:], c_blocks)
            const(rot[:], c_rot)
            const(dist[:], c_dist)
            const(slope[:], c_slope)
            const(sink[:], sinks[0].partition_broadcast(P))
            bs = b_s[0].rearrange("(q h) i -> h q i", h=2)
            for h in range(2):
                const(bias_s[h * 64:(h + 1) * 64, :, :], bs[h].partition_broadcast(64))
            assert c == N_CONST, c

            act.preload_act_table_set("natural_log_exp_and_others")
            act.wait_ge(s["meta_turned"], 1)
            act.activation(meta_t[:], ps[:, 2, 0:P].rearrange("p (k m) -> p k m", m=META), ACT.Copy)\
                .then_inc(s["meta_ready"], 1)
            for k in range(KT):
                act.wait_ge(s["x_turned"], k + 1)
                act.activation(x_t[:, k, :], ps[:, k % 2, :], ACT.Copy).then_inc(s["x_ready"], 1)
            act.wait_ge(s["meta_ready"], 1)
            act.wait_ge(s["ones_set"], 2)
            norm_act(act, 0, ps[:, 4, 0:META], lambda k: meta_t[:, k, :], sq, root, scaled, META,
                     lambda k: h_high[:, k, 0:META])
            act.wait_ge(s["norm_low"], 8)
            norm_act(act, 1, ps[:, 3, :], xs, sq, root, scaled, S, hh, "x_ready")

            after(act, "setup")
            for n in range(8):
                act.wait_ge(strip_used, N_SGU + n + 1)
                act.activation(uv[:, n, :], ps[:, n % 4, :], ACT.Gelu_apprx_tanh).then_inc(s["gelu_done"], 1)

            act.preload_act_table_set("natural_log_exp_and_others")
            for k in range(4):
                act.wait_ge(s["gelu_done"], 5 + k)
                if k >= 2:
                    act.wait_ge(s["sv_sum"], k - 1)
                act.activation(sq[:, k % 2, 0:S], uv[:, 4 + k, :], ACT.Square).then_inc(s["sv_sq"], 1)
            act.wait_ge(s["sv_sum"], 4)
            act.activation(root[:, 1, 0:S], ps[:, 2, :], ACT.Ln, bias=eps[:, 0:1], scale=1.0 / SGU)\
                .then_inc(s["sv_root"], 1)
            act.wait_ge(s["sv_root"], 1)
            act.activation(root[:, 1, 0:S], root[:, 1, 0:S], ACT.Exp, scale=-0.5).then_inc(s["sv_root"], 1)
            banks = [4, 6, 7, 4, 5]
            strips = [0, 2, 3, 4, 5]

            def i1_root(j):
                act.wait_ge(s["i1_sum"], j + 1)
                if j >= 2:
                    act.wait_ge(s["i1_normed"], j - 1)
                if j == 1:
                    act.wait_ge(s["sv_normed"], 4)
                act.activation(root[:, j % 2, 0:S], ps[:, j % 2, :], ACT.Ln, bias=eps[:, 0:1], scale=1.0 / HD)\
                    .then_inc(s["i1_ln"], 1)
                act.wait_ge(s["i1_ln"], j + 1)
                act.activation(root[:, j % 2, 0:S], root[:, j % 2, 0:S], ACT.Exp, scale=-0.5)\
                    .then_inc(s["i1_root"], 1)

            for j in range(5):
                act.wait_ge(strip_used, N_QKV + strips[j] + 1)
                if j >= 2:
                    act.wait_ge(s["i1_sum"], j - 1)
                act.activation(sq[:, j % 2, 0:S], ps[:, banks[j], :], ACT.Square).then_inc(s["i1_sq"], 1)
                if j == 0:
                    i1_root(0)
                    act.wait_ge(strip_used, N_QKV + 2)
                    act.activation(v_f[:], ps[:, 5, :], ACT.Copy).then_inc(s["v_copied"], 1)
                elif j >= 2:
                    if j == 2:
                        pass
                    i1_root(j - 1)
            i1_root(4)

            after(act, "qkv")
            act.wait_ge(s["ws_turned"], 1)
            act.activation(ws_t[:].rearrange("p (b g) i -> p b (g i)", b=2), ps[:, 6:8, :], ACT.Copy)\
                .then_inc(s["ws_ready"], 1)
            for q in range(4):
                act.wait_ge(s["mix_gated"], 2 * (q + 1))
                act.activation(a_high[:, 4 + q, :], uv[:, q, :], ACT.Copy).then_inc(s["mix_high"], 1)

            after(act, "mix")
            with act.Fori(0, 4) as j:
                act.activation(q_st[:], q_t[:, bass.ds(j, 1), :], ACT.Copy).then_inc(s["j_staged"], 1)
                for t in range(4):
                    w = 2 * P if t else P
                    for h in range(2):
                        act.wait_ge(s["a_part"], j * 20 + (5 * t + 2))
                        act.activation(att_e[:, h, 0:w], att_e[:, h, 0:w], ACT.Exp, bias=att_m[:, 1, h:h + 1],
                                       accum_out=att_m[:, 2, h:h + 1]).then_inc(s["a_exp"], 1)
                    act.wait_ge(s["a_part"], j * 20 + (5 * t + 3))
                    act.activation(att_m[:, 4, :], att_m[:, 3, :], ACT.Exp).then_inc(s["a_sink_exp"], 1)
                    act.wait_ge(s["a_turned"], j * 4 + (t + 1))
                    if t:
                        act.wait_ge(s["a_summed"], j * 4 + t)
                    act.activation(att_p[:, 0:w // 64, :], ps[:, 2, 0:2 * w].rearrange("p (a q) -> p a q", q=P),
                                   ACT.Copy).then_inc(s["a_copied"], 1)
                    act.wait_ge(s["a_summed"], j * 4 + (t + 1))
                    for h in range(2):
                        r = slice(h * HD, (h + 1) * HD)
                        act.activation(att_y[r, t * P:(t + 1) * P], ps[r, 3, h * P:(h + 1) * P], ACT.Copy)\
                            .then_inc(s["a_y"], 1)
                act.wait_ge(s["a_y"], j * 8 + 8)
                act.activation(a_high[:, bass.ds(j, 1), :], att_y[:], ACT.Copy).then_inc(s["a_high"], 1)
                act.wait_ge(s["a_low"], j + 1)

            after(act, "att")
            with act.Fori(0, 2) as i:
                for u in range(2):
                    for m in range(2):
                        for b in range(2):
                            g = gates[:, bass.ds(i * 4 + (8 * b + 2 * u + m), 1), :]
                            act.activation(g, g, ACT.Sigmoid).then_inc(s["g_sig"], 1)
                for m in range(4):
                    act.wait_ge(s["m_whole"], i * 4 + (m + 1))
                    act.activation(h_high[:, bass.ds(i * 4 + m, 1), META:L], merge[:, m % 2, :], ACT.Copy)\
                        .then_inc(s["m_high_"], 1)

            act.preload_act_table_set("natural_log_exp_and_others")
            after(act, "out")
            norm_act(act, 2, ps[:, 7, :], xs, sq, root, scaled, S, hh)

            after(act, "norm2")
            with act.Fori(0, 11) as i:
                for m in range(4):
                    ct = m % 2 + FT * (m // 2)
                    act.wait_ge(strip_used, i * 4 + (N_UP + m + 1))
                    act.activation(z[:, m, :], ps[:, m, :], ACT.Identity,
                                   scale=cv[:, bass.ds(i * 2 + (C_CONV + 2 * 2 * FT + ct), 1)],
                                   bias=cv[:, bass.ds(i * 2 + (C_CONVB + ct), 1)]).then_inc(s["z_first"], 1)
                    if m >= 2:
                        act.wait_ge(s["z_done"], i * 4 + (m - 1))
                        act.activation(z[:, m - 2, :], z[:, m - 2, :], ACT.Silu).then_inc(s["z_silu"], 1)
                for m in range(2):
                    act.wait_ge(s["z_gated"], i * 2 + (m + 1))
                    act.activation(m_high[:, bass.ds(i * 2 + m, 1), :], zg[:, m, :], ACT.Copy)\
                        .then_inc(s["z_high"], 1)

            with act.Fori(0, 2) as i:
                for m in range(4):
                    act.wait_ge(s["d_added"], i * 4 + (m + 1))
                    act.activation(x_t[:, bass.ds(i * 4 + m, 1), :].rearrange("p o (g r c) -> p (o r) g c", g=CG, c=16),
                                   z[:, m, :].rearrange("p (r g c) -> p r g c", g=CG, c=16), ACT.Copy)\
                        .then_inc(s["d_placed"], 1)

            act.preload_act_table_set("natural_log_exp_and_others")
            after(act, "down")
            norm_act(act, 3, ps[:, 0, :], xs, sq2, root2, scaled2, S, hh)

            after(act, "norm3")
            with act.Fori(0, 2) as i:
                for m in range(4):
                    act.wait_ge(strip_used, i * 4 + (N_GM + m + 1))
                    act.activation(gm[:, bass.ds(i * 4 + m, 1), :], ps[:, m, :], ACT.Silu).then_inc(s["gm_done"], 1)

            act.preload_act_table_set("natural_log_exp_and_others")
            after(act, "gm")
            act.wait_ge(strip_used, N_LAT + 5)
            act.activation(halves(sq2[:, 0, :]), wide(6), ACT.Square).then_inc(s["pe_root_part"], 1)
            act.wait_ge(s["pe_sum"], 1)
            act.activation(halves(root2[:, 0, :]), wide(6), ACT.Ln, bias=eps[:, 0:1], scale=1.0 / 64)\
                .then_inc(s["pe_root_part"], 1)
            act.wait_ge(s["pe_root_part"], 2)
            act.activation(root2[:, 0, :], root2[:, 0, :], ACT.Exp, scale=-0.5).then_inc(s["pe_root_part"], 1)
            for m in range(2):
                src, n = ((lambda k: ps[:, k, :]), S) if m == 0 else ((lambda k: wide(2 + 2 * k)), L)
                for k in range(2):
                    act.wait_ge(s["lat_sum"], 2 * m + k - 1) if m else None
                    dst = sq2[:, k, 0:n] if m == 0 else halves(sq2[:, k, :])
                    act.activation(dst, src(k), ACT.Square).then_inc(s["lat_sq"], 1)
                act.wait_ge(s["lat_sum"], 2 * m + 2)
                if m == 0:
                    act.wait_ge(s["pe_part"], 2)
                else:
                    act.wait_ge(s["lat_scaled"], 2)
                dst, acc = (root2[:, 0, 0:n], ps[:, 6, :]) if m == 0 else (halves(root2[:, 0, :]), wide(6))
                act.activation(dst, acc, ACT.Ln, bias=eps[:, 0:1], scale=1.0 / 256).then_inc(s["lat_root"], 1)
                act.wait_ge(s["lat_root"], m * 2 + 1)
                act.activation(root2[:, 0, 0:n], root2[:, 0, 0:n], ACT.Exp, scale=-0.5).then_inc(s["lat_root"], 1)
                for k in range(2):
                    act.wait_ge(s["lat_scaled"], 2 * m + k + 1)
                    act.activation((ql_high if m == 0 else kl_high)[:, k, :], scaled2[:, k, 0:n], ACT.Copy)\
                        .then_inc(s["lat_high"], 1)

            after(act, "lat")
            with act.Fori(0, 4) as p:
                used = [1, 1, 2, 2, 3]
                for m in range(5):
                    act.wait_ge(strip_used, p * 4 + (N_MLA + used[m]))
                    if m >= 2:
                        act.wait_ge(s["p_sum"], p * 5 + (m - 1))
                    src = wide(2 * m) if m < 2 else ps[:, 2 + m, :]
                    dst = halves(sq2[:, m % 2, :]) if m < 2 else sq2[:, m % 2, 0:S]
                    act.activation(dst, src, ACT.Square).then_inc(s["p_sq"], 1)
                for m in range(5):
                    act.wait_ge(s["p_sum"], p * 5 + (m + 1))
                    if m >= 2:
                        act.wait_ge(s["p_normed"], p * 5 + (m - 1))
                    src = wide(2 * m) if m < 2 else ps[:, 2 + m, :]
                    dst = halves(root2[:, m % 2, :]) if m < 2 else root2[:, m % 2, 0:S]
                    n = L if m < 2 else S
                    act.activation(dst, src, ACT.Ln, bias=eps[:, 0:1], scale=1.0 / (P if m < 4 else 64))\
                        .then_inc(s["p_ln"], 1)
                    act.wait_ge(s["p_ln"], p * 5 + (m + 1))
                    act.activation(root2[:, m % 2, 0:n], root2[:, m % 2, 0:n], ACT.Exp, scale=-0.5)\
                        .then_inc(s["p_root"], 1)
                for h in range(2):
                    act.wait_ge(strip_used, p * 4 + (N_MLA + 4))
                    act.wait_ge(s["p_sum"], p * 5 + 5)
                    act.activation(halves(mvf[:, h, :]), wide(2 * h), ACT.Copy).then_inc(s["mv_kept"], 1)
                for h in range(2):
                    act.wait_ge(s["mv_turned"], p * 2 + (h + 1))
                    act.activation(mv[:, 0:4, h * P:(h + 1) * P], ps[:, 4, :].rearrange("p (a d) -> p a d", d=P),
                                   ACT.Copy).then_inc(s["mv_ready"], 1)
                    act.activation(mv[0:META, 4, h * P:(h + 1) * P], ps[0:META, 5, 0:P], ACT.Copy)\
                        .then_inc(s["mv_ready"], 1)
                for u in range(9):
                    if u < 8:
                        act.wait_ge(s["s_neg"], p * 8 + (u + 1))
                        if u >= 2:
                            act.wait_ge(s["s_turned"], p * 8 + (u - 1))
                        act.activation(halves(me[:, u % 2, :]), wide(2 * (u % 2)), ACT.Exp, scale=MLA_SCALE,
                                       bias=mm_[:, u % 2, 1:2], accum_out=mm_[:, u % 2, 2:3]).then_inc(s["s_exp"], 1)
                    if u >= 1:
                        act.wait_ge(s["s_turned"], p * 8 + u)
                        if u >= 2:
                            act.wait_ge(s["s_summed"], p * 8 + (u - 1))
                        act.activation(mp[:, 0:4 * P], ps[:, 4, :], ACT.Copy).then_inc(s["s_copied_a"], 1)
                for h in range(2):
                    act.wait_ge(s["s_y"], p * 2 + (h + 1))
                    act.activation(y_high[:, bass.ds(p * 2 + h, 1), :], (y_f[:], scaled2[:, 0, 0:S])[h], ACT.Copy)\
                        .then_inc(s["s_high"], 1)

            after(act, "om")
            with act.Fori(0, 8) as p:
                for m in range(2):
                    act.wait_ge(strip_used, p * 4 + (N_NA + m + 1))
                    src = wide(0) if m == 0 else ps[:, 2, :]
                    dst = halves(sq2[:, 0, :]) if m == 0 else sq2[:, 1, 0:S]
                    act.activation(dst, src, ACT.Square).then_inc(s["q_sq"], 1)
                for m in range(2):
                    act.wait_ge(s["q_sum"], p * 2 + (m + 1))
                    src = wide(0) if m == 0 else ps[:, 2, :]
                    n = L if m == 0 else S
                    dst = halves(root2[:, 0, :]) if m == 0 else root2[:, 1, 0:S]
                    act.activation(dst, src, ACT.Ln, bias=eps[:, 0:1], scale=1.0 / HD).then_inc(s["q_root"], 1)
                    act.wait_ge(s["q_root"], p * 4 + (2 * m + 1))
                    act.activation(root2[:, m, 0:n], root2[:, m, 0:n], ACT.Exp, scale=-0.5).then_inc(s["q_root"], 1)
                    if m == 0:
                        act.wait_ge(strip_used, p * 4 + (N_NA + 3))
                        act.activation(halves(nvf[:]), wide(4), ACT.Copy).then_inc(s["nv_kept"], 1)
                act.wait_ge(strip_used, p * 4 + (N_NA + 4))
                act.activation(ng[:, 1, :], ps[:, 7, :], ACT.Exp, scale=-1.0).then_inc(s["g_exp"], 1)
                act.wait_ge(s["nv_turned"], p + 1)
                act.activation(nv[:, 0:4, :], ps[:, 4, :].rearrange("p (a d) -> p a d", d=P), ACT.Copy)\
                    .then_inc(s["nv_ready"], 1)
                act.activation(nv[0:META, 4, :], ps[0:META, 5, 0:P], ACT.Copy).then_inc(s["nv_ready"], 1)
                for t in range(5):
                    if t < 4:
                        w = META + NA_W[t]
                        act.wait_ge(s["t_neg"], p * 4 + (t + 1))
                        for h in range(2):
                            act.activation(ne[:, t % 2, h, 0:w], ne[:, t % 2, h, 0:w], ACT.Exp,
                                           bias=nm[:, t % 2, 0, h:h + 1],
                                           accum_out=nm[:, t % 2, 1, h:h + 1]).then_inc(s["t_exp"], 1)
                    if t >= 1:
                        act.wait_ge(s["t_turned"], p * 4 + t)
                        if t >= 2:
                            act.wait_ge(s["t_summed"], p * 4 + (t - 1))
                        act.activation(npt[:, 0:2, :], ps[:, 4, :].rearrange("p (a q) -> p a q", a=2), ACT.Copy)\
                            .then_inc(s["t_copied_a"], 1)
                act.wait_ge(s["t_y"], p * 8 + 8)
                act.activation(y_high[:, bass.ds(p, 1), :], y_f[:], ACT.Copy).then_inc(s["t_high"], 1)

            after(act, "on")
            for t in range(4):
                act.wait_ge(s["out_turned"], 2 * t + 1)
                act.activation(y_tok[:, t, 0:512], ps[:, 2 * t, :], ACT.Copy).then_inc(s["out_left"], 1)

        @block.vector
        def _(dve):
            dve.wait_ge(s["rows_turned"], 1)
            dve.tensor_copy(cv[:], ps[:, 7, 0:C_V + V_ROWS]).then_inc(s["cols_ready"], 1)
            dve.wait_ge(s["cols_ready"], 1)
            dve.tensor_scalar(aq_gain[:], col(V_AQ), HD ** -0.5, None, ALU.mult).then_inc(s["gain_ready"], 1)
            dve.tensor_scalar(nq_gain[:], col(V_NQ), HD ** -0.5, None, ALU.mult).then_inc(s["gain_ready"], 1)
            make_high(dve, 0)
            norm_dve(dve, 0, lambda k: meta_t[:, k, :], V_N2, root, scaled, META,
                     lambda k: h_high[:, k, 0:META], lambda k: h_low[:, k, 0:META])
            make_high(dve, 1)
            make_high(dve, 2)
            dve.wait_ge(s["norm_low"], 8)
            norm_dve(dve, 1, xs, V_MIX, root, scaled, S, hh, hl)

            for n in range(N_SGU, N_QKV):
                make_high(dve, n + 3)

            dve.wait_ge(s["gain_ready"], 2)

            def i1_norm(j):
                dve.wait_ge(s["i1_root"], j + 1)
                dst = k_t[:] if j == 0 else q_t[:, j - 1, :]
                gain = col(V_AK) if j == 0 else aq_gain[:, 0:1]
                dve.scalar_tensor_tensor(dst, ps[:, [4, 6, 7, 4, 5][j], :], gain, root[:, j % 2, 0:S],
                                         ALU.mult, ALU.mult).then_inc(s["i1_normed"], 1)

            make_high(dve, N_QKV + 3)
            dve.wait_ge(s["sv_root"], 2)
            for k in range(4):
                dve.scalar_tensor_tensor(uv[:, 4 + k, :], uv[:, 4 + k, :], col(V_SGU + k), root[:, 1, 0:S],
                                         ALU.mult, ALU.mult).then_inc(s["sv_normed"], 1)
            i1_norm(0)
            make_high(dve, N_QKV + 4)
            make_high(dve, N_QKV + 5)
            dve.wait_ge(s["v_turned"], 1)
            dve.tensor_copy(v_tok[:], ps[:, 3, :].rearrange("p (a d) -> p a d", d=P)).then_inc(s["v_ready"], 1)
            for m in range(3, 6):
                i1_norm(m - 2)
                make_high(dve, N_QKV + m + 3)
            i1_norm(4)

            after(dve, "qkv")
            for c in range(4):
                dve.wait_ge(s["sv_turned"], c + 1)
                dve.tensor_copy(uv_tok[:, c, :], ps[:, c % 2, :]).then_inc(s["sv_tok_ready"], 1)
            for q in range(4):
                dve.wait_ge(s["mixed"], q + 1)
                b = 2 + 2 * (q % 2)
                for h in range(2):
                    r = slice(h * 64, (h + 1) * 64)
                    src = ps[r, b:b + 2, :].rearrange("p b (c g i) -> p b c g i", c=2, g=2)[:, :, :, h, :]
                    for c in range(2):
                        ins = dve.tensor_tensor(scaled[r, 0, 256 * c:256 * c + 256].rearrange("p (c i) -> p c i", c=2),
                                                src[:, c], bias_s[r, q:q + 1, :].broadcast_to([64, 2, P]), ALU.add)
                    ins.then_inc(s["mix_biased"], 1)
                    dve.wait_ge(s["mix_biased"], 2 * q + h + 1)
                    dve.tensor_tensor(uv[r, q, :], uv[r, q, :], scaled[r, 0, :], ALU.mult)\
                        .then_inc(s["mix_gated"], 1)
                dve.wait_ge(s["mix_high"], q + 1)
                dve.tensor_tensor(a_low[:, 4 + q, :], uv[:, q, :], a_high[:, 4 + q, :].bitcast(F32),
                                  ALU.subtract).then_inc(s["mix_low"], 1)

            after(dve, "mix")
            with dve.Fori(0, 4) as j:
                for h in range(2):
                    dve.tensor_scalar(bias_h[:, h, :], dist[:], slope[:, bass.ds(j + 4 * h, 1)], None, ALU.mult)\
                        .then_inc(s["j_bias"], 1)
                sinks_j = sink[:].rearrange("p (h j) -> p h j", h=2)[:, :, bass.ds(j, 1)]
                for t in range(4):
                    w = 2 * P if t else P
                    dve.wait_ge(s["j_bias"], j * 2 + 2)
                    dve.wait_ge(s["a_scored"], j * 4 + (t + 1))
                    if t:
                        dve.wait_ge(s["a_turned"], j * 4 + t)
                    make_high(dve, N_GATE + t + 3, j * 4)
                    for h in range(2):
                        dve.tensor_tensor_reduce(att_e[:, h, 0:w], ps[:, h, 0:w], bias_h[:, h, 2 * P - w:2 * P],
                                                 1.0, -3e38, ALU.add, ALU.max, att_m[:, 0, h:h + 1])\
                            .then_inc(s["a_masked"], 1)
                    dve.wait_ge(s["a_masked"], j * 8 + (2 * t + 2))
                    dve.tensor_tensor(att_m[:, 5, :], att_m[:, 0, :], sinks_j, ALU.max).then_inc(s["a_part"], 1)
                    dve.wait_ge(s["a_part"], j * 20 + (5 * t + 1))
                    dve.tensor_scalar(att_m[:, 1, :], att_m[:, 5, :], -1.0, None, ALU.mult).then_inc(s["a_part"], 1)
                    dve.tensor_tensor(att_m[:, 3, :], sinks_j, att_m[:, 5, :], ALU.subtract).then_inc(s["a_part"], 1)
                    dve.wait_ge(s["a_exp"], j * 8 + (2 * t + 2))
                    dve.wait_ge(s["a_sink_exp"], j * 4 + (t + 1))
                    dve.tensor_tensor(att_m[:, 3, :], att_m[:, 2, :], att_m[:, 4, :], ALU.add)\
                        .then_inc(s["a_part"], 1)
                    dve.wait_ge(s["a_part"], j * 20 + (5 * t + 4))
                    dve.reciprocal(att_m[:, 5, :], att_m[:, 3, :]).then_inc(s["a_part"], 1)
                    dve.wait_ge(s["a_part"], j * 20 + (5 * t + 5))
                    for h in range(2):
                        dve.tensor_scalar(att_e[:, h, 0:w], att_e[:, h, 0:w], att_m[:, 5, h:h + 1], None, ALU.mult)\
                            .then_inc(s["a_probs"], 1)
                    dve.wait_ge(strip_used, j * 4 + (N_GATE + t + 1))
                    dve.tensor_copy(gates[:, bass.ds(j * 4 + t, 1), :], ps[:, 4 + t, :]).then_inc(s["gate_kept"], 1)
                dve.wait_ge(s["a_high"], j + 1)
                dve.tensor_tensor(a_low[:, bass.ds(j, 1), :], att_y[:], a_high[:, bass.ds(j, 1), :].bitcast(F32),
                                  ALU.subtract).then_inc(s["a_low"], 1)

            after(dve, "att")
            with dve.Fori(0, 2) as i:
                for u in range(2):
                    for m in range(2):
                        o = 2 * u + m
                        dve.wait_ge(strip_used, i * 4 + (N_MERGE + 2 * u + 2))
                        for b in range(2):
                            dve.wait_ge(s["g_sig"], i * 8 + (4 * u + 2 * m + b + 1))
                            g = gates[:, bass.ds(i * 4 + (8 * b + o), 1), :]
                            dve.tensor_tensor(g, g, ps[:, 4 * b + o, :], ALU.mult).then_inc(s["m_part"], 1)
                        dve.wait_ge(s["m_part"], i * 8 + (4 * u + 2 * m + 2))
                        if o >= 2:
                            dve.wait_ge(s["m_low_"], i * 4 + (o - 1))
                        dve.tensor_tensor(merge[:, m, :], gates[:, bass.ds(i * 4 + o, 1), :],
                                          gates[:, bass.ds(i * 4 + (8 + o), 1), :], ALU.add)\
                            .then_inc(s["m_whole"], 1)
                        dve.wait_ge(s["m_high_"], i * 4 + (o + 1))
                        dve.tensor_tensor(h_low[:, bass.ds(i * 4 + o, 1), META:L], merge[:, m, :],
                                          h_high[:, bass.ds(i * 4 + o, 1), META:L].bitcast(F32), ALU.subtract)\
                            .then_inc(s["m_low_"], 1)
                        if m == 1:
                            make_high(dve, N_MERGE + 2 * u + 3, i * 4)
                            make_high(dve, N_MERGE + 2 * u + 4, i * 4)

            def add_out(n0, banks, done, i, lag):
                for m in range(4):
                    dve.wait_ge(strip_used, i * 4 + (n0 + m + 1))
                    xm = x_t[:, bass.ds(i * 4 + m, 1), :]
                    dve.tensor_tensor(xm, xm, ps[:, banks[m], :], ALU.add).then_inc(s[done], 1)
                    make_high(dve, n0 + m + lag, i * 4)

            with dve.Fori(0, 2) as i:
                add_out(N_OUT, [0, 1, 2, 3], "o_added", i, 3)

            after(dve, "out")
            norm_dve(dve, 2, xs, V_FFN, root, scaled, S, hh, hl)

            after(dve, "norm2")
            with dve.Fori(0, 11) as i:
                for m in range(4):
                    ct = m % 2 + FT * (m // 2)
                    dve.wait_ge(s["z_first"], i * 4 + (m + 1))
                    dve.scalar_tensor_tensor(z[:, m, 1:S], ps[:, m, 0:S - 1],
                                             cv[:, bass.ds(i * 2 + (C_CONV + 2 * FT + ct), 1)], z[:, m, 1:S],
                                             ALU.mult, ALU.add).then_inc(s["z_mid"], 1)
                    dve.wait_ge(s["z_mid"], i * 4 + (m + 1))
                    dve.scalar_tensor_tensor(z[:, m, 2:S], ps[:, m, 0:S - 2],
                                             cv[:, bass.ds(i * 2 + (C_CONV + ct), 1)], z[:, m, 2:S],
                                             ALU.mult, ALU.add).then_inc(s["z_done"], 1)
                    make_high(dve, N_UP + m + 3, i * 4)
                    if m >= 2:
                        g = m - 2
                        dve.wait_ge(s["z_done"], i * 4 + (m + 1))
                        dve.wait_ge(s["z_silu"], i * 2 + (g + 1))
                        dve.tensor_tensor(zg[:, g, :], z[:, g, :], z[:, m, :], ALU.mult).then_inc(s["z_gated"], 1)
                for g in range(2):
                    dve.wait_ge(s["z_high"], i * 2 + (g + 1))
                    dve.tensor_tensor(m_low[:, bass.ds(i * 2 + g, 1), :], zg[:, g, :],
                                      m_high[:, bass.ds(i * 2 + g, 1), :].bitcast(F32), ALU.subtract)\
                        .then_inc(s["z_low"], 1)

            after(dve, "up")
            with dve.Fori(0, 2) as i:
                for m in range(4):
                    for part in range(3):
                        make_high(dve, N_DOWN + 3 * m + part + 3, i * 12)
                    dve.wait_ge(strip_used, i * 12 + (N_DOWN + 3 * m + 3))
                    dve.tensor_tensor(z[:, m, :], x_t[:, bass.ds(i * 4 + m, 1), :], ps[:, 4 + m, :], ALU.add)\
                        .then_inc(s["d_added"], 1)
                dve.wait_ge(s["d_placed"], i * 4 + 4)

            after(dve, "down")
            norm_dve(dve, 3, xs, V_N2, root2, scaled2, S, hh, hl)
            with dve.Fori(0, 2) as i:
                for m in range(4):
                    make_high(dve, N_GM + m + 3, i * 4)

            after(dve, "gm")
            for m in range(5):
                make_high(dve, N_LAT + m + 3)
            dve.wait_ge(s["pe_root_part"], 1)
            dve.tensor_copy(halves(k_pe[:]), wide(6)).then_inc(s["pe_part"], 1)
            dve.wait_ge(s["pe_part"], 1)
            dve.wait_ge(s["pe_root_part"], 3)
            dve.scalar_tensor_tensor(k_pe[:], k_pe[:], col(V_KPE), root2[:, 0, :],
                                     ALU.mult, ALU.mult).then_inc(s["pe_part"], 1)
            for m in range(2):
                dve.wait_ge(s["lat_root"], m * 2 + 2)
                n = S if m == 0 else L
                for k in range(2):
                    if m:
                        dve.wait_ge(s["lat_low"], 2)
                    else:
                        dve.wait_ge(s["pe_part"], 2)
                    src = ps[:, k, :] if m == 0 else wide(2 + 2 * k)
                    dst = scaled2[:, k, 0:n] if m == 0 else halves(scaled2[:, k, :])
                    r = root2[:, 0, 0:n] if m == 0 else halves(root2[:, 0, :])
                    dve.scalar_tensor_tensor(dst, src, col((V_QL, V_KL)[m] + k), r, ALU.mult, ALU.mult)\
                        .then_inc(s["lat_scaled"], 1)
                for k in range(2):
                    dve.wait_ge(s["lat_high"], 2 * m + k + 1)
                    hi, lo = (ql_high, ql_low) if m == 0 else (kl_high, kl_low)
                    dve.tensor_tensor(lo[:, k, :], scaled2[:, k, 0:n], hi[:, k, :].bitcast(F32), ALU.subtract)\
                        .then_inc(s["lat_low"], 1)
            dve.wait_ge(s["tables_in"], 32)
            dve.wait_ge(s["pe_turned"], 1)
            dve.wait_ge(s["lat_low"], 4)
            dve.tensor_tensor(k_pe[:], k_pe[:], cos[:], ALU.mult).then_inc(s["pe_part"], 1)
            dve.tensor_tensor(halves(scaled2[:, 0, :]), wide(0), halves(sin[:]), ALU.mult).then_inc(s["pe_part"], 1)
            dve.wait_ge(s["pe_part"], 3)
            dve.wait_ge(s["pe_part"], 4)
            dve.tensor_tensor(k_pe[:], k_pe[:], scaled2[:, 0, :], ALU.add).then_inc(s["pe_part"], 1)

            after(dve, "lat")
            with dve.Fori(0, 4) as p:
                used = [1, 1, 2, 2, 3]
                out_of = [kn[:, 0, :], kn[:, 1, :], qn[:, 0, :], qn[:, 1, :], q_pe[:]]
                gain = [V_KN, V_KN, V_QN, V_QN, V_QPE]
                for m in range(5):
                    dve.wait_ge(s["p_sq"], p * 5 + (m + 1))
                    if m < 2:
                        dve.tensor_copy(halves(out_of[m]), wide(2 * m)).then_inc(s["p_kept"], 1)
                    else:
                        dve.tensor_copy(out_of[m], ps[:, 2 + m, :]).then_inc(s["p_kept"], 1)
                    if m in (1, 3, 4):
                        make_high(dve, N_MLA + used[m] - 1 + 3, p * 4)
                for m in range(5):
                    n = L if m < 2 else S
                    dve.wait_ge(s["p_root"], p * 5 + (m + 1))
                    dve.scalar_tensor_tensor(out_of[m], out_of[m], col(gain[m]), root2[:, m % 2, 0:n],
                                             ALU.mult, ALU.mult).then_inc(s["p_normed"], 1)
                make_high(dve, N_MLA + 6, p * 4)
                dve.wait_ge(s["qr_turned"], p + 1)
                dve.tensor_tensor(scaled2[:, 1, 0:S], ps[:, 7, :], sin[:, META:L], ALU.mult).then_inc(s["qr_part"], 1)
                dve.tensor_tensor(q_pe[:], q_pe[:], cos[:, META:L], ALU.mult).then_inc(s["qr_part"], 1)
                dve.wait_ge(s["qr_part"], p * 3 + 2)
                dve.wait_ge(s["qr_part"], p * 3 + 1)
                dve.tensor_tensor(q_pe[:], q_pe[:], scaled2[:, 1, 0:S], ALU.add).then_inc(s["qr_part"], 1)

                def top(u):
                    dve.wait_ge(s["s_scored"], p * 8 + (u + 1))
                    if u >= 2:
                        dve.wait_ge(s["s_probs"], p * 8 + (u - 1))
                    dve.tensor_reduce(mm_[:, u % 2, 0:1], wide(2 * (u % 2)), AX.XY, ALU.max).then_inc(s["s_top"], 1)
                    dve.wait_ge(s["s_top"], p * 8 + (u + 1))
                    dve.tensor_scalar(mm_[:, u % 2, 1:2], mm_[:, u % 2, 0:1], -MLA_SCALE, None, ALU.mult)\
                        .then_inc(s["s_neg"], 1)

                top(0)
                for u in range(9):
                    if u < 7:
                        top(u + 1)
                    if u >= 1:
                        dve.wait_ge(s["s_turned"], p * 8 + u)
                        if u >= 2:
                            dve.wait_ge(s["s_summed"], p * 8 + (u - 1))
                        dve.tensor_copy(mp[0:META, 4 * P:5 * P], ps[0:META, 5, 0:P]).then_inc(s["s_copied_b"], 1)
                    if u < 8:
                        dve.wait_ge(s["s_exp"], p * 8 + (u + 1))
                        dve.reciprocal(mm_[:, u % 2, 3:4], mm_[:, u % 2, 2:3]).then_inc(s["s_inv"], 1)
                        dve.wait_ge(s["s_inv"], p * 8 + (u + 1))
                        dve.tensor_scalar(me[:, u % 2, :], me[:, u % 2, :], mm_[:, u % 2, 3:4], None, ALU.mult)\
                            .then_inc(s["s_probs"], 1)
                for h in range(2):
                    y = (y_f[:], scaled2[:, 0, 0:S])[h]
                    dve.wait_ge(s["s_summed"], p * 8 + 4 * (h + 1))
                    dve.tensor_tensor(y, ps[:, 6 + h, :], gm[:, bass.ds(p * 2 + h, 1), :], ALU.mult)\
                        .then_inc(s["s_y"], 1)
                for h in range(2):
                    y = (y_f[:], scaled2[:, 0, 0:S])[h]
                    dve.wait_ge(s["s_high"], p * 2 + (h + 1))
                    dve.tensor_tensor(y_low[:, bass.ds(p * 2 + h, 1), :], y,
                                      y_high[:, bass.ds(p * 2 + h, 1), :].bitcast(F32), ALU.subtract)\
                        .then_inc(s["s_low"], 1)

            with dve.Fori(0, 2) as i:
                add_out(N_OM, [0, 1, 2, 3], "om_added", i, 3)

            after(dve, "om")
            with dve.Fori(0, 8) as p:
                for m in range(2):
                    dve.wait_ge(s["q_sq"], p * 2 + (m + 1))
                    if m == 0:
                        dve.tensor_copy(halves(nk[:]), wide(0)).then_inc(s["q_kept"], 1)
                    else:
                        dve.tensor_copy(nq[:], ps[:, 2, :]).then_inc(s["q_kept"], 1)
                    make_high(dve, N_NA + m + 3, p * 4)
                for m in range(2):
                    n = L if m == 0 else S
                    dst = (nk, nq)[m][:]
                    dve.wait_ge(s["q_root"], p * 4 + (2 * m + 2))
                    dve.scalar_tensor_tensor(dst, dst, (col(V_NK), nq_gain[:, 0:1])[m], root2[:, m, 0:n],
                                             ALU.mult, ALU.mult).then_inc(s["q_normed"], 1)
                    if m == 1:
                        dve.wait_ge(s["t_scored"], p * 4 + 1)
                        dve.wait_ge(s["nb_ready"], p * 9 + 9)
                    make_high(dve, N_NA + m + 5, p * 4)

                def masked(t):
                    w = META + NA_W[t]
                    for h in range(2):
                        dve.tensor_tensor_reduce(ne[:, t % 2, h, 0:w], ps[:, 2 * (t % 2) + h, 0:w],
                                                 nb[:, h, NA_OFF[t]:NA_OFF[t] + w], 1.0, -3e38, ALU.add, ALU.max,
                                                 nm[:, t % 2, 2, h:h + 1]).then_inc(s["t_masked"], 1)
                    dve.wait_ge(s["t_masked"], p * 8 + (2 * t + 2))
                    dve.tensor_scalar(nm[:, t % 2, 0, :], nm[:, t % 2, 2, :], -1.0, None, ALU.mult)\
                        .then_inc(s["t_neg"], 1)

                masked(0)
                dve.wait_ge(s["g_exp"], p + 1)
                dve.tensor_copy(ng[:, 0, :], ps[:, 7, :]).then_inc(s["g_part"], 1)
                dve.wait_ge(s["g_exp"], p + 1)
                dve.tensor_scalar(ng[:, 1, :], ng[:, 1, :], 1.0, None, ALU.add).then_inc(s["g_part"], 1)
                dve.wait_ge(s["g_part"], p * 4 + 2)
                dve.reciprocal(ng[:, 1, :], ng[:, 1, :]).then_inc(s["g_part"], 1)
                dve.wait_ge(s["g_part"], p * 4 + 3)
                dve.wait_ge(s["g_part"], p * 4 + 1)
                dve.wait_ge(s["t_scored"], p * 4 + 2)
                dve.tensor_tensor(ng[:, 0, :], ng[:, 0, :], ng[:, 1, :], ALU.mult).then_inc(s["g_part"], 1)
                for t in range(5):
                    if t >= 1:
                        if t < 3:
                            dve.wait_ge(s["t_scored"], p * 4 + (t + 2))
                        dve.wait_ge(s["t_turned"], p * 4 + t)
                        if t >= 2:
                            dve.wait_ge(s["t_summed"], p * 4 + (t - 1))
                        if NA_W[t - 1] == 3 * P:
                            dve.tensor_copy(npt[:, 2, :], ps[:, 5, 0:2 * P])
                        dve.tensor_copy(npt[0:META, 3, :], ps[0:META, 5, 2 * P:4 * P]).then_inc(s["t_copied_b"], 1)
                    if t < 3:
                        masked(t + 1)
                    if t < 4:
                        w = META + NA_W[t]
                        dve.wait_ge(s["t_exp"], p * 8 + (2 * t + 2))
                        dve.reciprocal(nm[:, t % 2, 2, :], nm[:, t % 2, 1, :]).then_inc(s["t_inv"], 1)
                        dve.wait_ge(s["t_inv"], p * 4 + (t + 1))
                        for h in range(2):
                            dve.tensor_scalar(ne[:, t % 2, h, 0:w], ne[:, t % 2, h, 0:w], nm[:, t % 2, 2, h:h + 1],
                                              None, ALU.mult).then_inc(s["t_probs"], 1)
                    if t >= 1:
                        dve.wait_ge(s["t_summed"], p * 4 + t)
                        dve.wait_ge(s["g_part"], p * 4 + 4)
                        for h in range(2):
                            r = slice(h * HD, (h + 1) * HD)
                            q = slice((t - 1) * P, t * P)
                            dve.tensor_tensor(y_f[r, q], ps[r, 6, h * P:(h + 1) * P], ng[r, 0, q], ALU.mult)\
                                .then_inc(s["t_y"], 1)
                dve.wait_ge(s["t_high"], p + 1)
                dve.tensor_tensor(y_low[:, bass.ds(p, 1), :], y_f[:], y_high[:, bass.ds(p, 1), :].bitcast(F32),
                                  ALU.subtract).then_inc(s["t_low"], 1)

            for m in range(8):
                dve.wait_ge(strip_used, N_ON + m + 1)
                dve.tensor_tensor(x_t[:, m, :], x_t[:, m, :], ps[:, m, :], ALU.add).then_inc(s["on_added"], 1)
                make_high(dve, N_ON + m + 3)

            after(dve, "on")
            for t in range(4):
                dve.wait_ge(s["out_turned"], 2 * t + 2)
                dve.tensor_copy(y_tok[:, t, 512:D], ps[:, 2 * t + 1, :]).then_inc(s["out_right"], 1)


_INS = ["x", "mix_norm", "w_in", "q_norm", "k_norm", "sinks", "sgu_norm", "w_s", "b_s", "w_oa", "w_ob", "w_out",
        "ffn_norm", "w_up", "conv_w", "conv_b", "w_down", "meta_tokens_2", "norm_w_2", "w_in_2",
        "q_lat_norm_w_2", "kv_lat_norm_w_2", "w_uq_2", "w_ukv_2", "mla_qn_w_2", "mla_qpe_w_2", "mla_kn_w_2",
        "mla_kpe_w_2", "na_q_norm_w_2", "na_k_norm_w_2", "na_meta_bias_2", "w_out_2"]


def _grouped():
    g, r, c = np.meshgrid(np.arange(CG), np.arange(8), np.arange(16), indexing="ij")
    return (r * GW + g * 16 + c).ravel()


def _constants():
    f = np.float32
    i = np.arange(P)
    rot = np.zeros((P, P), f)
    for b in (0, 64):
        for d in range(32):
            rot[b + d + 32, b + d] = -1
            rot[b + d, b + d + 32] = 1
    pos = np.concatenate([np.arange(META), META + _grouped()]).astype(f)
    inv = (f(10000.0) ** (-(np.arange(0, 64, 2, dtype=f) / f(64)))).astype(f)
    ang = (pos[None, :] * np.tile(inv, 4)[:, None]).astype(f)
    gap = i[:, None] + P - np.arange(2 * P)[None, :]
    dist = np.where((gap >= 0) & (gap < 128), -gap, -1e33).astype(f)
    slope = np.broadcast_to(np.exp2(-(np.arange(ATT_H) + 1.0)).astype(f), (P, ATT_H))
    cq = i % 16
    ck = np.arange(3 * P) % 16 + np.arange(3 * P) // P * 16

    def window(first, at, n):
        c0 = np.clip(at + cq - 8, 0, GW - 16)
        k = first + ck[:n]
        return np.where((k[None, :] >= c0[:, None]) & (k[None, :] < c0[:, None] + 16), 0, -1e30)

    mask = np.concatenate([window(0, 16, 3 * P), window(0, 0, 2 * P), window(32, 48, 2 * P)], 1).astype(f)
    return {"c_ident": np.eye(P, dtype=f), "c_blocks": np.kron(np.eye(2), np.ones((64, 64))).astype(f),
            "c_rot": rot, "c_cos": np.cos(ang).astype(f), "c_sin": np.sin(ang).astype(f), "c_dist": dist,
            "c_slope": slope, "c_mask": mask}


def _relative():
    q, k = np.arange(P), np.arange(3 * P)
    dr = (k % P // 16)[None, :] - (q // 16)[:, None] + 7
    dc = (k // P * 16 - 16 + k % 16)[None, :] - (q % 16)[:, None] + 15
    return dr, np.clip(dc, 0, 30)


def kernel(**inputs):
    import concourse.bacc as _bacc
    from concourse.bass_utils import run_bass_kernel_spmd as _run

    nc = _bacc.Bacc("TRN2", target_bir_lowering=False, num_devices=1)
    feeds = {n: inputs[n] for n in _INS}
    dr, dc = _relative()
    feeds["rel_bias"] = np.asarray(inputs["na_rel_bias_2"])[0][:, dr, dc]
    feeds.update(_constants())
    arrays, args = {}, []
    for name, a in feeds.items():
        a = np.ascontiguousarray(a)
        arrays[f"in_{name}_dram"] = a
        args.append(nc.dram_tensor(f"in_{name}_dram", a.shape, mybir.dt.from_np(a.dtype), kind="ExternalInput").ap())
    args.append(nc.dram_tensor("out_0_dram", (1, S, D), F32, kind="ExternalOutput").ap())
    program(nc, *args)
    r = _run(nc, [arrays], core_ids=[0])
    return r.results[0]["out_0_dram"]
```

```python
from contextlib import ExitStack

import numpy as np

import concourse.bass as bass
from concourse import mybir

ACT = mybir.ActivationFunctionType
ALU = mybir.AluOpType
AX = mybir.AxisListType
F32 = mybir.dt.float32
F32R = mybir.dt.float32r

P = 128
D = 1024
KT = D // P
S = 512
META = 16
L = S + META
HALF = L // 2
EPS = 1e-6
ATT_H, KV_H, HD = 8, 2, 64
SGU = 512
FF = 2816
FT = FF // P
MH = 8
MLA_SCALE = 192.0 ** -0.5
NH = 16
GW = 64
CG = 4

N_SGU = 0
N_QKV = N_SGU + 8
N_GATE = N_QKV + 6
N_MERGE = N_GATE + 16
N_OUT = N_MERGE + 8
N_UP = N_OUT + 8
N_DOWN = N_UP + 2 * FT
N_GM = N_DOWN + 3 * KT
N_LAT = N_GM + 8
N_MLA = N_LAT + 5
N_OM = N_MLA + 16
N_NA = N_OM + 8
N_ON = N_NA + 32
N_END = N_ON + 8
RAW = 2
RING = 4

V_MIX, V_FFN, V_N2, V_QL, V_KL, V_QN, V_KN, V_SGU = 0, 8, 16, 24, 26, 28, 29, 30
V_AQ, V_AK, V_NQ, V_NK, V_QPE, V_KPE, V_ROWS = 34, 35, 36, 37, 38, 39, 40
C_CONV, C_CONVB = 0, 3 * 2 * FT
C_V = C_CONVB + 2 * FT

NA_W = [2 * P, 3 * P, 3 * P, 2 * P]
NA_G = [0, 0, 1, 2]
NA_OFF = [META + 3 * P, 0, 0, 2 * META + 5 * P]
NA_COLS = 3 * META + 7 * P
EARLY = 3
MASK_COLS = 7 * P


def program(nc, x, mix_norm, w_in, q_norm, k_norm, sinks, sgu_norm, w_s, b_s, w_oa, w_ob, w_out,
            ffn_norm, w_up, conv_w, conv_b, w_down, meta_tokens_2, norm_w_2, w_in_2,
            q_lat_norm_w_2, kv_lat_norm_w_2, w_uq_2, w_ukv_2, mla_qn_w_2, mla_qpe_w_2, mla_kn_w_2,
            mla_kpe_w_2, na_q_norm_w_2, na_k_norm_w_2, na_meta_bias_2, w_out_2, rel_bias,
            c_ident, c_blocks, c_rot, c_cos, c_sin, c_dist, c_slope, c_mask, out):
    with ExitStack() as ctx:
        def sb(name, shape, dt=F32, at=ctx):
            return at.enter_context(nc.sbuf_tensor(name, shape, dt))

        def sem(name):
            return ctx.enter_context(nc.semaphore(name))

        ident = sb("ident", [P, P])
        ones = sb("ones", [P, P])
        blocks = sb("blocks", [P, P])
        rot = sb("rot", [P, P])
        eps = sb("eps", [P, 1])
        cv = sb("cv", [P, C_V + V_ROWS])
        aq_gain = sb("aq_gain", [P, 1])
        nq_gain = sb("nq_gain", [P, 1])
        x_t = sb("x_t", [P, KT, S])
        h_high = sb("h_high", [P, KT, L], F32R)
        h_low = sb("h_low", [P, KT, L], F32R)
        w_raw = sb("w_raw", [P, RAW, KT * P])
        w_high = sb("w_high", [P, RING, KT * P], F32R)
        w_low = sb("w_low", [P, RING, KT * P], F32R)
        with ExitStack() as one:
            sq = sb("sq", [P, 2, L], F32, one)
            root = sb("root", [P, 2, L], F32, one)
            scaled = sb("scaled", [P, 2, S], F32, one)
            a_high = sb("a_high", [P, 8, S], F32R, one)
            a_low = sb("a_low", [P, 8, S], F32R, one)
            bias_s = sb("bias_s", [P, 4, P], F32, one)
            dist = sb("dist", [P, 2 * P], F32, one)
            slope = sb("slope", [P, ATT_H], F32, one)
            sink = sb("sink", [P, ATT_H], F32, one)
            k_t = sb("k_t", [P, S], F32, one)
            q_t = sb("q_t", [P, 4, S], F32, one)
            v_f = sb("v_f", [P, S], F32, one)
            v_tok = sb("v_tok", [P, 4, P], F32, one)
            with ExitStack() as a:
                x_tok = sb("x_tok", [P, 4, D], F32, a)
                meta_tok = sb("meta_tok", [META, D], F32, a)
                meta_t = sb("meta_t", [P, KT, META], F32, a)
                rows_a = sb("rows_a", [4 * FT, P], F32, a)
                rows_b = sb("rows_b", [4 * FT, P], F32, a)
                rows_v = sb("rows_v", [V_ROWS, P], F32, a)
            with ExitStack() as a:
                uv = sb("uv", [P, 8, S], F32, a)
                uv_tok = sb("uv_tok", [P, 4, SGU], F32, a)
            with ExitStack() as a:
                gates = sb("gates", [P, 16, S], F32, a)
                ws_raw = sb("ws_raw", [P, 8, P], F32, a)
                ws_t = sb("ws_t", [P, 8, P], F32, a)
            with ExitStack() as a:
                a.enter_context(nc.sbuf_tensor("gates_", [P, 16, S], F32))
                q_st = sb("q_st", [P, S], F32, a)
                bias_h = sb("bias_h", [P, 2, 2 * P], F32, a)
                att_e = sb("att_e", [P, 2, 2 * P], F32, a)
                att_p = sb("att_p", [P, 4, P], F32, a)
                att_m = sb("att_m", [P, 6, 2], F32, a)
                att_y = sb("att_y", [P, S], F32, a)
            merge = scaled
        with ExitStack() as two:
            m_high = sb("m_high", [P, FT, S], F32R, two)
            m_low = sb("m_low", [P, FT, S], F32R, two)
            z = sb("z", [P, 4, S], F32, two)
            zg = sb("zg", [P, 2, S], F32, two)
        with ExitStack() as three:
            sq2 = sb("sq2", [P, 2, L], F32, three)
            root2 = sb("root2", [P, 2, L], F32, three)
            scaled2 = sb("scaled2", [P, 2, L], F32, three)
            y_high = sb("y_high", [P, 8, S], F32R, three)
            y_low = sb("y_low", [P, 8, S], F32R, three)
            y_f = sb("y_f", [P, S], F32, three)
            with ExitStack() as a:
                cos = sb("cos", [P, L], F32, a)
                sin = sb("sin", [P, L], F32, a)
                gm = sb("gm", [P, MH, S], F32, a)
                ql_high = sb("ql_high", [P, 2, S], F32R, a)
                ql_low = sb("ql_low", [P, 2, S], F32R, a)
                kl_high = sb("kl_high", [P, 2, L], F32R, a)
                kl_low = sb("kl_low", [P, 2, L], F32R, a)
                k_pe = sb("k_pe", [P, L], F32, a)
                q_pe = sb("q_pe", [P, S], F32, a)
                kn = sb("kn", [P, 2, L], F32, a)
                qn = sb("qn", [P, 2, S], F32, a)
                me = sb("me", [P, 2, L], F32, a)
                mv = sb("mv", [P, 5, 2 * P], F32, a)
                mp = sb("mp", [P, 5 * P], F32, a)
                mm_ = sb("mm_", [P, 2, 4], F32, a)
                mvf = sq2
            with ExitStack() as a:
                mask = sb("mask", [P, MASK_COLS], F32, a)
                meta_b = sb("meta_b", [P, NH * META], F32, a)
                rel = sb("rel", [P, 2, 2, 3 * P], F32, a)
                nb = sb("nb", [P, 2, 2, NA_COLS], F32, a)
                nk = sb("nk", [P, 2, L], F32, a)
                nq = sb("nq", [P, 2, S], F32, a)
                nv = sb("nv", [P, 2, 5, P], F32, a)
                ng = sb("ng", [P, 2, S], F32, a)
                nvf = sb("nvf", [P, L], F32, a)
                sig = sb("sig", [P, S], F32, a)
                ne = sb("ne", [P, 2, 2, META + 3 * P], F32, a)
                npt = sb("npt", [P, 4, 2 * P], F32, a)
                nm = sb("nm", [P, 2, 4, 2], F32, a)
                no = sb("no", [P, 2, P], F32, a)
                ny = sb("ny", [P, 2, P], F32, a)
            with ExitStack() as a:
                y_tok = sb("y_tok", [P, 4, D], F32, a)
        ps = ctx.enter_context(nc.psum_tensor("ps", [P, 8, 512], F32))

        def wide(bank):
            return ps[:, bank:bank + 2, 0:HALF]

        def halves(ap):
            return ap.rearrange("p (h c) -> p h c", h=2)

        landed = [sem(f"strip_landed_{i}") for i in range(RAW)]
        high_made = sem("high_made")
        low_made = sem("low_made")
        strip_used = sem("strip_used")

        def strip_sources(n, i):
            def cols(w, c, k0=0, kn=KT):
                v = w[0].rearrange("(k p) c -> p k c", p=P)
                h = (kn + 1) // 2
                return [(slice(0, P), (a, b), P, v[:, k0 + a:k0 + b, bass.ds(c, P)])
                        for a, b in ((0, h), (h, kn))]
            if n < N_QKV:
                return cols(w_in, (n - N_SGU + i) * P + 768)
            if n < N_GATE:
                m = n - N_QKV
                if m < 2:
                    return cols(w_in, 512 + m * P)
                v = w_in[0].rearrange("(k p) c -> p k c", p=P)
                return [("c", g * HD, HD, v[:, :, g * 256 + (m - 2) * HD:g * 256 + (m - 1) * HD])
                        for g in range(2)]
            if n < N_MERGE:
                return cols(w_in, (n - N_GATE + i) * P + 1792)
            if n < N_OUT:
                m = n - N_MERGE
                c = i * P + ((m - m % 4) * P + (m % 4) // 2 * 256)
                if m % 2 == 0:
                    v = w_oa[0].rearrange("(g j d) c -> g d j c", g=2, d=HD)
                    return [(slice(g * HD, g * HD + HD), (0, 4), 256, v[g][:, :, bass.ds(c, 256)])
                            for g in range(2)]
                v = w_ob[0].rearrange("(k p) c -> p k c", p=P)
                return [(slice(0, P), (a, a + 2), 256, v[:, a:a + 2, bass.ds(c, 256)]) for a in (0, 2)]
            if n < N_UP:
                return cols(w_out, (n - N_OUT + i) * P)
            if n < N_DOWN:
                m = n - N_UP
                c = ((m - m % 4) // 2 + m % 2) * P + (m % 4) // 2 * FF
                return cols(w_up, i * (P // 2) + c)
            if n < N_GM:
                m, part = divmod(n - N_DOWN, 3)
                return cols(w_down, i * P + m * P, 8 * part, 8 if part < 2 else 6)
            if n < N_LAT:
                return cols(w_in_2, (n - N_GM + i) * P + 576)
            if n < N_MLA:
                m = n - N_LAT
                if m < 4:
                    return cols(w_in_2, m * P)
                v = w_in_2[0].rearrange("(k p) c -> p k c", p=P)
                return [("c", g * 64, 64, v[:, :, 512:576]) for g in range(2)]
            if n < N_OM:
                m = n - N_MLA
                pair = (m - m % 4) // 4
                s = m % 4
                w, head, off, width = ((w_ukv_2, 256, 0, P), (w_uq_2, 192, 0, P), (w_uq_2, 192, P, 64),
                                       (w_ukv_2, 256, P, P))[s]
                v = w[0].rearrange("(k p) c -> p k c", p=P)
                base = i * (head // 2) + pair * 2 * head + off
                return [("h", h * width, (2, 2 * width), v[:, :, bass.ds(base + h * head, width)])
                        for h in range(2)]
            if n < N_NA:
                return cols(w_out_2, (n - N_OM + i) * P)
            if n < N_ON:
                m = n - N_NA
                pair, s = (m - m % 4) // 4, m % 4
                c = (2624, 1600, 3648, 4672)[s]
                return cols(w_in_2, i * (P // 4) + pair * P + c)
            return cols(w_out_2, (n - N_ON + i) * P, KT)

        def load_strip(sp, n, i=0):
            if n >= RAW:
                sp.wait_ge(low_made, i + (n - RAW + 1))
            slot = w_raw[:, n % RAW, :]
            for load in strip_sources(n, i):
                if load[0] == "c":
                    _, c, width, src = load
                    dst = slot.rearrange("p (k c) -> p k c", c=P)[:, :, c:c + width]
                elif load[0] == "h":
                    _, c, (k, row), src = load
                    dst = slot[:, 0:k * row].rearrange("p (k c) -> p k c", k=k)[:, :, c:c + row // 2]
                else:
                    rows, (a, b), width, src = load
                    dst = slot.rearrange("p (k c) -> p k c", c=width)[rows, a:b, :]
                sp.dma_start(dst, src).then_inc(landed[n % RAW], 16)

        def make_high(dve, n, i=0):
            if isinstance(i, int) and n + i >= N_END:
                return
            dve.wait_ge(landed[n % RAW], i * 16 + 32 * (n // RAW + 1))
            if n >= RING:
                dve.wait_ge(strip_used, i + (n - RING + 1))
            dve.tensor_copy(w_high[:, n % RING, :], w_raw[:, n % RAW, :]).then_inc(high_made, 1)

        def make_low(pool, n, i=0):
            pool.wait_ge(high_made, i + (n + 1))
            pool.tensor_tensor(w_low[:, n % RING, :], w_raw[:, n % RAW, :],
                               w_high[:, n % RING, :].bitcast(F32), ALU.subtract).then_inc(low_made, 1)

        def product(pe, acc, n, col, step, tiles, moving, first=True, last=True):
            for k in range(tiles):
                c = col + k * step
                wh, wl = w_high[:, n % RING, c:c + P], w_low[:, n % RING, c:c + P]
                mh, ml = moving(k)
                pe.matmul(acc, wh, mh, start=first and k == 0, stop=False)
                pe.matmul(acc, wh, ml, start=False, stop=False)
                done = pe.matmul(acc, wl, mh, start=False, stop=last and k == tiles - 1)
            return done

        def product_wide(pe, bank, n, col, step, tiles, high, low):
            for k in range(tiles):
                c = col + k * step
                wh, wl = w_high[:, n % RING, c:c + P], w_low[:, n % RING, c:c + P]
                for wt, mt, one_, end in ((wh, high, k == 0, False), (wh, low, False, False),
                                          (wl, high, False, k == tiles - 1)):
                    for h in range(2):
                        done = pe.matmul(ps[:, bank + h, 0:HALF], wt, mt[:, k, h * HALF:h * HALF + HALF],
                                         start=one_, stop=end)
            return done

        def hx(k):
            return h_high[:, k, META:L], h_low[:, k, META:L]

        def yx(k):
            return y_high[:, k, :], y_low[:, k, :]

        names = """consts_in x_in meta_in ones_set x_turned x_ready rows_turned cols_ready gain_ready meta_turned
            meta_ready ws_cut ws_turned ws_ready
            norm_sq norm_sum norm_root norm_scaled norm_high norm_low
            gelu_done sv_sq sv_sum sv_root  sv_normed sv_turned sv_tok_ready mixed mix_biased mix_gated
            mix_high mix_low
            i1_sq i1_sum i1_ln i1_root i1_normed v_copied v_turned v_ready
            j_staged j_bias a_scored a_masked a_part   a_exp a_sink_exp   a_probs a_turned
            a_copied a_summed a_y a_high a_low gate_kept
            g_sig m_part m_whole m_high_ m_low_ o_added
            z_first z_mid z_done z_silu z_gated z_high z_low d_added d_placed
            gm_done lat_sq lat_sum lat_root  lat_scaled lat_high lat_low pe_root_part pe_sum  
            pe_part  pe_turned    tables_in
            p_sq p_kept p_sum p_ln p_root p_normed qr_turned  qr_part  mv_kept mv_turned mv_ready
            s_scored s_top s_neg s_exp s_inv s_probs s_turned s_copied_a s_copied_b s_summed s_y s_high s_low
            om_added rel_in nb_ready
            q_sq q_kept q_sum q_root q_normed nv_kept nv_turned nv_ready g_part g_done
            t_scored t_masked t_neg t_exp t_inv t_turned t_copied_a t_copied_b t_summed t_out t_back t_y
            t_high t_low
            on_added out_turned out_left out_right out_stored""".split()
        s = {name: sem(name) for name in names}
        N_CONST = 33

        ends = {
            "setup": [("x_ready", 8), ("gain_ready", 2), ("meta_ready", 1), ("norm_low", 16)],
            "sgu": [("gelu_done", 8)],
            "qkv": [("i1_normed", 5), ("v_ready", 1), ("sv_normed", 4)],
            "mix": [("mix_low", 4), ("sv_tok_ready", 4), ("mixed", 4)],
            "att": [("a_low", 4), ("gate_kept", 16)],
            "merge": [("m_low_", 8)],
            "out": [("o_added", 8)],
            "norm2": [("norm_low", 24)],
            "up": [("z_low", FT)],
            "down": [("d_placed", 8)],
            "norm3": [("norm_low", 32)],
            "gm": [("gm_done", 8)],
            "lat": [("lat_low", 4), ("pe_part", 5)],
            "mla": [("s_low", 8)],
            "om": [("om_added", 8)],
            "na": [("t_low", 32)],
            "on": [("on_added", 8)],
        }

        def after(eng, stage):
            for name, value in ends[stage]:
                eng.wait_ge(s[name], value)

        def col(c):
            return cv[:, C_V + c:C_V + c + 1]

        def norm_pe(pe, t, acc, sq_, n):
            for k in range(KT):
                pe.wait_ge(s["norm_sq"], 8 * t + k + 1)
                pe.matmul(acc, ones[:], sq_[:, k % 2, 0:n], start=k == 0, stop=k == KT - 1)\
                    .then_inc(s["norm_sum"], 1)

        def norm_act(act, t, acc, src, sq_, root_, scaled_, n, high, ready=None):
            for k in range(KT):
                if ready:
                    act.wait_ge(s[ready], k + 1)
                if k >= 2:
                    act.wait_ge(s["norm_sum"], 8 * t + k - 1)
                act.activation(sq_[:, k % 2, 0:n], src(k), ACT.Square).then_inc(s["norm_sq"], 1)
            act.wait_ge(s["norm_sum"], 8 * t + KT)
            act.activation(root_[:, 0, 0:n], acc, ACT.Ln, bias=eps[:, 0:1], scale=1.0 / D).then_inc(s["norm_root"], 1)
            act.wait_ge(s["norm_root"], 2 * t + 1)
            act.activation(root_[:, 0, 0:n], root_[:, 0, 0:n], ACT.Exp, scale=-0.5).then_inc(s["norm_root"], 1)
            for k in range(KT):
                act.wait_ge(s["norm_scaled"], 8 * t + k + 1)
                act.activation(high(k), scaled_[:, k % 2, 0:n], ACT.Copy).then_inc(s["norm_high"], 1)

        def norm_dve(dve, t, src, gain, root_, scaled_, n, high, low):
            dve.wait_ge(s["norm_root"], 2 * t + 2)
            for k in range(KT + 1):
                if k < KT:
                    if k >= 2:
                        dve.wait_ge(s["norm_low"], 8 * t + k - 1)
                    dve.scalar_tensor_tensor(scaled_[:, k % 2, 0:n], src(k), col(gain + k), root_[:, 0, 0:n],
                                             ALU.mult, ALU.mult).then_inc(s["norm_scaled"], 1)
                if k >= 1:
                    dve.wait_ge(s["norm_high"], 8 * t + k)
                    dve.tensor_tensor(low(k - 1), scaled_[:, (k - 1) % 2, 0:n], high(k - 1).bitcast(F32),
                                      ALU.subtract).then_inc(s["norm_low"], 1)

        def xs(k):
            return x_t[:, k, :]

        def hh(k):
            return h_high[:, k, META:L]

        def hl(k):
            return h_low[:, k, META:L]

        block = ctx.enter_context(nc.Block())

        @block.sync
        def _(sp):
            for t in range(4):
                sp.dma_start(x_tok[:, t, :], x[0, t * P:(t + 1) * P, :]).then_inc(s["x_in"], 16)
            for n in range(RAW):
                load_strip(sp, n)
            sp.dma_start(ws_raw[:], w_s[0].rearrange("g i j -> i g j")).then_inc(s["meta_in"], 16)
            for n in range(RAW, 4):
                load_strip(sp, n)
            for n in range(4, N_GATE):
                load_strip(sp, n)
            for n0, n1, step in ((N_GATE, N_MERGE, 4), (N_MERGE, N_OUT, 4), (N_OUT, N_UP, 4), (N_UP, N_DOWN, 4)):
                with sp.Fori(0, (n1 - n0) // step) as turn:
                    i = turn * step
                    for n in range(n0, n0 + step):
                        load_strip(sp, n, i)
            with sp.Fori(0, 2) as i:
                for n in range(N_DOWN, N_DOWN + 12):
                    sp.wait_ge(low_made, i * 12 + (n - RAW + 1))
                    slot = w_raw[:, n % RAW, :].rearrange("p (k c) -> p k c", c=P)
                    for rows, (a, b), width, src in strip_sources(n, i * 4):
                        sp.dma_start(slot[:, a:b, :], src).then_inc(landed[n % RAW], 16)
            with sp.Fori(0, 2) as turn:
                i = turn * 4
                for n in range(N_GM, N_GM + 4):
                    load_strip(sp, n, i)
            after(sp, "down")
            sp.dma_start(cos[:], c_cos).then_inc(s["tables_in"], 16)
            sp.dma_start(sin[:], c_sin).then_inc(s["tables_in"], 16)
            for n in range(N_LAT, N_MLA):
                load_strip(sp, n)
            for n0, n1 in ((N_MLA, N_OM), (N_OM, N_NA)):
                with sp.Fori(0, (n1 - n0) // 4) as turn:
                    i = turn * 4
                    for n in range(n0, n0 + 4):
                        load_strip(sp, n, i)
            for n in range(N_NA, N_NA + 3):
                load_strip(sp, n)
            after(sp, "mla")
            sp.dma_start(mask[:], c_mask).then_inc(s["tables_in"], 16)
            sp.dma_start(meta_b[:], na_meta_bias_2[0].rearrange("h m -> (h m)").partition_broadcast(P))\
                .then_inc(s["tables_in"], 16)
            sp.dma_start(rel[:, 0], rel_bias[0:2].rearrange("h q k -> q h k")).then_inc(s["rel_in"], 16)
            for n in range(N_NA + 3, N_NA + 4):
                load_strip(sp, n)

            def na_loads(i, c):
                for m in range(4):
                    load_strip(sp, N_NA + 4 * c + m, i * 8)
                    if m == 1:
                        sp.wait_ge(s["nb_ready"], i * 18 + 9 * c)
                        sp.dma_start(rel[:, c % 2], rel_bias[bass.ds(i * 4 + 2 * c, 2)].rearrange("h q k -> q h k"))\
                            .then_inc(s["rel_in"], 16)

            with sp.Fori(0, 3) as i:
                na_loads(i, 1)
                na_loads(i, 2)
            na_loads(3, 1)
            for n in range(N_ON, N_END):
                load_strip(sp, n)
            for t in range(4):
                sp.wait_ge(s["out_left"], t + 1)
                sp.wait_ge(s["out_right"], t + 1)
                dst = out[0].rearrange("(r g c) d -> g r c d", g=CG, c=16)[t]
                for r in range(8):
                    sp.dma_start(dst[r], y_tok[r * 16:(r + 1) * 16, t, :]).then_inc(s["out_stored"], 16)
            sp.wait_ge(s["out_stored"], 16 * 32)

        @block.gpsimd
        def _(pool):
            nc.gpsimd.memset(ones[:], 1.0).then_inc(s["ones_set"], 1)
            nc.gpsimd.memset(eps[:], EPS).then_inc(s["ones_set"], 1)
            for n in range(0, N_GATE):
                make_low(pool, n)
                if n == 3:
                    pool.wait_ge(s["meta_in"], 16)
                    pool.affine_select(out=ws_raw[:], in_=ws_raw[:], compare_op=ALU.is_ge, fill=0.0, base=0,
                                       pattern=[[0, 8], [-1, P]], channel_multiplier=1).then_inc(s["ws_cut"], 1)
            for n0, n1, step in ((N_GATE, N_MERGE, 4), (N_MERGE, N_OUT, 4), (N_OUT, N_UP, 4), (N_UP, N_DOWN, 4),
                                 (N_DOWN, N_GM, 12), (N_GM, N_LAT, 4)):
                with pool.Fori(0, (n1 - n0) // step) as turn:
                    i = turn * step
                    for n in range(n0, n0 + step):
                        make_low(pool, n, i)
            for n in range(N_LAT, N_MLA):
                make_low(pool, n)
            for n0, n1 in ((N_MLA, N_OM), (N_OM, N_NA)):
                with pool.Fori(0, (n1 - n0) // 4) as turn:
                    i = turn * 4
                    for n in range(n0, n0 + 4):
                        make_low(pool, n, i)
            for n in range(N_NA, N_NA + 4):
                make_low(pool, n)

            def bias_table(i, c):
                pool.wait_ge(s["rel_in"], i * 32 + (16 * c + 16))
                if c:
                    pool.wait_ge(s["q_normed"], i * 4 + 2 * c)
                z_ = c % 2
                for h in range(2):
                    for o, m, r in ((0, 0, 0), (META + 3 * P, 3 * P, P), (2 * META + 5 * P, 5 * P, 0)):
                        w = 3 * P if o == 0 else 2 * P
                        pool.tensor_tensor(nb[:, z_, h, o + META:o + META + w], rel[:, z_, h, r:r + w],
                                           mask[:, m:m + w], ALU.add).then_inc(s["nb_ready"], 1)
                for o in (0, META + 3 * P, 2 * META + 5 * P):
                    pool.tensor_copy(nb[:, z_, :, o:o + META],
                                     meta_b[:, bass.ds(i * 64 + 32 * c, 32)].rearrange("p (h m) -> p h m", h=2))\
                        .then_inc(s["nb_ready"], 1)

            pool.wait_ge(s["tables_in"], 64)
            bias_table(0, 0)
            with pool.Fori(0, 3) as i:
                for c in (1, 2):
                    for m in range(4):
                        make_low(pool, N_NA + 4 * c + m, i * 8)
                    bias_table(i, c)
            for m in range(4):
                make_low(pool, N_NA + 28 + m)
            bias_table(3, 1)
            for n in range(N_ON, N_END):
                make_low(pool, n)

        @block.tensor
        def _(pe):
            pe.wait_ge(s["consts_in"], 16 * N_CONST)
            pe.transpose(ps[:, 7, 0:88], rows_a[:], ident[0:88, 0:88])
            pe.transpose(ps[:, 7, 88:176], rows_b[:], ident[0:88, 0:88])
            pe.transpose(ps[:, 7, 176:176 + V_ROWS], rows_v[:], ident[0:V_ROWS, 0:V_ROWS])\
                .then_inc(s["rows_turned"], 1)
            for k in range(KT):
                t = pe.transpose(ps[:, 2, k * META:(k + 1) * META], meta_tok[:, k * P:(k + 1) * P],
                                 ident[0:META, 0:META])
            t.then_inc(s["meta_turned"], 1)
            pe.wait_ge(s["x_in"], 64)
            for k in range(KT):
                if k >= 2:
                    pe.wait_ge(s["x_ready"], k - 1)
                for t in range(4):
                    mm = pe.transpose(ps[:, k % 2, t * P:(t + 1) * P], x_tok[:, t, k * P:(k + 1) * P], ident[:])
                mm.then_inc(s["x_turned"], 1)
            pe.wait_ge(s["ones_set"], 2)
            norm_pe(pe, 0, ps[:, 4, 0:META], sq, META)
            norm_pe(pe, 1, ps[:, 3, :], sq, S)

            for n in range(N_SGU, N_QKV):
                pe.wait_ge(low_made, n + 1)
                if n == 0:
                    after(pe, "setup")
                if n >= 4:
                    pe.wait_ge(s["gelu_done"], n - 3)
                product(pe, ps[:, n % 4, :], n, 0, P, KT, hx).then_inc(strip_used, 1)

            bank = [4, 5, 6, 7, 4, 5]
            item = [0, None, 1, 2, 3, 4]

            def qkv_sum(m):
                j = item[m]
                pe.wait_ge(s["i1_sq"], j + 1)
                if m in (0, 2, 3):
                    pass
                if j >= 2:
                    pe.wait_ge(s["i1_root"], j - 1)
                pe.matmul(ps[:, j % 2, :], blocks[:], sq[:, j % 2, 0:S], start=True, stop=True)\
                    .then_inc(s["i1_sum"], 1)

            def sv_sum(k):
                pe.wait_ge(s["sv_sq"], k + 1)
                pe.matmul(ps[:, 2, :], ones[:], sq[:, k % 2, 0:S], start=k == 0, stop=k == 3).then_inc(s["sv_sum"], 1)

            for m in range(6):
                n = N_QKV + m
                pe.wait_ge(low_made, n + 1)
                if m >= 4:
                    pe.wait_ge(s["i1_normed"], 1) if m == 4 else pe.wait_ge(s["v_copied"], 1)
                product(pe, ps[:, bank[m], :], n, 0, P, KT, hx).then_inc(strip_used, 1)
                if m == 0:
                    pe.wait_ge(s["gelu_done"], 8)
                    for k in range(4):
                        sv_sum(k)
                    qkv_sum(0)
                elif m == 2:
                    pe.wait_ge(s["v_copied"], 1)
                    for t in range(4):
                        mm = pe.transpose(ps[:, 3, t * P:(t + 1) * P], v_f[:, t * P:(t + 1) * P], ident[:])
                    mm.then_inc(s["v_turned"], 1)
                    qkv_sum(2)
                elif m > 2:
                    qkv_sum(m)

            after(pe, "qkv")
            pe.wait_ge(s["ws_cut"], 1)
            for g in range(8):
                mm = pe.transpose(ps[:, 6 + g // 4, (g % 4) * P:(g % 4 + 1) * P], ws_raw[:, g, :], ident[:])
            mm.then_inc(s["ws_turned"], 1)
            for c in range(4):
                if c >= 2:
                    pe.wait_ge(s["sv_tok_ready"], c - 1)
                for k in range(4):
                    mm = pe.transpose(ps[:, c % 2, k * P:(k + 1) * P], uv[:, 4 + k, c * P:(c + 1) * P], ident[:])
                mm.then_inc(s["sv_turned"], 1)
            pe.wait_ge(s["ws_ready"], 1)
            pe.wait_ge(s["sv_tok_ready"], 4)
            for q in range(4):
                if q >= 2:
                    pe.wait_ge(s["mix_biased"], 2 * (q - 1))
                for c in range(4):
                    mm = pe.matmul(ps[:, 2 + 2 * (q % 2) + c // 2, (c % 2) * 256:(c % 2) * 256 + 256],
                                   uv_tok[:, c, q * P:(q + 1) * P],
                                   ws_t[:, 2 * q:2 * q + 2, :].rearrange("p g i -> p (g i)"), start=True, stop=True)
                mm.then_inc(s["mixed"], 1)

            after(pe, "mix")
            with pe.Fori(0, 4) as j:
                def scores(t):
                    w = 2 * P if t else P
                    pe.wait_ge(s["j_staged"], j + 1)
                    if t:
                        pe.wait_ge(s["a_masked"], j * 8 + 2 * t)
                    for h in range(2):
                        mm = pe.matmul(ps[:, h, 0:w], q_st[h * HD:(h + 1) * HD, t * P:(t + 1) * P],
                                       k_t[h * HD:(h + 1) * HD, (t + 1) * P - w:(t + 1) * P], start=True, stop=True)
                    mm.then_inc(s["a_scored"], 1)

                def turn(t):
                    pe.wait_ge(s["a_probs"], j * 8 + (2 * t + 2))
                    for a in range(2 if t else 1):
                        for h in range(2):
                            mm = pe.transpose(ps[:, 2, (2 * a + h) * P:(2 * a + h + 1) * P],
                                              att_e[:, h, a * P:(a + 1) * P], ident[:])
                    mm.then_inc(s["a_turned"], 1)

                def weigh(t):
                    pe.wait_ge(s["a_copied"], j * 4 + (t + 1))
                    if t:
                        pe.wait_ge(s["a_y"], j * 8 + 2 * t)
                    ks = [t - 1, t] if t else [0]
                    for a, kt in enumerate(ks):
                        mm = pe.matmul(ps[:, 3, 0:2 * P], v_tok[:, kt, :],
                                       att_p[:, 2 * a:2 * a + 2, :].rearrange("p h q -> p (h q)"),
                                       start=a == 0, stop=a == len(ks) - 1)
                    mm.then_inc(s["a_summed"], 1)

                scores(0)
                for t in range(4):
                    pe.wait_ge(low_made, j * 4 + (N_GATE + t + 1))
                    if t >= 2:
                        pe.wait_ge(s["gate_kept"], j * 4 + (t - 1))
                    product(pe, ps[:, 4 + t, :], N_GATE + t, 0, P, KT, hx).then_inc(strip_used, 1)
                    turn(t)
                    if t < 3:
                        scores(t + 1)
                    weigh(t)
                pe.wait_ge(s["gate_kept"], j * 4 + 3)

            after(pe, "att")
            with pe.Fori(0, 2) as i:
                for u in range(2):
                    for b in range(2):
                        n = N_MERGE + 2 * u + b
                        pe.wait_ge(low_made, i * 4 + (n + 1))
                        for m in range(2):
                            mm = product(pe, ps[:, 4 * b + 2 * u + m, :], n, m * P, 2 * P, 4,
                                         lambda k: (a_high[:, 4 * b + k, :], a_low[:, 4 * b + k, :]))
                        mm.then_inc(strip_used, 1)
                pe.wait_ge(s["m_part"], i * 8 + 8)

            after(pe, "merge")
            with pe.Fori(0, 2) as i:
                for m in range(4):
                    pe.wait_ge(low_made, i * 4 + (N_OUT + m + 1))
                    if m >= 2:
                        pe.wait_ge(s["o_added"], i * 4 + (m - 1))
                    product(pe, ps[:, m, :], N_OUT + m, 0, P, KT, hx).then_inc(strip_used, 1)
                pe.wait_ge(s["o_added"], i * 4 + 3)

            after(pe, "out")
            norm_pe(pe, 2, ps[:, 7, :], sq, S)

            after(pe, "norm2")
            with pe.Fori(0, 11) as i:
                for m in range(4):
                    pe.wait_ge(low_made, i * 4 + (N_UP + m + 1))
                    if m >= 2:
                        pe.wait_ge(s["z_done"], i * 4 + (m - 1))
                    product(pe, ps[:, m, :], N_UP + m, 0, P, KT, hx).then_inc(strip_used, 1)
                pe.wait_ge(s["z_done"], i * 4 + 3)

            after(pe, "up")
            with pe.Fori(0, 2) as i:
                for m in range(4):
                    for part in range(3):
                        n = N_DOWN + 3 * m + part
                        pe.wait_ge(low_made, i * 12 + (n + 1))
                        if part == 0 and m >= 2:
                            pe.wait_ge(s["d_added"], i * 4 + (m - 1))
                        product(pe, ps[:, 4 + m, :], n, 0, P, 8 if part < 2 else 6,
                                lambda k: (m_high[:, 8 * part + k, :], m_low[:, 8 * part + k, :]),
                                part == 0, part == 2).then_inc(strip_used, 1)
                pe.wait_ge(s["d_added"], i * 4 + 3)

            after(pe, "down")
            norm_pe(pe, 3, ps[:, 0, :], sq2, S)

            after(pe, "norm3")
            with pe.Fori(0, 2) as i:
                for m in range(4):
                    pe.wait_ge(low_made, i * 4 + (N_GM + m + 1))
                    if m >= 2:
                        pe.wait_ge(s["gm_done"], i * 4 + (m - 1))
                    product(pe, ps[:, m, :], N_GM + m, 0, P, KT, hx).then_inc(strip_used, 1)
                pe.wait_ge(s["gm_done"], i * 4 + 3)

            after(pe, "gm")
            for m in range(5):
                n = N_LAT + m
                pe.wait_ge(low_made, n + 1)
                if m < 2:
                    mm = product(pe, ps[:, m, :], n, 0, P, KT, hx)
                else:
                    mm = product_wide(pe, 2 * m - 2, n, 0, P, KT, h_high, h_low)
                mm.then_inc(strip_used, 1)
            pe.wait_ge(s["pe_root_part"], 1)
            pe.wait_ge(s["pe_part"], 1)
            for h in range(2):
                mm = pe.matmul(ps[:, 6 + h, 0:HALF], blocks[:], sq2[:, 0, h * HALF:(h + 1) * HALF],
                               start=True, stop=True)
            mm.then_inc(s["pe_sum"], 1)
            pe.wait_ge(s["pe_root_part"], 3)
            for k in range(2):
                pe.wait_ge(s["lat_sq"], k + 1)
                pe.matmul(ps[:, 6, :], ones[:], sq2[:, k % 2, 0:S], start=k == 0, stop=k == 1)\
                    .then_inc(s["lat_sum"], 1)
            pe.wait_ge(s["lat_root"], 2)
            for k in range(2):
                pe.wait_ge(s["lat_sq"], k + 3)
                for h in range(2):
                    mm = pe.matmul(ps[:, 6 + h, 0:HALF], ones[:], sq2[:, k % 2, h * HALF:(h + 1) * HALF],
                                   start=k == 0, stop=k == 1)
                mm.then_inc(s["lat_sum"], 1)
            pe.wait_ge(s["pe_part"], 2)
            pe.wait_ge(s["lat_scaled"], 2)
            for h in range(2):
                mm = pe.matmul(ps[:, h, 0:HALF], rot[:], k_pe[:, h * HALF:(h + 1) * HALF], start=True, stop=True)
            mm.then_inc(s["pe_turned"], 1)

            after(pe, "lat")
            with pe.Fori(0, 4) as p:
                pe.wait_ge(low_made, p * 4 + (N_MLA + 1))
                for h in range(2):
                    mm = product_wide(pe, 2 * h, N_MLA, h * P, 2 * P, 2, kl_high, kl_low)
                mm.then_inc(strip_used, 1)
                pe.wait_ge(low_made, p * 4 + (N_MLA + 2))
                for h in range(2):
                    mm = product(pe, ps[:, 4 + h, :], N_MLA + 1, h * P, 2 * P, 2,
                                 lambda k: (ql_high[:, k, :], ql_low[:, k, :]))
                mm.then_inc(strip_used, 1)
                pe.wait_ge(low_made, p * 4 + (N_MLA + 3))
                product(pe, ps[:, 6, :], N_MLA + 2, 0, P, 2,
                        lambda k: (ql_high[:, k, :], ql_low[:, k, :])).then_inc(strip_used, 1)
                for m in range(5):
                    pe.wait_ge(s["p_sq"], p * 5 + (m + 1))
                    pe.wait_ge(s["p_kept"], p * 5 + (m + 1))
                    if m < 2:
                        for h in range(2):
                            mm = pe.matmul(ps[:, 2 * m + h, 0:HALF], ones[:],
                                           sq2[:, m % 2, h * HALF:(h + 1) * HALF], start=True, stop=True)
                    else:
                        mm = pe.matmul(ps[:, 2 + m, :], ones[:] if m < 4 else blocks[:], sq2[:, m % 2, 0:S],
                                       start=True, stop=True)
                    mm.then_inc(s["p_sum"], 1)
                pe.wait_ge(low_made, p * 4 + (N_MLA + 4))
                for h in range(2):
                    pe.wait_ge(s["p_ln"], p * 5 + (h + 1))
                    mm = product_wide(pe, 2 * h, N_MLA + 3, h * P, 2 * P, 2, kl_high, kl_low)
                mm.then_inc(strip_used, 1)
                pe.wait_ge(s["p_normed"], p * 5 + 5)
                pe.matmul(ps[:, 7, :], rot[:], q_pe[:], start=True, stop=True).then_inc(s["qr_turned"], 1)
                for h in range(2):
                    pe.wait_ge(s["mv_kept"], p * 2 + (h + 1))
                    if h:
                        pe.wait_ge(s["mv_ready"], p * 4 + 2)
                    for a in range(4):
                        pe.transpose(ps[:, 4, a * P:(a + 1) * P], mvf[:, h, a * P:(a + 1) * P], ident[:])
                    pe.transpose(ps[0:META, 5, 0:P], mvf[:, h, 4 * P:L], ident[:]).then_inc(s["mv_turned"], 1)

                def scores(u):
                    h, t = divmod(u, 4)
                    b = 2 * (u % 2)
                    if u == 0:
                        pe.wait_ge(s["qr_part"], p * 3 + 3)
                        pe.wait_ge(s["mv_kept"], p * 2 + 2)
                    if u >= 2:
                        pe.wait_ge(s["s_exp"], p * 8 + (u - 1))
                    for c in range(2):
                        pe.matmul(ps[:, b + c, 0:HALF], qn[:, h, t * P:(t + 1) * P],
                                  kn[:, h, c * HALF:(c + 1) * HALF], start=True, stop=False)
                        mm = pe.matmul(ps[:, b + c, 0:HALF], q_pe[h * 64:(h + 1) * 64, t * P:(t + 1) * P],
                                       k_pe[h * 64:(h + 1) * 64, c * HALF:(c + 1) * HALF], start=False, stop=True)
                    mm.then_inc(s["s_scored"], 1)

                def turn(u):
                    pe.wait_ge(s["s_probs"], p * 8 + (u + 1))
                    if u:
                        pe.wait_ge(s["s_copied_a"], p * 8 + u)
                        pe.wait_ge(s["s_copied_b"], p * 8 + u)
                    else:
                        pe.wait_ge(s["mv_ready"], p * 4 + 4)
                    for a in range(4):
                        pe.transpose(ps[:, 4, a * P:(a + 1) * P], me[:, u % 2, a * P:(a + 1) * P], ident[:])
                    pe.transpose(ps[0:META, 5, 0:P], me[:, u % 2, 4 * P:L], ident[:]).then_inc(s["s_turned"], 1)

                def weigh(u):
                    h, t = divmod(u, 4)
                    pe.wait_ge(s["s_copied_a"], p * 8 + (u + 1))
                    pe.wait_ge(s["s_copied_b"], p * 8 + (u + 1))
                    if u == 4:
                        pe.wait_ge(s["qr_part"], p * 3 + 1)
                    for a in range(5):
                        r = P if a < 4 else META
                        mm = pe.matmul(ps[:, 6 + h, t * P:(t + 1) * P], mv[0:r, a, h * P:(h + 1) * P],
                                       mp[0:r, a * P:(a + 1) * P], start=a == 0, stop=a == 4)
                    mm.then_inc(s["s_summed"], 1)

                scores(0)
                for u in range(9):
                    if u < 7:
                        scores(u + 1)
                    if u < 8:
                        turn(u)
                    if u >= 1:
                        weigh(u - 1)
                pe.wait_ge(s["s_y"], p * 2 + 2)

            after(pe, "mla")
            with pe.Fori(0, 2) as i:
                for m in range(4):
                    pe.wait_ge(low_made, i * 4 + (N_OM + m + 1))
                    if m >= 2:
                        pe.wait_ge(s["om_added"], i * 4 + (m - 1))
                    product(pe, ps[:, m, :], N_OM + m, 0, P, KT, yx).then_inc(strip_used, 1)
                pe.wait_ge(s["om_added"], i * 4 + 3)

            after(pe, "om")

            def scores(i, c, t, first=False):
                w, g, z_ = NA_W[t], NA_G[t], c % 2
                if t == 0:
                    pe.wait_ge(s["q_normed"], i * 4 + (2 * c + 2))
                if not first:
                    pe.wait_ge(s["t_masked"], i * 16 + (8 * c + 2 * t))
                for h in range(2):
                    q = nq[h * HD:(h + 1) * HD, z_, t * P:(t + 1) * P]
                    pe.matmul(ps[:, h, 0:META], q, nk[h * HD:(h + 1) * HD, z_, 0:META], start=True, stop=True)
                    mm = pe.matmul(ps[:, h, META:META + w], q,
                                   nk[h * HD:(h + 1) * HD, z_, META + g * P:META + g * P + w],
                                   start=True, stop=True)
                mm.then_inc(s["t_scored"], 1)

            def turn(i, c, t):
                pe.wait_ge(s["t_exp"], i * 16 + (8 * c + 2 * t + 2))
                for a in range(NA_W[t] // P):
                    for h in range(2):
                        o = (2 * a + h) % 4 * P
                        pe.transpose(ps[:, 2 + a // 2, o:o + P], ne[:, t % 2, h, META + a * P:META + (a + 1) * P],
                                     ident[:])
                for h in range(2):
                    mm = pe.transpose(ps[0:META, 3, (2 + h) * P:(3 + h) * P], ne[:, t % 2, h, 0:META], ident[:])
                mm.then_inc(s["t_turned"], 1)

            def weigh(i, c, t):
                n, z_ = NA_W[t] // P, c % 2
                pe.wait_ge(s["t_copied_a"], i * 8 + (4 * c + t + 1))
                pe.wait_ge(s["t_copied_b"], i * 8 + (4 * c + t + 1))
                if t:
                    pe.wait_ge(s["t_y"], i * 8 + (4 * c + t))
                else:
                    pe.wait_ge(s["nv_ready"], i * 4 + (2 * c + 2))
                for h in range(2):
                    d = slice(h * HD, (h + 1) * HD)
                    for a in range(n):
                        pe.matmul(ps[:, 4, d], npt[:, a, h * P:(h + 1) * P], nv[:, z_, NA_G[t] + a, d],
                                  start=a == 0, stop=False)
                    mm = pe.matmul(ps[:, 4, d], npt[0:META, 3, h * P:(h + 1) * P], nv[0:META, z_, 4, d],
                                   start=False, stop=True)
                mm.then_inc(s["t_summed"], 1)

            def back(i, c, t):
                pe.wait_ge(s["t_out"], i * 16 + (8 * c + 2 * t + 2))
                pe.transpose(ps[:, 4, 0:P], no[:, t % 2, :], ident[:]).then_inc(s["t_back"], 1)

            def project(i, c, m):
                n = N_NA + 4 * c + m
                pe.wait_ge(low_made, i * 8 + (n + 1))
                if m in (0, 2):
                    product_wide(pe, 5, n, 0, P, KT, h_high, h_low).then_inc(strip_used, 1)
                else:
                    product(pe, ps[:, 7, :], n, 0, P, KT, hx).then_inc(strip_used, 1)

            def sums(i, c, m):
                pe.wait_ge(s["q_sq"], i * 4 + (2 * c + m + 1))
                pe.wait_ge(s["q_kept"], i * 4 + (2 * c + m + 1))
                if m:
                    mm = pe.matmul(ps[:, 7, :], blocks[:], sq2[:, 1, 0:S], start=True, stop=True)
                else:
                    for h in range(2):
                        mm = pe.matmul(ps[:, 5 + h, 0:HALF], blocks[:], sq2[:, 0, h * HALF:(h + 1) * HALF],
                                       start=True, stop=True)
                mm.then_inc(s["q_sum"], 1)

            def turn_v(i, c):
                pe.wait_ge(s["nv_kept"], i * 2 + (c + 1))
                for a in range(4):
                    pe.transpose(ps[:, 5, a * P:(a + 1) * P], nvf[:, META + a * P:META + (a + 1) * P], ident[:])
                pe.transpose(ps[0:META, 6, 0:P], nvf[:, 0:META], ident[:]).then_inc(s["nv_turned"], 1)

            def pair(i, c):
                pe.wait_ge(s["nv_ready"], i * 4 + (2 * c + 2))
                project(i, c + 1, 0)
                turn(i, c, 0)
                scores(i, c, 1)
                weigh(i, c, 0)
                pe.wait_ge(s["g_done"], i * 2 + (c + 1))
                project(i, c + 1, 1)
                back(i, c, 0)
                sums(i, c + 1, 0)
                turn(i, c, 1)
                scores(i, c, 2)
                weigh(i, c, 1)
                pe.wait_ge(s["q_root"], i * 8 + (4 * c + 5))
                project(i, c + 1, 2)
                back(i, c, 1)
                sums(i, c + 1, 1)
                turn(i, c, 2)
                scores(i, c, 3)
                weigh(i, c, 2)
                pe.wait_ge(s["q_root"], i * 8 + (4 * c + 7))
                project(i, c + 1, 3)
                back(i, c, 2)
                turn(i, c, 3)
                scores(i, c + 1, 0)
                weigh(i, c, 3)
                turn_v(i, c + 1)
                back(i, c, 3)

            project(0, 0, 0)
            project(0, 0, 1)
            sums(0, 0, 0)
            pe.wait_ge(s["q_root"], 1)
            project(0, 0, 2)
            sums(0, 0, 1)
            pe.wait_ge(s["q_root"], 3)
            project(0, 0, 3)
            turn_v(0, 0)
            scores(0, 0, 0, first=True)
            with pe.Fori(0, 3) as i:
                pair(i, 0)
                pair(i, 1)
            pair(3, 0)
            for t in range(4):
                if t < EARLY:
                    pe.wait_ge(low_made, N_ON + t + 1)
                    if t == 0:
                        pe.wait_ge(s["nv_ready"], 16)
                        pe.wait_ge(s["g_done"], 8)
                        pe.wait_ge(s["t_low"], 28)
                    product(pe, ps[:, 5 + t, :], N_ON + t, 0, P, KT - 1, yx, last=False)
                if t:
                    back(3, 1, t - 1)
                turn(3, 1, t)
                if t < 3:
                    scores(3, 1, t + 1)
                weigh(3, 1, t)
            back(3, 1, 3)

            after(pe, "na")
            for m in range(8):
                pe.wait_ge(low_made, N_ON + m + 1)
                if m < EARLY:
                    product(pe, ps[:, 5 + m, :], N_ON + m, (KT - 1) * P, P, 1,
                            lambda k: yx(KT - 1), first=False).then_inc(strip_used, 1)
                else:
                    product(pe, ps[:, m - EARLY, :], N_ON + m, 0, P, KT, yx).then_inc(strip_used, 1)

            after(pe, "on")
            for t in range(4):
                for h in range(2):
                    for k in range(4):
                        mm = pe.transpose(ps[:, 2 * t + h, k * P:(k + 1) * P],
                                          x_t[:, 4 * h + k, t * P:(t + 1) * P], ident[:])
                    mm.then_inc(s["out_turned"], 1)

        @block.scalar
        def _(act):
            c = 0

            def const(dst, src):
                nonlocal c
                c += 1
                act.dma_start(dst, src).then_inc(s["consts_in"], 16)

            const(ident[:], c_ident)
            taps = conv_w[0].rearrange("t (c p) -> t c p", p=P)
            const(rows_a[0:44, :], taps[0])
            const(rows_a[44:88, :], taps[1])
            const(rows_b[0:44, :], taps[2])
            const(rows_b[44:88, :], conv_b[0].rearrange("(c p) -> c p", p=P))
            for r, k, v in ((V_MIX, 8, mix_norm), (V_FFN, 8, ffn_norm), (V_N2, 8, norm_w_2),
                            (V_QL, 2, q_lat_norm_w_2), (V_KL, 2, kv_lat_norm_w_2), (V_QN, 1, mla_qn_w_2),
                            (V_KN, 1, mla_kn_w_2), (V_SGU, 4, sgu_norm)):
                const(rows_v[r:r + k, :], v[0].rearrange("(c p) -> c p", p=P))
            for r, v in ((V_AQ, q_norm), (V_AK, k_norm), (V_NQ, na_q_norm_w_2), (V_NK, na_k_norm_w_2),
                         (V_QPE, mla_qpe_w_2), (V_KPE, mla_kpe_w_2)):
                for h in range(2):
                    const(rows_v[r:r + 1, h * 64:(h + 1) * 64], v)
            const(meta_tok[:], meta_tokens_2)
            const(blocks[:], c_blocks)
            const(rot[:], c_rot)
            const(dist[:], c_dist)
            const(slope[:], c_slope)
            const(sink[:], sinks[0].partition_broadcast(P))
            bs = b_s[0].rearrange("(q h) i -> h q i", h=2)
            for h in range(2):
                const(bias_s[h * 64:(h + 1) * 64, :, :], bs[h].partition_broadcast(64))
            assert c == N_CONST, c

            act.preload_act_table_set("natural_log_exp_and_others")
            act.wait_ge(s["meta_turned"], 1)
            act.activation(meta_t[:], ps[:, 2, 0:P].rearrange("p (k m) -> p k m", m=META), ACT.Copy)\
                .then_inc(s["meta_ready"], 1)
            for k in range(KT):
                act.wait_ge(s["x_turned"], k + 1)
                act.activation(x_t[:, k, :], ps[:, k % 2, :], ACT.Copy).then_inc(s["x_ready"], 1)
            act.wait_ge(s["meta_ready"], 1)
            act.wait_ge(s["ones_set"], 2)
            norm_act(act, 0, ps[:, 4, 0:META], lambda k: meta_t[:, k, :], sq, root, scaled, META,
                     lambda k: h_high[:, k, 0:META])
            act.wait_ge(s["norm_low"], 8)
            norm_act(act, 1, ps[:, 3, :], xs, sq, root, scaled, S, hh, "x_ready")

            after(act, "setup")
            for n in range(8):
                act.wait_ge(strip_used, N_SGU + n + 1)
                act.activation(uv[:, n, :], ps[:, n % 4, :], ACT.Gelu_apprx_tanh).then_inc(s["gelu_done"], 1)

            act.preload_act_table_set("natural_log_exp_and_others")
            for k in range(4):
                act.wait_ge(s["gelu_done"], 5 + k)
                if k >= 2:
                    act.wait_ge(s["sv_sum"], k - 1)
                act.activation(sq[:, k % 2, 0:S], uv[:, 4 + k, :], ACT.Square).then_inc(s["sv_sq"], 1)
            act.wait_ge(s["sv_sum"], 4)
            act.activation(root[:, 1, 0:S], ps[:, 2, :], ACT.Ln, bias=eps[:, 0:1], scale=1.0 / SGU)\
                .then_inc(s["sv_root"], 1)
            act.wait_ge(s["sv_root"], 1)
            act.activation(root[:, 1, 0:S], root[:, 1, 0:S], ACT.Exp, scale=-0.5).then_inc(s["sv_root"], 1)
            banks = [4, 6, 7, 4, 5]
            strips = [0, 2, 3, 4, 5]

            def i1_root(j):
                act.wait_ge(s["i1_sum"], j + 1)
                if j >= 2:
                    act.wait_ge(s["i1_normed"], j - 1)
                if j == 1:
                    act.wait_ge(s["sv_normed"], 4)
                act.activation(root[:, j % 2, 0:S], ps[:, j % 2, :], ACT.Ln, bias=eps[:, 0:1], scale=1.0 / HD)\
                    .then_inc(s["i1_ln"], 1)
                act.wait_ge(s["i1_ln"], j + 1)
                act.activation(root[:, j % 2, 0:S], root[:, j % 2, 0:S], ACT.Exp, scale=-0.5)\
                    .then_inc(s["i1_root"], 1)

            for j in range(5):
                act.wait_ge(strip_used, N_QKV + strips[j] + 1)
                if j >= 2:
                    act.wait_ge(s["i1_sum"], j - 1)
                act.activation(sq[:, j % 2, 0:S], ps[:, banks[j], :], ACT.Square).then_inc(s["i1_sq"], 1)
                if j == 0:
                    i1_root(0)
                    act.wait_ge(strip_used, N_QKV + 2)
                    act.activation(v_f[:], ps[:, 5, :], ACT.Copy).then_inc(s["v_copied"], 1)
                elif j >= 2:
                    if j == 2:
                        pass
                    i1_root(j - 1)
            i1_root(4)

            after(act, "qkv")
            act.wait_ge(s["ws_turned"], 1)
            act.activation(ws_t[:].rearrange("p (b g) i -> p b (g i)", b=2), ps[:, 6:8, :], ACT.Copy)\
                .then_inc(s["ws_ready"], 1)
            for q in range(4):
                act.wait_ge(s["mix_gated"], 2 * (q + 1))
                act.activation(a_high[:, 4 + q, :], uv[:, q, :], ACT.Copy).then_inc(s["mix_high"], 1)

            after(act, "mix")
            with act.Fori(0, 4) as j:
                act.activation(q_st[:], q_t[:, bass.ds(j, 1), :], ACT.Copy).then_inc(s["j_staged"], 1)
                for t in range(4):
                    w = 2 * P if t else P
                    for h in range(2):
                        act.wait_ge(s["a_part"], j * 20 + (5 * t + 2))
                        act.activation(att_e[:, h, 0:w], att_e[:, h, 0:w], ACT.Exp, bias=att_m[:, 1, h:h + 1],
                                       accum_out=att_m[:, 2, h:h + 1]).then_inc(s["a_exp"], 1)
                    act.wait_ge(s["a_part"], j * 20 + (5 * t + 3))
                    act.activation(att_m[:, 4, :], att_m[:, 3, :], ACT.Exp).then_inc(s["a_sink_exp"], 1)
                    act.wait_ge(s["a_turned"], j * 4 + (t + 1))
                    if t:
                        act.wait_ge(s["a_summed"], j * 4 + t)
                    act.activation(att_p[:, 0:w // 64, :], ps[:, 2, 0:2 * w].rearrange("p (a q) -> p a q", q=P),
                                   ACT.Copy).then_inc(s["a_copied"], 1)
                    act.wait_ge(s["a_summed"], j * 4 + (t + 1))
                    for h in range(2):
                        r = slice(h * HD, (h + 1) * HD)
                        act.activation(att_y[r, t * P:(t + 1) * P], ps[r, 3, h * P:(h + 1) * P], ACT.Copy)\
                            .then_inc(s["a_y"], 1)
                act.wait_ge(s["a_y"], j * 8 + 8)
                act.activation(a_high[:, bass.ds(j, 1), :], att_y[:], ACT.Copy).then_inc(s["a_high"], 1)
                act.wait_ge(s["a_low"], j + 1)

            after(act, "att")
            with act.Fori(0, 2) as i:
                for u in range(2):
                    for m in range(2):
                        for b in range(2):
                            g = gates[:, bass.ds(i * 4 + (8 * b + 2 * u + m), 1), :]
                            act.activation(g, g, ACT.Sigmoid).then_inc(s["g_sig"], 1)
                for m in range(4):
                    act.wait_ge(s["m_whole"], i * 4 + (m + 1))
                    act.activation(h_high[:, bass.ds(i * 4 + m, 1), META:L], merge[:, m % 2, :], ACT.Copy)\
                        .then_inc(s["m_high_"], 1)

            act.preload_act_table_set("natural_log_exp_and_others")
            after(act, "out")
            norm_act(act, 2, ps[:, 7, :], xs, sq, root, scaled, S, hh)

            after(act, "norm2")
            with act.Fori(0, 11) as i:
                for m in range(4):
                    ct = m % 2 + FT * (m // 2)
                    act.wait_ge(strip_used, i * 4 + (N_UP + m + 1))
                    act.activation(z[:, m, :], ps[:, m, :], ACT.Identity,
                                   scale=cv[:, bass.ds(i * 2 + (C_CONV + 2 * 2 * FT + ct), 1)],
                                   bias=cv[:, bass.ds(i * 2 + (C_CONVB + ct), 1)]).then_inc(s["z_first"], 1)
                    if m >= 2:
                        act.wait_ge(s["z_done"], i * 4 + (m - 1))
                        act.activation(z[:, m - 2, :], z[:, m - 2, :], ACT.Silu).then_inc(s["z_silu"], 1)
                for m in range(2):
                    act.wait_ge(s["z_gated"], i * 2 + (m + 1))
                    act.activation(m_high[:, bass.ds(i * 2 + m, 1), :], zg[:, m, :], ACT.Copy)\
                        .then_inc(s["z_high"], 1)

            with act.Fori(0, 2) as i:
                for m in range(4):
                    act.wait_ge(s["d_added"], i * 4 + (m + 1))
                    act.activation(x_t[:, bass.ds(i * 4 + m, 1), :].rearrange("p o (g r c) -> p (o r) g c", g=CG, c=16),
                                   z[:, m, :].rearrange("p (r g c) -> p r g c", g=CG, c=16), ACT.Copy)\
                        .then_inc(s["d_placed"], 1)

            act.preload_act_table_set("natural_log_exp_and_others")
            after(act, "down")
            norm_act(act, 3, ps[:, 0, :], xs, sq2, root2, scaled2, S, hh)

            after(act, "norm3")
            with act.Fori(0, 2) as i:
                for m in range(4):
                    act.wait_ge(strip_used, i * 4 + (N_GM + m + 1))
                    act.activation(gm[:, bass.ds(i * 4 + m, 1), :], ps[:, m, :], ACT.Silu).then_inc(s["gm_done"], 1)

            act.preload_act_table_set("natural_log_exp_and_others")
            after(act, "gm")
            act.wait_ge(strip_used, N_LAT + 5)
            act.activation(halves(sq2[:, 0, :]), wide(6), ACT.Square).then_inc(s["pe_root_part"], 1)
            act.wait_ge(s["pe_sum"], 1)
            act.activation(halves(root2[:, 0, :]), wide(6), ACT.Ln, bias=eps[:, 0:1], scale=1.0 / 64)\
                .then_inc(s["pe_root_part"], 1)
            act.wait_ge(s["pe_root_part"], 2)
            act.activation(root2[:, 0, :], root2[:, 0, :], ACT.Exp, scale=-0.5).then_inc(s["pe_root_part"], 1)
            for m in range(2):
                src, n = ((lambda k: ps[:, k, :]), S) if m == 0 else ((lambda k: wide(2 + 2 * k)), L)
                for k in range(2):
                    act.wait_ge(s["lat_sum"], 2 * m + k - 1) if m else None
                    dst = sq2[:, k, 0:n] if m == 0 else halves(sq2[:, k, :])
                    act.activation(dst, src(k), ACT.Square).then_inc(s["lat_sq"], 1)
                act.wait_ge(s["lat_sum"], 2 * m + 2)
                if m == 0:
                    act.wait_ge(s["pe_part"], 2)
                else:
                    act.wait_ge(s["lat_scaled"], 2)
                dst, acc = (root2[:, 0, 0:n], ps[:, 6, :]) if m == 0 else (halves(root2[:, 0, :]), wide(6))
                act.activation(dst, acc, ACT.Ln, bias=eps[:, 0:1], scale=1.0 / 256).then_inc(s["lat_root"], 1)
                act.wait_ge(s["lat_root"], m * 2 + 1)
                act.activation(root2[:, 0, 0:n], root2[:, 0, 0:n], ACT.Exp, scale=-0.5).then_inc(s["lat_root"], 1)
                for k in range(2):
                    act.wait_ge(s["lat_scaled"], 2 * m + k + 1)
                    act.activation((ql_high if m == 0 else kl_high)[:, k, :], scaled2[:, k, 0:n], ACT.Copy)\
                        .then_inc(s["lat_high"], 1)

            after(act, "lat")
            with act.Fori(0, 4) as p:
                used = [1, 1, 2, 2, 3]
                for m in range(5):
                    act.wait_ge(strip_used, p * 4 + (N_MLA + used[m]))
                    if m >= 2:
                        act.wait_ge(s["p_sum"], p * 5 + (m - 1))
                    src = wide(2 * m) if m < 2 else ps[:, 2 + m, :]
                    dst = halves(sq2[:, m % 2, :]) if m < 2 else sq2[:, m % 2, 0:S]
                    act.activation(dst, src, ACT.Square).then_inc(s["p_sq"], 1)
                for m in range(5):
                    act.wait_ge(s["p_sum"], p * 5 + (m + 1))
                    if m >= 2:
                        act.wait_ge(s["p_normed"], p * 5 + (m - 1))
                    src = wide(2 * m) if m < 2 else ps[:, 2 + m, :]
                    dst = halves(root2[:, m % 2, :]) if m < 2 else root2[:, m % 2, 0:S]
                    n = L if m < 2 else S
                    act.activation(dst, src, ACT.Ln, bias=eps[:, 0:1], scale=1.0 / (P if m < 4 else 64))\
                        .then_inc(s["p_ln"], 1)
                    act.wait_ge(s["p_ln"], p * 5 + (m + 1))
                    act.activation(root2[:, m % 2, 0:n], root2[:, m % 2, 0:n], ACT.Exp, scale=-0.5)\
                        .then_inc(s["p_root"], 1)
                for h in range(2):
                    act.wait_ge(strip_used, p * 4 + (N_MLA + 4))
                    act.wait_ge(s["p_sum"], p * 5 + 5)
                    act.activation(halves(mvf[:, h, :]), wide(2 * h), ACT.Copy).then_inc(s["mv_kept"], 1)
                for h in range(2):
                    act.wait_ge(s["mv_turned"], p * 2 + (h + 1))
                    act.activation(mv[:, 0:4, h * P:(h + 1) * P], ps[:, 4, :].rearrange("p (a d) -> p a d", d=P),
                                   ACT.Copy).then_inc(s["mv_ready"], 1)
                    act.activation(mv[0:META, 4, h * P:(h + 1) * P], ps[0:META, 5, 0:P], ACT.Copy)\
                        .then_inc(s["mv_ready"], 1)
                for u in range(9):
                    if u < 8:
                        act.wait_ge(s["s_neg"], p * 8 + (u + 1))
                        if u >= 2:
                            act.wait_ge(s["s_turned"], p * 8 + (u - 1))
                        act.activation(halves(me[:, u % 2, :]), wide(2 * (u % 2)), ACT.Exp, scale=MLA_SCALE,
                                       bias=mm_[:, u % 2, 1:2], accum_out=mm_[:, u % 2, 2:3]).then_inc(s["s_exp"], 1)
                    if u >= 1:
                        act.wait_ge(s["s_turned"], p * 8 + u)
                        if u >= 2:
                            act.wait_ge(s["s_summed"], p * 8 + (u - 1))
                        act.activation(mp[:, 0:4 * P], ps[:, 4, :], ACT.Copy).then_inc(s["s_copied_a"], 1)
                for h in range(2):
                    act.wait_ge(s["s_y"], p * 2 + (h + 1))
                    act.activation(y_high[:, bass.ds(p * 2 + h, 1), :], (y_f[:], scaled2[:, 0, 0:S])[h], ACT.Copy)\
                        .then_inc(s["s_high"], 1)

            after(act, "mla")

            def expo(i, c, t):
                w = META + NA_W[t]
                act.wait_ge(s["t_neg"], i * 8 + (4 * c + t + 1))
                for h in range(2):
                    act.activation(ne[:, t % 2, h, 0:w], ne[:, t % 2, h, 0:w], ACT.Exp, bias=nm[:, t % 2, 0, h:h + 1],
                                   accum_out=nm[:, t % 2, 1, h:h + 1]).then_inc(s["t_exp"], 1)

            def copy_a(i, c, t):
                act.wait_ge(s["t_turned"], i * 8 + (4 * c + t + 1))
                act.activation(npt[:, 0:2, :], ps[:, 2, :].rearrange("p (a q) -> p a q", a=2), ACT.Copy)\
                    .then_inc(s["t_copied_a"], 1)

            def square(i, c, m):
                act.wait_ge(strip_used, i * 8 + (N_NA + 4 * c + m + 1))
                src = wide(5) if m == 0 else ps[:, 7, :]
                dst = halves(sq2[:, 0, :]) if m == 0 else sq2[:, 1, 0:S]
                act.activation(dst, src, ACT.Square).then_inc(s["q_sq"], 1)

            def root_ln(i, c, m):
                act.wait_ge(s["q_sum"], i * 4 + (2 * c + m + 1))
                if c:
                    act.wait_ge(s["q_normed"], i * 4 + (2 * c + m - 1))
                src = wide(5) if m == 0 else ps[:, 7, :]
                dst = halves(root2[:, 0, :]) if m == 0 else root2[:, 1, 0:S]
                act.activation(dst, src, ACT.Ln, bias=eps[:, 0:1], scale=1.0 / HD).then_inc(s["q_root"], 1)

            def root_exp(i, c, m):
                n = L if m == 0 else S
                act.wait_ge(s["q_root"], i * 8 + (4 * c + 2 * m + 1))
                act.activation(root2[:, m, 0:n], root2[:, m, 0:n], ACT.Exp, scale=-0.5).then_inc(s["q_root"], 1)

            def keep_v(i, c):
                act.wait_ge(strip_used, i * 8 + (N_NA + 4 * c + 3))
                if c:
                    act.wait_ge(s["nv_turned"], i * 2 + c)
                act.activation(halves(nvf[:]), wide(5), ACT.Copy).then_inc(s["nv_kept"], 1)

            def gate(i, c):
                act.wait_ge(strip_used, i * 8 + (N_NA + 4 * c + 4))
                if c:
                    act.wait_ge(s["g_done"], i * 2 + c)
                act.activation(sig[:], ps[:, 7, :], ACT.Exp, scale=-1.0).then_inc(s["g_part"], 1)
                act.wait_ge(s["g_part"], i * 6 + (3 * c + 1))
                act.activation(sig[:], sig[:], ACT.Ln, bias=1.0).then_inc(s["g_part"], 1)
                act.wait_ge(s["g_part"], i * 6 + (3 * c + 2))
                act.activation(sig[:], sig[:], ACT.Exp, scale=-1.0).then_inc(s["g_part"], 1)

            def place_v(i, c):
                act.wait_ge(s["nv_turned"], i * 2 + (c + 1))
                act.activation(nv[:, c % 2, 0:4, :], ps[:, 5, :].rearrange("p (a d) -> p a d", d=P), ACT.Copy)\
                    .then_inc(s["nv_ready"], 1)
                act.activation(nv[0:META, c % 2, 4, :], ps[0:META, 6, 0:P], ACT.Copy).then_inc(s["nv_ready"], 1)

            def pair(i, c):
                expo(i, c, 0)
                copy_a(i, c, 0)
                square(i, c + 1, 0)
                expo(i, c, 1)
                copy_a(i, c, 1)
                root_ln(i, c + 1, 0)
                square(i, c + 1, 1)
                root_exp(i, c + 1, 0)
                expo(i, c, 2)
                copy_a(i, c, 2)
                root_ln(i, c + 1, 1)
                root_exp(i, c + 1, 1)
                keep_v(i, c + 1)
                expo(i, c, 3)
                copy_a(i, c, 3)
                gate(i, c + 1)
                place_v(i, c + 1)

            square(0, 0, 0)
            square(0, 0, 1)
            root_ln(0, 0, 0)
            root_exp(0, 0, 0)
            root_ln(0, 0, 1)
            root_exp(0, 0, 1)
            keep_v(0, 0)
            gate(0, 0)
            place_v(0, 0)
            with act.Fori(0, 3) as i:
                pair(i, 0)
                pair(i, 1)
            pair(3, 0)
            for t in range(4):
                expo(3, 1, t)
                copy_a(3, 1, t)

            after(act, "on")
            for t in range(4):
                act.wait_ge(s["out_turned"], 2 * t + 1)
                act.activation(y_tok[:, t, 0:512], ps[:, 2 * t, :], ACT.Copy).then_inc(s["out_left"], 1)

        @block.vector
        def _(dve):
            dve.wait_ge(s["rows_turned"], 1)
            dve.tensor_copy(cv[:], ps[:, 7, 0:C_V + V_ROWS]).then_inc(s["cols_ready"], 1)
            dve.wait_ge(s["cols_ready"], 1)
            dve.tensor_scalar(aq_gain[:], col(V_AQ), HD ** -0.5, None, ALU.mult).then_inc(s["gain_ready"], 1)
            dve.tensor_scalar(nq_gain[:], col(V_NQ), HD ** -0.5, None, ALU.mult).then_inc(s["gain_ready"], 1)
            make_high(dve, 0)
            norm_dve(dve, 0, lambda k: meta_t[:, k, :], V_N2, root, scaled, META,
                     lambda k: h_high[:, k, 0:META], lambda k: h_low[:, k, 0:META])
            make_high(dve, 1)
            make_high(dve, 2)
            dve.wait_ge(s["norm_low"], 8)
            norm_dve(dve, 1, xs, V_MIX, root, scaled, S, hh, hl)

            for n in range(N_SGU, N_QKV):
                make_high(dve, n + 3)

            dve.wait_ge(s["gain_ready"], 2)

            def i1_norm(j):
                dve.wait_ge(s["i1_root"], j + 1)
                dst = k_t[:] if j == 0 else q_t[:, j - 1, :]
                gain = col(V_AK) if j == 0 else aq_gain[:, 0:1]
                dve.scalar_tensor_tensor(dst, ps[:, [4, 6, 7, 4, 5][j], :], gain, root[:, j % 2, 0:S],
                                         ALU.mult, ALU.mult).then_inc(s["i1_normed"], 1)

            make_high(dve, N_QKV + 3)
            dve.wait_ge(s["sv_root"], 2)
            for k in range(4):
                dve.scalar_tensor_tensor(uv[:, 4 + k, :], uv[:, 4 + k, :], col(V_SGU + k), root[:, 1, 0:S],
                                         ALU.mult, ALU.mult).then_inc(s["sv_normed"], 1)
            i1_norm(0)
            make_high(dve, N_QKV + 4)
            make_high(dve, N_QKV + 5)
            dve.wait_ge(s["v_turned"], 1)
            dve.tensor_copy(v_tok[:], ps[:, 3, :].rearrange("p (a d) -> p a d", d=P)).then_inc(s["v_ready"], 1)
            for m in range(3, 6):
                i1_norm(m - 2)
                make_high(dve, N_QKV + m + 3)
            i1_norm(4)

            after(dve, "qkv")
            for c in range(4):
                dve.wait_ge(s["sv_turned"], c + 1)
                dve.tensor_copy(uv_tok[:, c, :], ps[:, c % 2, :]).then_inc(s["sv_tok_ready"], 1)
            for q in range(4):
                dve.wait_ge(s["mixed"], q + 1)
                b = 2 + 2 * (q % 2)
                for h in range(2):
                    r = slice(h * 64, (h + 1) * 64)
                    src = ps[r, b:b + 2, :].rearrange("p b (c g i) -> p b c g i", c=2, g=2)[:, :, :, h, :]
                    for c in range(2):
                        ins = dve.tensor_tensor(scaled[r, 0, 256 * c:256 * c + 256].rearrange("p (c i) -> p c i", c=2),
                                                src[:, c], bias_s[r, q:q + 1, :].broadcast_to([64, 2, P]), ALU.add)
                    ins.then_inc(s["mix_biased"], 1)
                    dve.wait_ge(s["mix_biased"], 2 * q + h + 1)
                    dve.tensor_tensor(uv[r, q, :], uv[r, q, :], scaled[r, 0, :], ALU.mult)\
                        .then_inc(s["mix_gated"], 1)
                dve.wait_ge(s["mix_high"], q + 1)
                dve.tensor_tensor(a_low[:, 4 + q, :], uv[:, q, :], a_high[:, 4 + q, :].bitcast(F32),
                                  ALU.subtract).then_inc(s["mix_low"], 1)

            after(dve, "mix")
            with dve.Fori(0, 4) as j:
                for h in range(2):
                    dve.tensor_scalar(bias_h[:, h, :], dist[:], slope[:, bass.ds(j + 4 * h, 1)], None, ALU.mult)\
                        .then_inc(s["j_bias"], 1)
                sinks_j = sink[:].rearrange("p (h j) -> p h j", h=2)[:, :, bass.ds(j, 1)]
                for t in range(4):
                    w = 2 * P if t else P
                    dve.wait_ge(s["j_bias"], j * 2 + 2)
                    dve.wait_ge(s["a_scored"], j * 4 + (t + 1))
                    if t:
                        dve.wait_ge(s["a_turned"], j * 4 + t)
                    make_high(dve, N_GATE + t + 3, j * 4)
                    for h in range(2):
                        dve.tensor_tensor_reduce(att_e[:, h, 0:w], ps[:, h, 0:w], bias_h[:, h, 2 * P - w:2 * P],
                                                 1.0, -3e38, ALU.add, ALU.max, att_m[:, 0, h:h + 1])\
                            .then_inc(s["a_masked"], 1)
                    dve.wait_ge(s["a_masked"], j * 8 + (2 * t + 2))
                    dve.tensor_tensor(att_m[:, 5, :], att_m[:, 0, :], sinks_j, ALU.max).then_inc(s["a_part"], 1)
                    dve.wait_ge(s["a_part"], j * 20 + (5 * t + 1))
                    dve.tensor_scalar(att_m[:, 1, :], att_m[:, 5, :], -1.0, None, ALU.mult).then_inc(s["a_part"], 1)
                    dve.tensor_tensor(att_m[:, 3, :], sinks_j, att_m[:, 5, :], ALU.subtract).then_inc(s["a_part"], 1)
                    dve.wait_ge(s["a_exp"], j * 8 + (2 * t + 2))
                    dve.wait_ge(s["a_sink_exp"], j * 4 + (t + 1))
                    dve.tensor_tensor(att_m[:, 3, :], att_m[:, 2, :], att_m[:, 4, :], ALU.add)\
                        .then_inc(s["a_part"], 1)
                    dve.wait_ge(s["a_part"], j * 20 + (5 * t + 4))
                    dve.reciprocal(att_m[:, 5, :], att_m[:, 3, :]).then_inc(s["a_part"], 1)
                    dve.wait_ge(s["a_part"], j * 20 + (5 * t + 5))
                    for h in range(2):
                        dve.tensor_scalar(att_e[:, h, 0:w], att_e[:, h, 0:w], att_m[:, 5, h:h + 1], None, ALU.mult)\
                            .then_inc(s["a_probs"], 1)
                    dve.wait_ge(strip_used, j * 4 + (N_GATE + t + 1))
                    dve.tensor_copy(gates[:, bass.ds(j * 4 + t, 1), :], ps[:, 4 + t, :]).then_inc(s["gate_kept"], 1)
                dve.wait_ge(s["a_high"], j + 1)
                dve.tensor_tensor(a_low[:, bass.ds(j, 1), :], att_y[:], a_high[:, bass.ds(j, 1), :].bitcast(F32),
                                  ALU.subtract).then_inc(s["a_low"], 1)

            after(dve, "att")
            with dve.Fori(0, 2) as i:
                for u in range(2):
                    for m in range(2):
                        o = 2 * u + m
                        dve.wait_ge(strip_used, i * 4 + (N_MERGE + 2 * u + 2))
                        for b in range(2):
                            dve.wait_ge(s["g_sig"], i * 8 + (4 * u + 2 * m + b + 1))
                            g = gates[:, bass.ds(i * 4 + (8 * b + o), 1), :]
                            dve.tensor_tensor(g, g, ps[:, 4 * b + o, :], ALU.mult).then_inc(s["m_part"], 1)
                        dve.wait_ge(s["m_part"], i * 8 + (4 * u + 2 * m + 2))
                        if o >= 2:
                            dve.wait_ge(s["m_low_"], i * 4 + (o - 1))
                        dve.tensor_tensor(merge[:, m, :], gates[:, bass.ds(i * 4 + o, 1), :],
                                          gates[:, bass.ds(i * 4 + (8 + o), 1), :], ALU.add)\
                            .then_inc(s["m_whole"], 1)
                        dve.wait_ge(s["m_high_"], i * 4 + (o + 1))
                        dve.tensor_tensor(h_low[:, bass.ds(i * 4 + o, 1), META:L], merge[:, m, :],
                                          h_high[:, bass.ds(i * 4 + o, 1), META:L].bitcast(F32), ALU.subtract)\
                            .then_inc(s["m_low_"], 1)
                        if m == 1:
                            make_high(dve, N_MERGE + 2 * u + 3, i * 4)
                            make_high(dve, N_MERGE + 2 * u + 4, i * 4)

            def add_out(n0, banks, done, i, lag):
                for m in range(4):
                    dve.wait_ge(strip_used, i * 4 + (n0 + m + 1))
                    xm = x_t[:, bass.ds(i * 4 + m, 1), :]
                    dve.tensor_tensor(xm, xm, ps[:, banks[m], :], ALU.add).then_inc(s[done], 1)
                    make_high(dve, n0 + m + lag, i * 4)

            with dve.Fori(0, 2) as i:
                add_out(N_OUT, [0, 1, 2, 3], "o_added", i, 3)

            after(dve, "out")
            norm_dve(dve, 2, xs, V_FFN, root, scaled, S, hh, hl)

            after(dve, "norm2")
            with dve.Fori(0, 11) as i:
                for m in range(4):
                    ct = m % 2 + FT * (m // 2)
                    dve.wait_ge(s["z_first"], i * 4 + (m + 1))
                    dve.scalar_tensor_tensor(z[:, m, 1:S], ps[:, m, 0:S - 1],
                                             cv[:, bass.ds(i * 2 + (C_CONV + 2 * FT + ct), 1)], z[:, m, 1:S],
                                             ALU.mult, ALU.add).then_inc(s["z_mid"], 1)
                    dve.wait_ge(s["z_mid"], i * 4 + (m + 1))
                    dve.scalar_tensor_tensor(z[:, m, 2:S], ps[:, m, 0:S - 2],
                                             cv[:, bass.ds(i * 2 + (C_CONV + ct), 1)], z[:, m, 2:S],
                                             ALU.mult, ALU.add).then_inc(s["z_done"], 1)
                    make_high(dve, N_UP + m + 3, i * 4)
                    if m >= 2:
                        g = m - 2
                        dve.wait_ge(s["z_done"], i * 4 + (m + 1))
                        dve.wait_ge(s["z_silu"], i * 2 + (g + 1))
                        dve.tensor_tensor(zg[:, g, :], z[:, g, :], z[:, m, :], ALU.mult).then_inc(s["z_gated"], 1)
                for g in range(2):
                    dve.wait_ge(s["z_high"], i * 2 + (g + 1))
                    dve.tensor_tensor(m_low[:, bass.ds(i * 2 + g, 1), :], zg[:, g, :],
                                      m_high[:, bass.ds(i * 2 + g, 1), :].bitcast(F32), ALU.subtract)\
                        .then_inc(s["z_low"], 1)

            after(dve, "up")
            with dve.Fori(0, 2) as i:
                for m in range(4):
                    for part in range(3):
                        make_high(dve, N_DOWN + 3 * m + part + 3, i * 12)
                    dve.wait_ge(strip_used, i * 12 + (N_DOWN + 3 * m + 3))
                    dve.tensor_tensor(z[:, m, :], x_t[:, bass.ds(i * 4 + m, 1), :], ps[:, 4 + m, :], ALU.add)\
                        .then_inc(s["d_added"], 1)
                dve.wait_ge(s["d_placed"], i * 4 + 4)

            after(dve, "down")
            norm_dve(dve, 3, xs, V_N2, root2, scaled2, S, hh, hl)
            with dve.Fori(0, 2) as i:
                for m in range(4):
                    make_high(dve, N_GM + m + 3, i * 4)

            after(dve, "gm")
            for m in range(5):
                make_high(dve, N_LAT + m + 3)
            dve.wait_ge(s["pe_root_part"], 1)
            dve.tensor_copy(halves(k_pe[:]), wide(6)).then_inc(s["pe_part"], 1)
            dve.wait_ge(s["pe_part"], 1)
            dve.wait_ge(s["pe_root_part"], 3)
            dve.scalar_tensor_tensor(k_pe[:], k_pe[:], col(V_KPE), root2[:, 0, :],
                                     ALU.mult, ALU.mult).then_inc(s["pe_part"], 1)
            for m in range(2):
                dve.wait_ge(s["lat_root"], m * 2 + 2)
                n = S if m == 0 else L
                for k in range(2):
                    if m:
                        dve.wait_ge(s["lat_low"], 2)
                    else:
                        dve.wait_ge(s["pe_part"], 2)
                    src = ps[:, k, :] if m == 0 else wide(2 + 2 * k)
                    dst = scaled2[:, k, 0:n] if m == 0 else halves(scaled2[:, k, :])
                    r = root2[:, 0, 0:n] if m == 0 else halves(root2[:, 0, :])
                    dve.scalar_tensor_tensor(dst, src, col((V_QL, V_KL)[m] + k), r, ALU.mult, ALU.mult)\
                        .then_inc(s["lat_scaled"], 1)
                for k in range(2):
                    dve.wait_ge(s["lat_high"], 2 * m + k + 1)
                    hi, lo = (ql_high, ql_low) if m == 0 else (kl_high, kl_low)
                    dve.tensor_tensor(lo[:, k, :], scaled2[:, k, 0:n], hi[:, k, :].bitcast(F32), ALU.subtract)\
                        .then_inc(s["lat_low"], 1)
            dve.wait_ge(s["tables_in"], 32)
            dve.wait_ge(s["pe_turned"], 1)
            dve.wait_ge(s["lat_low"], 4)
            dve.tensor_tensor(k_pe[:], k_pe[:], cos[:], ALU.mult).then_inc(s["pe_part"], 1)
            dve.tensor_tensor(halves(scaled2[:, 0, :]), wide(0), halves(sin[:]), ALU.mult).then_inc(s["pe_part"], 1)
            dve.wait_ge(s["pe_part"], 3)
            dve.wait_ge(s["pe_part"], 4)
            dve.tensor_tensor(k_pe[:], k_pe[:], scaled2[:, 0, :], ALU.add).then_inc(s["pe_part"], 1)

            after(dve, "lat")
            with dve.Fori(0, 4) as p:
                used = [1, 1, 2, 2, 3]
                out_of = [kn[:, 0, :], kn[:, 1, :], qn[:, 0, :], qn[:, 1, :], q_pe[:]]
                gain = [V_KN, V_KN, V_QN, V_QN, V_QPE]
                for m in range(5):
                    dve.wait_ge(s["p_sq"], p * 5 + (m + 1))
                    if m < 2:
                        dve.tensor_copy(halves(out_of[m]), wide(2 * m)).then_inc(s["p_kept"], 1)
                    else:
                        dve.tensor_copy(out_of[m], ps[:, 2 + m, :]).then_inc(s["p_kept"], 1)
                    if m in (1, 3, 4):
                        make_high(dve, N_MLA + used[m] - 1 + 3, p * 4)
                for m in range(5):
                    n = L if m < 2 else S
                    dve.wait_ge(s["p_root"], p * 5 + (m + 1))
                    dve.scalar_tensor_tensor(out_of[m], out_of[m], col(gain[m]), root2[:, m % 2, 0:n],
                                             ALU.mult, ALU.mult).then_inc(s["p_normed"], 1)
                make_high(dve, N_MLA + 6, p * 4)
                dve.wait_ge(s["qr_turned"], p + 1)
                dve.tensor_tensor(scaled2[:, 1, 0:S], ps[:, 7, :], sin[:, META:L], ALU.mult).then_inc(s["qr_part"], 1)
                dve.tensor_tensor(q_pe[:], q_pe[:], cos[:, META:L], ALU.mult).then_inc(s["qr_part"], 1)
                dve.wait_ge(s["qr_part"], p * 3 + 2)
                dve.wait_ge(s["qr_part"], p * 3 + 1)
                dve.tensor_tensor(q_pe[:], q_pe[:], scaled2[:, 1, 0:S], ALU.add).then_inc(s["qr_part"], 1)

                def top(u):
                    dve.wait_ge(s["s_scored"], p * 8 + (u + 1))
                    if u >= 2:
                        dve.wait_ge(s["s_probs"], p * 8 + (u - 1))
                    dve.tensor_reduce(mm_[:, u % 2, 0:1], wide(2 * (u % 2)), AX.XY, ALU.max).then_inc(s["s_top"], 1)
                    dve.wait_ge(s["s_top"], p * 8 + (u + 1))
                    dve.tensor_scalar(mm_[:, u % 2, 1:2], mm_[:, u % 2, 0:1], -MLA_SCALE, None, ALU.mult)\
                        .then_inc(s["s_neg"], 1)

                top(0)
                for u in range(9):
                    if u < 7:
                        top(u + 1)
                    if u >= 1:
                        dve.wait_ge(s["s_turned"], p * 8 + u)
                        if u >= 2:
                            dve.wait_ge(s["s_summed"], p * 8 + (u - 1))
                        dve.tensor_copy(mp[0:META, 4 * P:5 * P], ps[0:META, 5, 0:P]).then_inc(s["s_copied_b"], 1)
                    if u < 8:
                        dve.wait_ge(s["s_exp"], p * 8 + (u + 1))
                        dve.reciprocal(mm_[:, u % 2, 3:4], mm_[:, u % 2, 2:3]).then_inc(s["s_inv"], 1)
                        dve.wait_ge(s["s_inv"], p * 8 + (u + 1))
                        dve.tensor_scalar(me[:, u % 2, :], me[:, u % 2, :], mm_[:, u % 2, 3:4], None, ALU.mult)\
                            .then_inc(s["s_probs"], 1)
                for h in range(2):
                    y = (y_f[:], scaled2[:, 0, 0:S])[h]
                    dve.wait_ge(s["s_summed"], p * 8 + 4 * (h + 1))
                    dve.tensor_tensor(y, ps[:, 6 + h, :], gm[:, bass.ds(p * 2 + h, 1), :], ALU.mult)\
                        .then_inc(s["s_y"], 1)
                for h in range(2):
                    y = (y_f[:], scaled2[:, 0, 0:S])[h]
                    dve.wait_ge(s["s_high"], p * 2 + (h + 1))
                    dve.tensor_tensor(y_low[:, bass.ds(p * 2 + h, 1), :], y,
                                      y_high[:, bass.ds(p * 2 + h, 1), :].bitcast(F32), ALU.subtract)\
                        .then_inc(s["s_low"], 1)

            with dve.Fori(0, 2) as i:
                add_out(N_OM, [0, 1, 2, 3], "om_added", i, 3)

            after(dve, "om")

            def masked(i, c, t, n):
                w, z_ = META + NA_W[t], c % 2
                if t == 0:
                    dve.wait_ge(s["nb_ready"], i * 18 + (9 * c + 9))
                if n:
                    dve.wait_ge(s["t_scored"], i * 8 + (4 * c + t + 1))
                    make_high(dve, n, i * 8)
                for h in range(2):
                    dve.tensor_tensor_reduce(ne[:, t % 2, h, 0:w], ps[:, h, 0:w],
                                             nb[:, z_, h, NA_OFF[t]:NA_OFF[t] + w], 1.0, -3e38, ALU.add, ALU.max,
                                             nm[:, t % 2, 2, h:h + 1]).then_inc(s["t_masked"], 1)
                dve.wait_ge(s["t_masked"], i * 16 + (8 * c + 2 * t + 2))
                dve.tensor_scalar(nm[:, t % 2, 0, :], nm[:, t % 2, 2, :], -1.0, None, ALU.mult)\
                    .then_inc(s["t_neg"], 1)

            def copy_b(i, c, t):
                dve.wait_ge(s["t_turned"], i * 8 + (4 * c + t + 1))
                if NA_W[t] == 3 * P:
                    dve.tensor_copy(npt[:, 2, :], ps[:, 3, 0:2 * P])
                dve.tensor_copy(npt[0:META, 3, :], ps[0:META, 3, 2 * P:4 * P]).then_inc(s["t_copied_b"], 1)

            def scale(i, c, t):
                dve.wait_ge(s["t_exp"], i * 16 + (8 * c + 2 * t + 2))
                dve.reciprocal(nm[:, t % 2, 3, :], nm[:, t % 2, 1, :]).then_inc(s["t_inv"], 1)
                dve.wait_ge(s["t_inv"], i * 8 + (4 * c + t + 1))
                dve.wait_ge(s["t_summed"], i * 8 + (4 * c + t + 1))
                for h in range(2):
                    d = slice(h * HD, (h + 1) * HD)
                    dve.tensor_scalar(no[:, t % 2, d], ps[:, 4, d], nm[:, t % 2, 3, h:h + 1], None, ALU.mult)\
                        .then_inc(s["t_out"], 1)

            def gated(i, c, t):
                q = slice(t * P, (t + 1) * P)
                dve.wait_ge(s["t_back"], i * 8 + (4 * c + t + 1))
                dve.tensor_tensor(ny[:, t % 2, :], ps[:, 4, 0:P], ng[:, c % 2, q], ALU.mult).then_inc(s["t_y"], 1)
                dve.wait_ge(s["t_y"], i * 8 + (4 * c + t + 1))
                hi = y_high[:, bass.ds(i * 2 + c, 1), q]
                y = ny[:, t % 2:t % 2 + 1, :]
                dve.tensor_copy(hi, y).then_inc(s["t_high"], 1)
                dve.wait_ge(s["t_high"], i * 8 + (4 * c + t + 1))
                dve.tensor_tensor(y_low[:, bass.ds(i * 2 + c, 1), q], y, hi.bitcast(F32), ALU.subtract)\
                    .then_inc(s["t_low"], 1)

            def keep(i, c, m):
                dve.wait_ge(s["q_sq"], i * 4 + (2 * c + m + 1))
                if m == 0:
                    dve.tensor_copy(halves(nk[:, c % 2, :]), wide(5)).then_inc(s["q_kept"], 1)
                else:
                    dve.tensor_copy(nq[:, c % 2, :], ps[:, 7, :]).then_inc(s["q_kept"], 1)

            def normed(i, c, m):
                dst = (nk, nq)[m][:, c % 2, :]
                dve.wait_ge(s["q_root"], i * 8 + (4 * c + 2 * m + 2))
                dve.scalar_tensor_tensor(dst, dst, (col(V_NK), nq_gain[:, 0:1])[m], root2[:, m, 0:(L, S)[m]],
                                         ALU.mult, ALU.mult).then_inc(s["q_normed"], 1)

            def gate(i, c):
                dve.wait_ge(s["g_part"], i * 6 + (3 * c + 3))
                dve.tensor_tensor(ng[:, c % 2, :], ps[:, 7, :], sig[:], ALU.mult).then_inc(s["g_done"], 1)

            def pair(i, c):
                ahead = N_NA + 4 * (c + 1) + 3
                masked(i, c, 0, ahead)
                copy_b(i, c, 0)
                keep(i, c + 1, 0)
                scale(i, c, 0)
                masked(i, c, 1, ahead + 1)
                copy_b(i, c, 1)
                keep(i, c + 1, 1)
                gated(i, c, 0)
                scale(i, c, 1)
                masked(i, c, 2, ahead + 2)
                normed(i, c + 1, 0)
                copy_b(i, c, 2)
                gated(i, c, 1)
                scale(i, c, 2)
                masked(i, c, 3, ahead + 3)
                normed(i, c + 1, 1)
                copy_b(i, c, 3)
                gated(i, c, 2)
                scale(i, c, 3)
                gate(i, c + 1)
                gated(i, c, 3)

            keep(0, 0, 0)
            make_high(dve, N_NA + 3)
            keep(0, 0, 1)
            make_high(dve, N_NA + 4)
            normed(0, 0, 0)
            normed(0, 0, 1)
            make_high(dve, N_NA + 5)
            make_high(dve, N_NA + 6)
            gate(0, 0)
            with dve.Fori(0, 3) as i:
                pair(i, 0)
                pair(i, 1)
            pair(3, 0)
            masked(3, 1, 0, N_NA + 4 * 2 + 3)
            for t in range(4):
                if t < 3:
                    dve.wait_ge(s["t_scored"], 28 + t + 2)
                copy_b(3, 1, t)
                if t < 3:
                    masked(3, 1, t + 1, None)
                if t:
                    gated(3, 1, t - 1)
                scale(3, 1, t)
            gated(3, 1, 3)
            for m in range(8):
                dve.wait_ge(strip_used, N_ON + m + 1)
                dve.tensor_tensor(x_t[:, m, :], x_t[:, m, :], ps[:, (m - EARLY) % 8, :], ALU.add)\
                    .then_inc(s["on_added"], 1)
                make_high(dve, N_ON + m + 4)

            after(dve, "on")
            for t in range(4):
                dve.wait_ge(s["out_turned"], 2 * t + 2)
                dve.tensor_copy(y_tok[:, t, 512:D], ps[:, 2 * t + 1, :]).then_inc(s["out_right"], 1)


_INS = ["x", "mix_norm", "w_in", "q_norm", "k_norm", "sinks", "sgu_norm", "w_s", "b_s", "w_oa", "w_ob", "w_out",
        "ffn_norm", "w_up", "conv_w", "conv_b", "w_down", "meta_tokens_2", "norm_w_2", "w_in_2",
        "q_lat_norm_w_2", "kv_lat_norm_w_2", "w_uq_2", "w_ukv_2", "mla_qn_w_2", "mla_qpe_w_2", "mla_kn_w_2",
        "mla_kpe_w_2", "na_q_norm_w_2", "na_k_norm_w_2", "na_meta_bias_2", "w_out_2"]


def _grouped():
    g, r, c = np.meshgrid(np.arange(CG), np.arange(8), np.arange(16), indexing="ij")
    return (r * GW + g * 16 + c).ravel()


def _constants():
    f = np.float32
    i = np.arange(P)
    rot = np.zeros((P, P), f)
    for b in (0, 64):
        for d in range(32):
            rot[b + d + 32, b + d] = -1
            rot[b + d, b + d + 32] = 1
    pos = np.concatenate([np.arange(META), META + _grouped()]).astype(f)
    inv = (f(10000.0) ** (-(np.arange(0, 64, 2, dtype=f) / f(64)))).astype(f)
    ang = (pos[None, :] * np.tile(inv, 4)[:, None]).astype(f)
    gap = i[:, None] + P - np.arange(2 * P)[None, :]
    dist = np.where((gap >= 0) & (gap < 128), -gap, -1e33).astype(f)
    slope = np.broadcast_to(np.exp2(-(np.arange(ATT_H) + 1.0)).astype(f), (P, ATT_H))
    cq = i % 16
    ck = np.arange(3 * P) % 16 + np.arange(3 * P) // P * 16

    def window(first, at, n):
        c0 = np.clip(at + cq - 8, 0, GW - 16)
        k = first + ck[:n]
        return np.where((k[None, :] >= c0[:, None]) & (k[None, :] < c0[:, None] + 16), 0, -1e30)

    mask = np.concatenate([window(0, 16, 3 * P), window(0, 0, 2 * P), window(32, 48, 2 * P)], 1).astype(f)
    return {"c_ident": np.eye(P, dtype=f), "c_blocks": np.kron(np.eye(2), np.ones((64, 64))).astype(f),
            "c_rot": rot, "c_cos": np.cos(ang).astype(f), "c_sin": np.sin(ang).astype(f), "c_dist": dist,
            "c_slope": slope, "c_mask": mask}


def _relative():
    q, k = np.arange(P), np.arange(3 * P)
    dr = (k % P // 16)[None, :] - (q // 16)[:, None] + 7
    dc = (k // P * 16 - 16 + k % 16)[None, :] - (q % 16)[:, None] + 15
    return dr, np.clip(dc, 0, 30)


def kernel(**inputs):
    import concourse.bacc as _bacc
    from concourse.bass_utils import run_bass_kernel_spmd as _run

    nc = _bacc.Bacc("TRN2", target_bir_lowering=False, num_devices=1)
    feeds = {n: inputs[n] for n in _INS}
    dr, dc = _relative()
    feeds["rel_bias"] = np.asarray(inputs["na_rel_bias_2"])[0][:, dr, dc]
    feeds.update(_constants())
    arrays, args = {}, []
    for name, a in feeds.items():
        a = np.ascontiguousarray(a)
        arrays[f"in_{name}_dram"] = a
        args.append(nc.dram_tensor(f"in_{name}_dram", a.shape, mybir.dt.from_np(a.dtype), kind="ExternalInput").ap())
    args.append(nc.dram_tensor("out_0_dram", (1, S, D), F32, kind="ExternalOutput").ap())
    program(nc, *args)
    r = _run(nc, [arrays], core_ids=[0])
    return r.results[0]["out_0_dram"]
```

```python
from contextlib import ExitStack

import numpy as np

import concourse.bass as bass
from concourse import mybir

ACT = mybir.ActivationFunctionType
ALU = mybir.AluOpType
AX = mybir.AxisListType
F32 = mybir.dt.float32
F32R = mybir.dt.float32r

P = 128
D = 1024
KT = D // P
S = 512
META = 16
L = S + META
HALF = L // 2
EPS = 1e-6
ATT_H, KV_H, HD = 8, 2, 64
SGU = 512
FF = 2816
FT = FF // P
MH = 8
MLA_SCALE = 192.0 ** -0.5
NH = 16
GW = 64
CG = 4

N_SGU = 0
N_QKV = N_SGU + 8
N_GATE = N_QKV + 6
N_MERGE = N_GATE + 16
N_OUT = N_MERGE + 8
N_UP = N_OUT + 8
N_DOWN = N_UP + 2 * FT
N_LAT = N_DOWN + 3 * KT
N_MLA = N_LAT + 5
N_OM = N_MLA + 16
N_NA = N_OM + 8
N_ON = N_NA + 32
N_END = N_ON + 8
RAW = 2
RING = 4

V_MIX, V_FFN, V_N2, V_QL, V_KL, V_QN, V_KN, V_SGU = 0, 8, 16, 24, 26, 28, 29, 30
V_AQ, V_AK, V_NQ, V_NK, V_QPE, V_KPE, V_ROWS = 34, 35, 36, 37, 38, 39, 40
C_CONV, C_CONVB = 0, 3 * 2 * FT
C_V = C_CONVB + 2 * FT

NA_W = [2 * P, 3 * P, 3 * P, 2 * P]
NA_G = [0, 0, 1, 2]
NA_OFF = [META + 3 * P, 0, 0, 2 * META + 5 * P]
NA_COLS = 3 * META + 7 * P
OUT_BANK = [[5, 6, 7, 0], [1, 2, 3, 4]]
GATE_BANK = [6, 7, 4, 5]
OM_BANK = [7, 5, 2, 3, 0, 1, 4, 7]
EARLY = 3
ON_CUT = [(0, 6, 7), (0, 6, 7), (0, 3, 4), (4, 6, 7)]
MASK_COLS = 7 * P


def program(nc, x, mix_norm, w_in, q_norm, k_norm, sinks, sgu_norm, w_s, b_s, w_oa, w_ob, w_out,
            ffn_norm, w_up, conv_w, conv_b, w_down, meta_tokens_2, norm_w_2, w_in_2,
            q_lat_norm_w_2, kv_lat_norm_w_2, w_uq_2, w_ukv_2, mla_qn_w_2, mla_qpe_w_2, mla_kn_w_2,
            mla_kpe_w_2, na_q_norm_w_2, na_k_norm_w_2, na_meta_bias_2, w_out_2, rel_bias,
            c_ident, c_blocks, c_rot, c_cos, c_sin, c_dist, c_slope, c_mask, out):
    with ExitStack() as ctx:
        def sb(name, shape, dt=F32, at=ctx):
            return at.enter_context(nc.sbuf_tensor(name, shape, dt))

        def sem(name):
            return ctx.enter_context(nc.semaphore(name))

        ident = sb("ident", [P, P])
        ones = sb("ones", [P, P])
        blocks = sb("blocks", [P, P])
        rot = sb("rot", [P, P])
        eps = sb("eps", [P, 1])
        cv = sb("cv", [P, C_V + V_ROWS])
        aq_gain = sb("aq_gain", [P, 1])
        nq_gain = sb("nq_gain", [P, 1])
        x_t = sb("x_t", [P, KT, S])
        h_high = sb("h_high", [P, KT, L], F32R)
        h_low = sb("h_low", [P, KT, L], F32R)
        w_raw = sb("w_raw", [P, RAW, KT * P])
        w_high = sb("w_high", [P, RING, KT * P], F32R)
        w_low = sb("w_low", [P, RING, KT * P], F32R)
        sq = sb("sq", [P, 2, L])
        root = sb("root", [P, 2, L])
        scaled = sb("scaled", [P, 2, L])
        with ExitStack() as one:
            a_high = sb("a_high", [P, 8, S], F32R, one)
            a_low = sb("a_low", [P, 8, S], F32R, one)
            bias_s = sb("bias_s", [P, 4, P], F32, one)
            dist = sb("dist", [P, 2 * P], F32, one)
            slope = sb("slope", [P, ATT_H], F32, one)
            sink = sb("sink", [P, ATT_H], F32, one)
            k_t = sb("k_t", [P, S], F32, one)
            q_t = sb("q_t", [P, 4, S], F32, one)
            v_f = sb("v_f", [P, S], F32, one)
            v_tok = sb("v_tok", [P, 4, P], F32, one)
            with ExitStack() as a:
                x_tok = sb("x_tok", [P, 4, D], F32, a)
                meta_tok = sb("meta_tok", [META, D], F32, a)
                meta_t = sb("meta_t", [P, KT, META], F32, a)
                rows_a = sb("rows_a", [4 * FT, P], F32, a)
                rows_b = sb("rows_b", [4 * FT, P], F32, a)
                rows_v = sb("rows_v", [V_ROWS, P], F32, a)
            with ExitStack() as a:
                uv = sb("uv", [P, 8, S], F32, a)
                uv_tok = sb("uv_tok", [P, 4, SGU], F32, a)
            with ExitStack() as a:
                gates = sb("gates", [P, 16, S], F32, a)
                ws_raw = sb("ws_raw", [P, 8, P], F32, a)
                ws_t = sb("ws_t", [P, 8, P], F32, a)
            with ExitStack() as a:
                a.enter_context(nc.sbuf_tensor("gates_", [P, 16, S], F32))
                q_st = sb("q_st", [P, S], F32, a)
                bias_h = sb("bias_h", [P, 2, 2 * P], F32, a)
                att_e = sb("att_e", [P, 2, 2 * P], F32, a)
                att_p = sb("att_p", [P, 4, P], F32, a)
                att_m = sb("att_m", [P, 6, 2], F32, a)
                att_y = sb("att_y", [P, 2, P], F32, a)
        with ExitStack() as two:
            m_high = sb("m_high", [P, FT, S], F32R, two)
            m_low = sb("m_low", [P, FT, S], F32R, two)
            z = sb("z", [P, 4, S], F32, two)
            zg = sb("zg", [P, 2, S], F32, two)
        with ExitStack() as three:
            y_high = sb("y_high", [P, 8, S], F32R, three)
            y_low = sb("y_low", [P, 8, S], F32R, three)
            y_f = sb("y_f", [P, S], F32, three)
            with ExitStack() as a:
                cos = sb("cos", [P, L], F32, a)
                sin = sb("sin", [P, L], F32, a)
                ql_high = sb("ql_high", [P, 2, S], F32R, a)
                ql_low = sb("ql_low", [P, 2, S], F32R, a)
                kl_high = sb("kl_high", [P, 2, L], F32R, a)
                kl_low = sb("kl_low", [P, 2, L], F32R, a)
                k_pe = sb("k_pe", [P, L], F32, a)
                q_pe = sb("q_pe", [64, 2, S], F32, a)
                kn = sb("kn", [P, 2, L], F32, a)
                qn = sb("qn", [P, 2, S], F32, a)
                mv = sb("mv", [P, 2, 5, P], F32, a)
                gm = sb("gm", [P, 2, S], F32, a)
                mvf = sb("mvf", [P, L], F32, a)
                m_sig = sb("m_sig", [P, S], F32, a)
                me = sb("me", [P, 2, L], F32, a)
                mp = sb("mp", [P, 5 * P], F32, a)
                mm_ = sb("mm_", [P, 2, 4], F32, a)
            with ExitStack() as a:
                mask = sb("mask", [P, MASK_COLS], F32, a)
                meta_b = sb("meta_b", [P, NH * META], F32, a)
                rel = sb("rel", [P, 2, 2, 3 * P], F32, a)
                nb = sb("nb", [P, 2, 2, NA_COLS], F32, a)
                nk = sb("nk", [P, 2, L], F32, a)
                nq = sb("nq", [P, 2, S], F32, a)
                nv = sb("nv", [P, 2, 5, P], F32, a)
                ng = sb("ng", [P, 2, S], F32, a)
                nvf = sb("nvf", [P, L], F32, a)
                sig = sb("sig", [P, S], F32, a)
                ne = sb("ne", [P, 2, 2, META + 3 * P], F32, a)
                npt = sb("npt", [P, 4, 2 * P], F32, a)
                nm = sb("nm", [P, 2, 4, 2], F32, a)
                no = sb("no", [P, 2, P], F32, a)
                ny = sb("ny", [P, 2, P], F32, a)
            with ExitStack() as a:
                y_tok = sb("y_tok", [P, 4, D], F32, a)
        ps = ctx.enter_context(nc.psum_tensor("ps", [P, 8, 512], F32))

        def wide(bank):
            return ps[:, bank:bank + 2, 0:HALF]

        def halves(ap):
            return ap.rearrange("p (h c) -> p h c", h=2)

        landed = [sem(f"strip_landed_{i}") for i in range(RAW)]
        high_made = sem("high_made")
        low_made = sem("low_made")
        strip_used = sem("strip_used")

        def strip_sources(n, i):
            def cols(w, c, k0=0, kn=KT):
                v = w[0].rearrange("(k p) c -> p k c", p=P)
                h = (kn + 1) // 2
                return [(slice(0, P), (a, b), P, v[:, k0 + a:k0 + b, bass.ds(c, P)])
                        for a, b in ((0, h), (h, kn))]
            if n < N_QKV:
                return cols(w_in, (n - N_SGU + i) * P + 768)
            if n < N_GATE:
                m = n - N_QKV
                if m < 2:
                    return cols(w_in, 512 + m * P)
                v = w_in[0].rearrange("(k p) c -> p k c", p=P)
                return [("c", g * HD, HD, v[:, :, g * 256 + (m - 2) * HD:g * 256 + (m - 1) * HD])
                        for g in range(2)]
            if n < N_MERGE:
                return cols(w_in, (n - N_GATE + i) * P + 1792)
            if n < N_OUT:
                m = n - N_MERGE
                c = i * P + ((m - m % 4) * P + (m % 4) // 2 * 256)
                if m % 2 == 0:
                    v = w_oa[0].rearrange("(g j d) c -> g d j c", g=2, d=HD)
                    return [(slice(g * HD, g * HD + HD), (0, 4), 256, v[g][:, :, bass.ds(c, 256)])
                            for g in range(2)]
                v = w_ob[0].rearrange("(k p) c -> p k c", p=P)
                return [(slice(0, P), (a, a + 2), 256, v[:, a:a + 2, bass.ds(c, 256)]) for a in (0, 2)]
            if n < N_UP:
                return cols(w_out, (n - N_OUT + i) * P)
            if n < N_DOWN:
                m = n - N_UP
                c = ((m - m % 4) // 2 + m % 2) * P + (m % 4) // 2 * FF
                return cols(w_up, i * (P // 2) + c)
            if n < N_LAT:
                m, part = divmod(n - N_DOWN, 3)
                return cols(w_down, i * P + m * P, 8 * part, 8 if part < 2 else 6)
            if n < N_MLA:
                m = n - N_LAT
                if m < 4:
                    return cols(w_in_2, m * P)
                v = w_in_2[0].rearrange("(k p) c -> p k c", p=P)
                return [("c", g * 64, 64, v[:, :, 512:576]) for g in range(2)]
            if n < N_OM:
                g, gate = divmod(n - N_MLA, 2)
                if gate:
                    return cols(w_in_2, i * (P // 2) + g * P + 576)
                kv, q = (w[0].rearrange("(k p) c -> p k c", p=P) for w in (w_ukv_2, w_uq_2))
                return [("h", 0, (2, 256), kv[:, :, bass.ds(i * 128 + g * 256, 256)]),
                        ("h", 512, (2, 192), q[:, :, bass.ds(i * 96 + g * 192, 192)])]
            if n < N_NA:
                return cols(w_out_2, (n - N_OM + i) * P)
            if n < N_ON:
                m = n - N_NA
                pair, s = (m - m % 4) // 4, m % 4
                c = (2624, 1600, 3648, 4672)[s]
                return cols(w_in_2, i * (P // 4) + pair * P + c)
            return cols(w_out_2, (n - N_ON + i) * P, KT)

        def load_strip(sp, n, i=0):
            if n >= RAW:
                sp.wait_ge(low_made, i + (n - RAW + 1))
            slot = w_raw[:, n % RAW, :]
            for load in strip_sources(n, i):
                if load[0] == "c":
                    _, c, width, src = load
                    dst = slot.rearrange("p (k c) -> p k c", c=P)[:, :, c:c + width]
                elif load[0] == "h":
                    _, c, (k, row), src = load
                    dst = slot[:, c:c + k * row].rearrange("p (k c) -> p k c", k=k)
                else:
                    rows, (a, b), width, src = load
                    dst = slot.rearrange("p (k c) -> p k c", c=width)[rows, a:b, :]
                sp.dma_start(dst, src).then_inc(landed[n % RAW], 16)

        def make_high(dve, n, i=0):
            if isinstance(i, int) and n + i >= N_END:
                return
            dve.wait_ge(landed[n % RAW], i * 16 + 32 * (n // RAW + 1))
            if n >= RING:
                dve.wait_ge(strip_used, i + (n - RING + 1))
            dve.tensor_copy(w_high[:, n % RING, :], w_raw[:, n % RAW, :]).then_inc(high_made, 1)

        def make_low(pool, n, i=0):
            pool.wait_ge(high_made, i + (n + 1))
            pool.tensor_tensor(w_low[:, n % RING, :], w_raw[:, n % RAW, :],
                               w_high[:, n % RING, :].bitcast(F32), ALU.subtract).then_inc(low_made, 1)

        def product(pe, acc, n, col, step, tiles, moving, first=True, last=True, ks=None, width=P, ready=None):
            for k in range(*(ks or (0, tiles))):
                if ready:
                    pe.wait_ge(s[ready[0]], ready[1] + k + 1)
                c = col + k * step
                wh, wl = w_high[:, n % RING, c:c + width], w_low[:, n % RING, c:c + width]
                mh, ml = moving(k)
                pe.matmul(acc, wh, mh, start=first and k == 0, stop=False)
                pe.matmul(acc, wh, ml, start=False, stop=False)
                done = pe.matmul(acc, wl, mh, start=False, stop=last and k == tiles - 1)
            return done

        def product_two(pe, banks, n, ready):
            for k in range(KT):
                pe.wait_ge(s[ready[0]], ready[1] + k + 1)
                for o in range(2):
                    done = product(pe, ps[:, banks[o], :], n + o, 0, P, KT, hx, ks=(k, k + 1))
                    if k == KT - 1:
                        done.then_inc(strip_used, 1)

        def product_wide(pe, bank, n, col, step, tiles, high, low, ks=None):
            for k in range(*(ks or (0, tiles))):
                c = col + k * step
                wh, wl = w_high[:, n % RING, c:c + P], w_low[:, n % RING, c:c + P]
                for wt, mt, one_, end in ((wh, high, k == 0, False), (wh, low, False, False),
                                          (wl, high, False, k == tiles - 1)):
                    for h in range(2):
                        done = pe.matmul(ps[:, bank + h, 0:HALF], wt, mt[:, k, h * HALF:h * HALF + HALF],
                                         start=one_, stop=end)
            return done

        def hx(k):
            return h_high[:, k, META:L], h_low[:, k, META:L]

        def yx(k):
            return y_high[:, k, :], y_low[:, k, :]

        names = """consts_in more_in ident_in x_in meta_in ones_set x_turned x_ready rows_turned cols_ready gain_ready meta_turned
            meta_ready ws_cut ws_turned ws_ready
            norm_sq norm_sum norm_root norm_scaled norm_high norm_low
            gelu_done sv_sq sv_sum sv_root sv_normed sv_turned sv_tok_ready mixed mix_biased mix_gated
            mix_high mix_low
            i1_sq i1_sum i1_ln i1_root i1_normed v_copied v_turned v_ready
            j_staged j_bias a_scored a_masked a_part a_exp a_sink_exp a_probs a_turned
            a_copied a_summed a_y a_high a_low gate_kept
            g_sig m_part m_whole m_high_ m_low_ o_added
            z_first z_mid z_done z_silu z_gated z_high z_low d_added d_placed
            lat_sq lat_sum lat_root lat_scaled lat_high lat_low pe_root_part pe_sum
            pe_part pe_turned tables_in
            p_made p_sq p_kept p_sum p_root p_normed qr_turned qr_part mv_kept mv_turned mv_ready mg_part mg_done
            s_scored s_top s_neg s_exp s_inv s_probs s_turned s_copied_a s_copied_b s_summed s_y s_high s_low
            om_added rel_in nb_ready
            q_sq q_kept q_sum q_root q_normed nv_kept nv_turned nv_ready g_part g_done
            t_scored t_masked t_neg t_exp t_inv t_turned t_copied_a t_copied_b t_summed t_out t_back t_y
            t_high t_low
            on_added out_turned out_left out_right out_stored""".split()
        s = {name: sem(name) for name in names}
        N_CONST, N_MORE = 20, 12

        ends = {
            "setup": [("x_ready", 8), ("gain_ready", 2), ("meta_ready", 1), ("norm_low", 16)],
            "qkv": [("i1_normed", 5), ("v_ready", 1), ("sv_normed", 4)],
            "att": [("a_low", 16), ("gate_kept", 16)],
            "out": [("o_added", 8)],
            "norm2": [("norm_low", 24)],
            "up": [("z_low", FT)],
            "down": [("d_placed", 8)],
            "norm3": [("norm_low", 32)],
            "lat": [("lat_low", 4), ("pe_part", 5)],
            "mla": [("s_low", 8)],
            "om": [("om_added", 8)],
            "na": [("t_low", 32)],
        }

        def after(eng, stage):
            for name, value in ends[stage]:
                eng.wait_ge(s[name], value)

        def col(c):
            return cv[:, C_V + c:C_V + c + 1]

        def norm_sum(pe, t, acc, k, n=S):
            pe.wait_ge(s["norm_sq"], 8 * t + k + 1)
            pe.matmul(acc, ones[:], sq[:, k % 2, 0:n], start=k == 0, stop=k == KT - 1)\
                .then_inc(s["norm_sum"], 1)

        def norm_square(act, t, k, src, n=S):
            if k >= 2:
                act.wait_ge(s["norm_sum"], 8 * t + k - 1)
            act.activation(sq[:, k % 2, 0:n], src, ACT.Square).then_inc(s["norm_sq"], 1)

        def norm_act(act, t, acc, n, high):
            act.wait_ge(s["norm_sum"], 8 * t + KT)
            act.activation(root[:, 0, 0:n], acc, ACT.Ln, bias=eps[:, 0:1], scale=1.0 / D).then_inc(s["norm_root"], 1)
            act.wait_ge(s["norm_root"], 2 * t + 1)
            act.activation(root[:, 0, 0:n], root[:, 0, 0:n], ACT.Exp, scale=-0.5).then_inc(s["norm_root"], 1)
            for k in range(KT):
                act.wait_ge(s["norm_scaled"], 8 * t + k + 1)
                act.activation(high(k), scaled[:, k % 2, 0:n], ACT.Copy).then_inc(s["norm_high"], 1)

        def norm_dve(dve, t, src, gain, n, high, low):
            dve.wait_ge(s["norm_root"], 2 * t + 2)
            for k in range(KT + 1):
                if k < KT:
                    if k >= 2:
                        dve.wait_ge(s["norm_low"], 8 * t + k - 1)
                    dve.scalar_tensor_tensor(scaled[:, k % 2, 0:n], src(k), col(gain + k), root[:, 0, 0:n],
                                             ALU.mult, ALU.mult).then_inc(s["norm_scaled"], 1)
                if k >= 1:
                    dve.wait_ge(s["norm_high"], 8 * t + k)
                    dve.tensor_tensor(low(k - 1), scaled[:, (k - 1) % 2, 0:n], high(k - 1).bitcast(F32),
                                      ALU.subtract).then_inc(s["norm_low"], 1)

        def xs(k):
            return x_t[:, k, :]

        def hh(k):
            return h_high[:, k, META:L]

        def hl(k):
            return h_low[:, k, META:L]

        block = ctx.enter_context(nc.Block())

        @block.sync
        def _(sp):
            sp.dma_start(ident[:], c_ident).then_inc(s["ident_in"], 16)
            for t in range(4):
                sp.dma_start(x_tok[:, t, :], x[0, t * P:(t + 1) * P, :]).then_inc(s["x_in"], 16)
            for n in range(RAW):
                load_strip(sp, n)
            sp.dma_start(ws_raw[:], w_s[0].rearrange("g i j -> i g j")).then_inc(s["meta_in"], 16)
            for n in range(RAW, 4):
                load_strip(sp, n)
            for n in range(4, N_GATE):
                load_strip(sp, n)
            for n0, n1, step in ((N_GATE, N_MERGE, 4), (N_MERGE, N_OUT, 4), (N_OUT, N_UP, 4), (N_UP, N_DOWN, 4)):
                with sp.Fori(0, (n1 - n0) // step) as turn:
                    i = turn * step
                    for n in range(n0, n0 + step):
                        load_strip(sp, n, i)
            with sp.Fori(0, 2) as i:
                for n in range(N_DOWN, N_DOWN + 12):
                    sp.wait_ge(low_made, i * 12 + (n - RAW + 1))
                    slot = w_raw[:, n % RAW, :].rearrange("p (k c) -> p k c", c=P)
                    for rows, (a, b), width, src in strip_sources(n, i * 4):
                        sp.dma_start(slot[:, a:b, :], src).then_inc(landed[n % RAW], 16)
            for n in range(N_LAT, N_LAT + 3):
                load_strip(sp, n)
            after(sp, "down")
            sp.dma_start(cos[:], c_cos).then_inc(s["tables_in"], 16)
            sp.dma_start(sin[:], c_sin).then_inc(s["tables_in"], 16)
            for n in range(N_LAT + 3, N_MLA):
                load_strip(sp, n)
            for n0, n1 in ((N_MLA, N_OM), (N_OM, N_NA)):
                with sp.Fori(0, (n1 - n0) // 4) as turn:
                    i = turn * 4
                    for n in range(n0, n0 + 4):
                        load_strip(sp, n, i)
            for n in range(N_NA, N_NA + 3):
                load_strip(sp, n)
            after(sp, "mla")
            sp.dma_start(mask[:], c_mask).then_inc(s["tables_in"], 16)
            sp.dma_start(meta_b[:], na_meta_bias_2[0].rearrange("h m -> (h m)").partition_broadcast(P))\
                .then_inc(s["tables_in"], 16)
            sp.dma_start(rel[:, 0], rel_bias[0:2].rearrange("h q k -> q h k")).then_inc(s["rel_in"], 16)
            for n in range(N_NA + 3, N_NA + 4):
                load_strip(sp, n)

            def na_loads(i, c):
                for m in range(4):
                    load_strip(sp, N_NA + 4 * c + m, i * 8)
                    if m == 1:
                        sp.wait_ge(s["nb_ready"], i * 18 + 9 * c)
                        sp.dma_start(rel[:, c % 2], rel_bias[bass.ds(i * 4 + 2 * c, 2)].rearrange("h q k -> q h k"))\
                            .then_inc(s["rel_in"], 16)

            with sp.Fori(0, 3) as i:
                na_loads(i, 1)
                na_loads(i, 2)
            na_loads(3, 1)
            for n in range(N_ON, N_END):
                load_strip(sp, n)
            for half in range(2):
                for t in range(4):
                    if half == 0:
                        sp.wait_ge(s["out_left"], t + 1)
                    elif t % 2 == 0:
                        sp.wait_ge(s["out_left"], 5 + t // 2)
                    else:
                        sp.wait_ge(s["out_right"], 1 + t // 2)
                    d = slice(half * 512, half * 512 + 512)
                    dst = out[0].rearrange("(r g c) d -> g r c d", g=CG, c=16)[t]
                    sp.dma_start(dst[:, :, d], y_tok[:, t, d]).then_inc(s["out_stored"], 16)
            sp.wait_ge(s["out_stored"], 16 * 8)

        @block.gpsimd
        def _(pool):
            nc.gpsimd.memset(ones[:], 1.0).then_inc(s["ones_set"], 1)
            nc.gpsimd.memset(eps[:], EPS).then_inc(s["ones_set"], 1)
            taps = conv_w[0].rearrange("t (c p) -> t c p", p=P)
            bs = b_s[0].rearrange("(q h) i -> h q i", h=2)
            more = [(rows_a[0:44, :], taps[0]), (rows_a[44:88, :], taps[1]), (rows_b[0:44, :], taps[2]),
                    (rows_b[44:88, :], conv_b[0].rearrange("(c p) -> c p", p=P)), (meta_tok[:], meta_tokens_2),
                    (blocks[:], c_blocks), (rot[:], c_rot), (dist[:], c_dist), (slope[:], c_slope),
                    (sink[:], sinks[0].partition_broadcast(P))]
            more += [(bias_s[h * 64:(h + 1) * 64, :, :], bs[h].partition_broadcast(64)) for h in range(2)]
            assert len(more) == N_MORE
            for dst, src in more:
                pool.dma_start(dst, src).then_inc(s["more_in"], 16)
            for n in range(0, N_GATE):
                make_low(pool, n)
                if n == 3:
                    pool.wait_ge(s["meta_in"], 16)
                    pool.affine_select(out=ws_raw[:], in_=ws_raw[:], compare_op=ALU.is_ge, fill=0.0, base=0,
                                       pattern=[[0, 8], [-1, P]], channel_multiplier=1).then_inc(s["ws_cut"], 1)
            for n0, n1, step in ((N_GATE, N_MERGE, 4), (N_MERGE, N_OUT, 4), (N_OUT, N_UP, 4), (N_UP, N_DOWN, 4),
                                 (N_DOWN, N_LAT, 12)):
                with pool.Fori(0, (n1 - n0) // step) as turn:
                    i = turn * step
                    for n in range(n0, n0 + step):
                        make_low(pool, n, i)
            for n in range(N_LAT, N_MLA):
                make_low(pool, n)
            for n0, n1 in ((N_MLA, N_OM), (N_OM, N_NA)):
                with pool.Fori(0, (n1 - n0) // 4) as turn:
                    i = turn * 4
                    for n in range(n0, n0 + 4):
                        make_low(pool, n, i)
            for n in range(N_NA, N_NA + 4):
                make_low(pool, n)

            def bias_table(i, c):
                pool.wait_ge(s["rel_in"], i * 32 + (16 * c + 16))
                if c:
                    pool.wait_ge(s["q_normed"], i * 4 + 2 * c)
                z_ = c % 2
                for h in range(2):
                    for o, m, r in ((0, 0, 0), (META + 3 * P, 3 * P, P), (2 * META + 5 * P, 5 * P, 0)):
                        w = 3 * P if o == 0 else 2 * P
                        pool.tensor_tensor(nb[:, z_, h, o + META:o + META + w], rel[:, z_, h, r:r + w],
                                           mask[:, m:m + w], ALU.add).then_inc(s["nb_ready"], 1)
                for o in (0, META + 3 * P, 2 * META + 5 * P):
                    pool.tensor_copy(nb[:, z_, :, o:o + META],
                                     meta_b[:, bass.ds(i * 64 + 32 * c, 32)].rearrange("p (h m) -> p h m", h=2))\
                        .then_inc(s["nb_ready"], 1)

            pool.wait_ge(s["tables_in"], 64)
            bias_table(0, 0)
            with pool.Fori(0, 3) as i:
                for c in (1, 2):
                    for m in range(4):
                        make_low(pool, N_NA + 4 * c + m, i * 8)
                    bias_table(i, c)
            for m in range(4):
                make_low(pool, N_NA + 28 + m)
            bias_table(3, 1)
            for n in range(N_ON, N_END):
                make_low(pool, n)

        @block.tensor
        def _(pe):
            pe.wait_ge(s["ident_in"], 16)
            pe.wait_ge(s["ones_set"], 2)
            for k in range(KT):
                if k == 0:
                    pe.wait_ge(s["x_in"], 64)
                if k >= 2:
                    pe.wait_ge(s["x_ready"], k - 1)
                for t in range(4):
                    mm = pe.transpose(ps[:, k % 2, t * P:(t + 1) * P], x_tok[:, t, k * P:(k + 1) * P], ident[:])
                mm.then_inc(s["x_turned"], 1)
                if k:
                    norm_sum(pe, 0, ps[:, 3, :], k - 1)
            pe.wait_ge(s["consts_in"], 16 * N_CONST)
            pe.wait_ge(s["more_in"], 16 * N_MORE)
            pe.transpose(ps[:, 7, 0:88], rows_a[:], ident[0:88, 0:88])
            pe.transpose(ps[:, 7, 88:176], rows_b[:], ident[0:88, 0:88])
            pe.transpose(ps[:, 7, 176:176 + V_ROWS], rows_v[:], ident[0:V_ROWS, 0:V_ROWS])\
                .then_inc(s["rows_turned"], 1)
            norm_sum(pe, 0, ps[:, 3, :], KT - 1)
            for k in range(KT):
                t = pe.transpose(ps[:, 2, k * META:(k + 1) * META], meta_tok[:, k * P:(k + 1) * P],
                                 ident[0:META, 0:META])
            t.then_inc(s["meta_turned"], 1)

            pe.wait_ge(low_made, 2)
            product_two(pe, (0, 1), N_SGU, ("norm_low", 0))
            for k in range(KT):
                norm_sum(pe, 1, ps[:, 4, 0:META], k, META)
            for n in range(N_SGU + 2, N_QKV):
                pe.wait_ge(low_made, n + 1)
                if n == 2:
                    pe.wait_ge(s["meta_ready"], 1)
                if n >= 4:
                    pe.wait_ge(s["gelu_done"], n - 3)
                product(pe, ps[:, n % 4, :], n, 0, P, KT, hx).then_inc(strip_used, 1)

            bank = [4, 5, 6, 7, 4, 5]
            item = [0, None, 1, 2, 3, 4]

            def qkv_sum(m):
                j = item[m]
                pe.wait_ge(s["i1_sq"], j + 1)
                if j >= 2:
                    pe.wait_ge(s["i1_root"], j - 1)
                pe.matmul(ps[:, j % 2, :], blocks[:], sq[:, j % 2, 0:S], start=True, stop=True)\
                    .then_inc(s["i1_sum"], 1)

            def sv_sum(k):
                pe.wait_ge(s["sv_sq"], k + 1)
                pe.matmul(ps[:, 2, :], ones[:], sq[:, k % 2, 0:S], start=k == 0, stop=k == 3).then_inc(s["sv_sum"], 1)

            for m in range(6):
                n = N_QKV + m
                pe.wait_ge(low_made, n + 1)
                if m >= 4:
                    pe.wait_ge(s["i1_normed"], 1) if m == 4 else pe.wait_ge(s["v_copied"], 1)
                product(pe, ps[:, bank[m], :], n, 0, P, KT, hx).then_inc(strip_used, 1)
                if m == 0:
                    pe.wait_ge(s["gelu_done"], 8)
                    for k in range(4):
                        sv_sum(k)
                    qkv_sum(0)
                elif m == 2:
                    pe.wait_ge(s["v_copied"], 1)
                    for t in range(4):
                        mm = pe.transpose(ps[:, 3, t * P:(t + 1) * P], v_f[:, t * P:(t + 1) * P], ident[:])
                    mm.then_inc(s["v_turned"], 1)
                    qkv_sum(2)
                elif m > 2:
                    qkv_sum(m)

            after(pe, "qkv")
            pe.wait_ge(s["ws_cut"], 1)
            for g in range(8):
                mm = pe.transpose(ps[:, 6 + g // 4, (g % 4) * P:(g % 4 + 1) * P], ws_raw[:, g, :], ident[:])
            mm.then_inc(s["ws_turned"], 1)
            for c in range(4):
                if c >= 2:
                    pe.wait_ge(s["sv_tok_ready"], c - 1)
                for k in range(4):
                    mm = pe.transpose(ps[:, c % 2, k * P:(k + 1) * P], uv[:, 4 + k, c * P:(c + 1) * P], ident[:])
                mm.then_inc(s["sv_turned"], 1)
            pe.wait_ge(s["ws_ready"], 1)
            pe.wait_ge(s["sv_tok_ready"], 4)
            for q in range(4):
                if q >= 2:
                    pe.wait_ge(s["mix_biased"], 2 * (q - 1))
                for c in range(4):
                    mm = pe.matmul(ps[:, 2 + 2 * (q % 2) + c // 2, (c % 2) * 256:(c % 2) * 256 + 256],
                                   uv_tok[:, c, q * P:(q + 1) * P],
                                   ws_t[:, 2 * q:2 * q + 2, :].rearrange("p g i -> p (g i)"), start=True, stop=True)
                mm.then_inc(s["mixed"], 1)


            def a_scores(j, t, first=False):
                w = 2 * P if t else P
                if t == 0:
                    pe.wait_ge(s["j_staged"], j + 1)
                if not first:
                    pe.wait_ge(s["a_masked"], j * 8 + 2 * t)
                for h in range(2):
                    mm = pe.matmul(ps[:, h, 0:w], q_st[h * HD:(h + 1) * HD, t * P:(t + 1) * P],
                                   k_t[h * HD:(h + 1) * HD, (t + 1) * P - w:(t + 1) * P], start=True, stop=True)
                mm.then_inc(s["a_scored"], 1)

            def a_turn(j, t):
                pe.wait_ge(s["a_probs"], j * 8 + (2 * t + 2))
                for a in range(2 if t else 1):
                    for h in range(2):
                        mm = pe.transpose(ps[:, 2, (2 * a + h) * P:(2 * a + h + 1) * P],
                                          att_e[:, h, a * P:(a + 1) * P], ident[:])
                mm.then_inc(s["a_turned"], 1)

            def a_weigh(j, t):
                pe.wait_ge(s["a_copied"], j * 4 + (t + 1))
                ks = [t - 1, t] if t else [0]
                for a, kt in enumerate(ks):
                    mm = pe.matmul(ps[:, 3, 0:2 * P], v_tok[:, kt, :],
                                   att_p[:, 2 * a:2 * a + 2, :].rearrange("p h q -> p (h q)"),
                                   start=a == 0, stop=a == len(ks) - 1)
                mm.then_inc(s["a_summed"], 1)

            def a_pair(j, more=True):
                for t in range(4):
                    pe.wait_ge(low_made, j * 4 + (N_GATE + t + 1))
                    product(pe, ps[:, GATE_BANK[t], :], N_GATE + t, 0, P, KT, hx, ks=(0, 7))
                    a_turn(j, t)
                    product(pe, ps[:, GATE_BANK[t], :], N_GATE + t, 0, P, KT, hx, ks=(7, 8)).then_inc(strip_used, 1)
                    if t < 3:
                        a_scores(j, t + 1)
                    elif more:
                        a_scores(j + 1, 0)
                    a_weigh(j, t)

            a_scores(0, 0, first=True)
            with pe.Fori(0, 3) as j:
                a_pair(j)
            a_pair(3, more=False)

            after(pe, "att")
            for u in range(4):
                if u >= 2:
                    pe.wait_ge(s["m_part"], 4 * (u - 1))
                for b in range(2):
                    n = N_MERGE + 2 * u + b
                    pe.wait_ge(low_made, n + 1)
                    for m in range(2):
                        mm = product(pe, ps[:, 4 * b + 2 * (u % 2) + m, :], n, m * P, 2 * P, 4,
                                     lambda k: (a_high[:, 4 * b + k, :], a_low[:, 4 * b + k, :]))
                    mm.then_inc(strip_used, 1)

            pe.wait_ge(s["m_part"], 12)
            pe.wait_ge(low_made, N_OUT + 2)
            product_two(pe, (0, 1), N_OUT, ("m_low_", 0))
            for m in range(2, 8):
                pe.wait_ge(low_made, N_OUT + m + 1)
                if m >= 4:
                    pe.wait_ge(s["o_added"], m - 3)
                product(pe, ps[:, m % 4, :], N_OUT + m, 0, P, KT, hx).then_inc(strip_used, 1)
                if m == 2:
                    norm_sum(pe, 2, ps[:, 7, :], 0)
                norm_sum(pe, 2, ps[:, 7, :], m - 1)
            norm_sum(pe, 2, ps[:, 7, :], 7)

            with pe.Fori(0, 11) as i:
                for m in range(4):
                    pe.wait_ge(low_made, i * 4 + (N_UP + m + 1))
                    if m >= 2:
                        pe.wait_ge(s["z_done"], i * 4 + (m - 1))
                    product(pe, ps[:, m, :], N_UP + m, 0, P, KT, hx, ready=("norm_low", 16) if m == 0 else None)\
                        .then_inc(strip_used, 1)
                pe.wait_ge(s["z_done"], i * 4 + 3)

            for m in range(8):
                for part in range(3):
                    n = N_DOWN + 3 * m + part
                    pe.wait_ge(low_made, n + 1)
                    if part == 0 and m >= 4:
                        pe.wait_ge(s["d_added"], m - 3)
                    product(pe, ps[:, 4 + m % 4, :], n, 0, P, 8 if part < 2 else 6,
                            lambda k: (m_high[:, 8 * part + k, :], m_low[:, 8 * part + k, :]),
                            part == 0, part == 2, ready=("z_low", 8 * part) if m == 0 else None)\
                        .then_inc(strip_used, 1)
                    if m and part == 0:
                        norm_sum(pe, 3, ps[:, 0, :], m - 1)
            norm_sum(pe, 3, ps[:, 0, :], 7)

            pe.wait_ge(low_made, N_LAT + 2)
            product_two(pe, (0, 1), N_LAT, ("norm_low", 24))
            for m in range(2, 5):
                pe.wait_ge(low_made, N_LAT + m + 1)
                product_wide(pe, 2 * m - 2, N_LAT + m, 0, P, KT, h_high, h_low).then_inc(strip_used, 1)
            pe.wait_ge(s["pe_root_part"], 1)
            pe.wait_ge(s["pe_part"], 1)
            for h in range(2):
                mm = pe.matmul(ps[:, 6 + h, 0:HALF], blocks[:], sq[:, 0, h * HALF:(h + 1) * HALF],
                               start=True, stop=True)
            mm.then_inc(s["pe_sum"], 1)
            pe.wait_ge(s["pe_root_part"], 3)
            for k in range(2):
                pe.wait_ge(s["lat_sq"], k + 1)
                pe.matmul(ps[:, 6, :], ones[:], sq[:, k % 2, 0:S], start=k == 0, stop=k == 1)\
                    .then_inc(s["lat_sum"], 1)
            pe.wait_ge(s["lat_root"], 2)
            for k in range(2):
                pe.wait_ge(s["lat_sq"], k + 3)
                for h in range(2):
                    mm = pe.matmul(ps[:, 6 + h, 0:HALF], ones[:], sq[:, k % 2, h * HALF:(h + 1) * HALF],
                                   start=k == 0, stop=k == 1)
                mm.then_inc(s["lat_sum"], 1)
            pe.wait_ge(s["pe_part"], 2)
            pe.wait_ge(s["lat_scaled"], 2)
            for h in range(2):
                mm = pe.matmul(ps[:, h, 0:HALF], rot[:], k_pe[:, h * HALF:(h + 1) * HALF], start=True, stop=True)
            mm.then_inc(s["pe_turned"], 1)

            after(pe, "lat")
            GATE_PART = ((0, 2), (2, 4), (4, 6), (6, 7), (7, 8))

            def ql(k):
                return ql_high[:, k, :], ql_low[:, k, :]

            def m_scores(i, c, t, first=False):
                z_ = c % 2
                if t == 0:
                    pe.wait_ge(s["p_normed"], i * 6 + (3 * c + 3))
                    pe.wait_ge(s["qr_part"], i * 6 + (3 * c + 3))
                if not first:
                    pe.wait_ge(s["s_copied_b"], i * 8 + (4 * c + t))
                for b in range(2):
                    pe.matmul(ps[:, b, 0:HALF], qn[:, z_, t * P:(t + 1) * P],
                              kn[:, z_, b * HALF:(b + 1) * HALF], start=True, stop=False)
                    mm = pe.matmul(ps[:, b, 0:HALF], q_pe[:, z_, t * P:(t + 1) * P],
                                   k_pe[0:64, b * HALF:(b + 1) * HALF], start=False, stop=True)
                mm.then_inc(s["s_scored"], 1)

            def m_turn(i, c, t):
                pe.wait_ge(s["s_probs"], i * 8 + (4 * c + t + 1))
                for a in range(4):
                    pe.transpose(ps[:, 4, a * P:(a + 1) * P], me[:, t % 2, a * P:(a + 1) * P], ident[:])
                pe.transpose(ps[0:META, 1, 3 * P:4 * P], me[:, t % 2, 4 * P:L], ident[:]).then_inc(s["s_turned"], 1)

            def m_weigh(i, c, t):
                pe.wait_ge(s["s_copied_a"], i * 8 + (4 * c + t + 1))
                pe.wait_ge(s["s_copied_b"], i * 8 + (4 * c + t + 1))
                if t == 0:
                    pe.wait_ge(s["mv_ready"], i * 4 + (2 * c + 2))
                    if c:
                        pe.wait_ge(s["s_y"], i * 2 + c)
                for a in range(5):
                    r = P if a < 4 else META
                    mm = pe.matmul(ps[:, 6, t * P:(t + 1) * P], mv[0:r, c % 2, a, :],
                                   mp[0:r, a * P:(a + 1) * P], start=a == 0, stop=a == 4)
                mm.then_inc(s["s_summed"], 1)

            def m_project(i, c, what):
                n = N_MLA + 2 * c
                if what == 0:
                    pe.wait_ge(low_made, i * 4 + (n + 1))
                    if c:
                        pe.wait_ge(s["p_root"], i * 12 + (6 * c - 1))
                    mm = product(pe, ps[0:64, 7, :], n, 512 + P, 192, 2, ql, width=64)
                elif what == 3:
                    pe.wait_ge(s["qr_part"], i * 6 + (3 * c + 1))
                    mm = product(pe, ps[:, 7, :], n, 512, 192, 2, ql)
                else:
                    if what == 2:
                        pe.wait_ge(s["p_root"], i * 12 + (6 * c + 3))
                    elif c:
                        pe.wait_ge(s["mv_ready"], i * 4 + 2 * c)
                    mm = product_wide(pe, 2, n, P if what == 2 else 0, 256, 2, kl_high, kl_low)
                mm.then_inc(strip_used if what == 3 else s["p_made"], 1)

            def m_sums(i, c, item):
                pe.wait_ge(s["p_sq"], i * 6 + (3 * c + item + 1))
                pe.wait_ge(s["p_kept"], i * 6 + (3 * c + item + 1))
                if item == 0:
                    mm = pe.matmul(ps[:, 7, :], ones[0:64, :], sq[0:64, 0, 0:S], start=True, stop=True)
                elif item == 2:
                    mm = pe.matmul(ps[:, 7, :], ones[:], sq[:, 0, 0:S], start=True, stop=True)
                else:
                    for b in range(2):
                        mm = pe.matmul(ps[:, 2 + b, 0:HALF], ones[:], sq[:, 1, b * HALF:(b + 1) * HALF],
                                       start=True, stop=True)
                mm.then_inc(s["p_sum"], 1)

            def m_rotate(i, c):
                pe.wait_ge(s["p_normed"], i * 6 + (3 * c + 1))
                pe.matmul(ps[:, 7, :], rot[0:64, :], q_pe[:, c % 2, :], start=True, stop=True)\
                    .then_inc(s["qr_turned"], 1)

            def m_gate(i, c, part):
                n = N_MLA + 2 * c + 1
                if part == 0:
                    pe.wait_ge(low_made, i * 4 + (n + 1))
                    if c:
                        pe.wait_ge(s["mg_done"], i * 2 + c)
                mm = product(pe, ps[:, 5, :], n, 0, P, KT, hx, ks=GATE_PART[part])
                if part == 4:
                    mm.then_inc(strip_used, 1)

            def m_turn_v(i, c):
                pe.wait_ge(s["mv_kept"], i * 2 + (c + 1))
                for a in range(4):
                    pe.transpose(ps[:, 2, a * P:(a + 1) * P], mvf[:, a * P:(a + 1) * P], ident[:])
                pe.transpose(ps[0:META, 3, 0:P], mvf[:, 4 * P:L], ident[:]).then_inc(s["mv_turned"], 1)

            def head(i, c, more=True):
                def early(t, ks):
                    if ks[0] == 0:
                        pe.wait_ge(low_made, N_OM + t + 1)
                    product(pe, ps[:, OM_BANK[t], :], N_OM + t, 0, P, KT, yx, last=False, ks=ks)

                if more:
                    m_project(i, c + 1, 0)
                    m_project(i, c + 1, 1)
                else:
                    pe.wait_ge(s["s_low"], 7)
                    pe.wait_ge(s["p_root"], 48)
                    pe.wait_ge(s["mg_done"], 8)
                    pe.wait_ge(s["mv_ready"], 16)
                    early(0, (0, 4))
                m_turn(i, c, 0)
                if more:
                    m_gate(i, c + 1, 0)
                else:
                    early(0, (4, 7))
                m_scores(i, c, 1)
                m_weigh(i, c, 0)
                if more:
                    m_sums(i, c + 1, 0)
                    m_sums(i, c + 1, 1)
                    m_gate(i, c + 1, 1)
                else:
                    early(1, (0, 4))
                m_turn(i, c, 1)
                if more:
                    m_rotate(i, c + 1)
                else:
                    early(1, (4, 7))
                m_scores(i, c, 2)
                m_weigh(i, c, 1)
                if more:
                    m_project(i, c + 1, 2)
                    m_gate(i, c + 1, 2)
                else:
                    early(2, (0, 4))
                m_turn(i, c, 2)
                if more:
                    m_project(i, c + 1, 3)
                m_scores(i, c, 3)
                m_weigh(i, c, 2)
                if more:
                    m_sums(i, c + 1, 2)
                    m_turn_v(i, c + 1)
                    m_gate(i, c + 1, 3)
                else:
                    early(2, (4, 7))
                m_turn(i, c, 3)
                if more:
                    m_gate(i, c + 1, 4)
                    m_scores(i, c + 1, 0)
                m_weigh(i, c, 3)

            m_project(0, 0, 0)
            m_project(0, 0, 1)
            m_gate(0, 0, 0)
            m_sums(0, 0, 0)
            m_sums(0, 0, 1)
            m_gate(0, 0, 1)
            m_gate(0, 0, 2)
            m_rotate(0, 0)
            m_project(0, 0, 2)
            m_project(0, 0, 3)
            m_gate(0, 0, 3)
            m_sums(0, 0, 2)
            m_turn_v(0, 0)
            m_gate(0, 0, 4)
            m_scores(0, 0, 0, first=True)
            head(0, 0)
            with pe.Fori(0, 3) as i:
                head(i, 1)
                head(i, 2)
            head(3, 1, more=False)

            after(pe, "mla")
            for m in range(8):
                pe.wait_ge(low_made, N_OM + m + 1)
                if m == 7:
                    pe.wait_ge(s["om_added"], 1)
                early = m < EARLY
                product(pe, ps[:, OM_BANK[m], :], N_OM + m, 0, P, KT, yx, first=not early,
                        ks=(7, 8) if early else None).then_inc(strip_used, 1)

            pe.wait_ge(s["om_added"], 2)

            def scores(i, c, t, first=False):
                w, g, z_ = NA_W[t], NA_G[t], c % 2
                if t == 0:
                    pe.wait_ge(s["q_normed"], i * 4 + (2 * c + 2))
                if not first:
                    pe.wait_ge(s["t_masked"], i * 16 + (8 * c + 2 * t))
                for h in range(2):
                    q = nq[h * HD:(h + 1) * HD, z_, t * P:(t + 1) * P]
                    spans = [(0, META + w, 0)] if g == 0 else [(0, META, 0), (META, META + w, META + g * P)]
                    for a, b, k0 in spans:
                        mm = pe.matmul(ps[:, h, a:b], q, nk[h * HD:(h + 1) * HD, z_, k0:k0 + b - a],
                                       start=True, stop=True)
                mm.then_inc(s["t_scored"], 1)

            def turn(i, c, t):
                pe.wait_ge(s["t_exp"], i * 16 + (8 * c + 2 * t + 2))
                for a in range(NA_W[t] // P):
                    for h in range(2):
                        o = (2 * a + h) % 4 * P
                        pe.transpose(ps[:, 2 + a // 2, o:o + P], ne[:, t % 2, h, META + a * P:META + (a + 1) * P],
                                     ident[:])
                for h in range(2):
                    mm = pe.transpose(ps[0:META, 3, (2 + h) * P:(3 + h) * P], ne[:, t % 2, h, 0:META], ident[:])
                mm.then_inc(s["t_turned"], 1)

            def weigh(i, c, t):
                n, z_ = NA_W[t] // P, c % 2
                pe.wait_ge(s["t_copied_a"], i * 8 + (4 * c + t + 1))
                pe.wait_ge(s["t_copied_b"], i * 8 + (4 * c + t + 1))
                if t or c:
                    pe.wait_ge(s["t_y"], i * 8 + (4 * c + t))
                if t == 0:
                    pe.wait_ge(s["nv_ready"], i * 4 + (2 * c + 2))
                for h in range(2):
                    d = slice(h * HD, (h + 1) * HD)
                    for a in range(n):
                        pe.matmul(ps[:, 4, d], npt[:, a, h * P:(h + 1) * P], nv[:, z_, NA_G[t] + a, d],
                                  start=a == 0, stop=False)
                    mm = pe.matmul(ps[:, 4, d], npt[0:META, 3, h * P:(h + 1) * P], nv[0:META, z_, 4, d],
                                   start=False, stop=True)
                mm.then_inc(s["t_summed"], 1)

            def back(i, c, t):
                pe.wait_ge(s["t_out"], i * 16 + (8 * c + 2 * t + 2))
                pe.transpose(ps[:, 4, 0:P], no[:, t % 2, :], ident[:]).then_inc(s["t_back"], 1)

            def project(i, c, m, half=None):
                n = N_NA + 4 * c + m
                if half != 1:
                    pe.wait_ge(low_made, i * 8 + (n + 1))
                ks = {None: (0, 8), 0: (0, 4), 1: (4, 8)}[half]
                if m in (0, 2):
                    mm = product_wide(pe, 5, n, 0, P, KT, h_high, h_low, ks)
                else:
                    mm = product(pe, ps[:, 7, :], n, 0, P, KT, hx, ks=ks)
                if half != 0:
                    mm.then_inc(strip_used, 1)

            def sums(i, c, m):
                pe.wait_ge(s["q_sq"], i * 4 + (2 * c + m + 1))
                pe.wait_ge(s["q_kept"], i * 4 + (2 * c + m + 1))
                if m:
                    mm = pe.matmul(ps[:, 7, :], blocks[:], sq[:, 1, 0:S], start=True, stop=True)
                else:
                    for h in range(2):
                        mm = pe.matmul(ps[:, 5 + h, 0:HALF], blocks[:], sq[:, 0, h * HALF:(h + 1) * HALF],
                                       start=True, stop=True)
                mm.then_inc(s["q_sum"], 1)

            def turn_v(i, c):
                pe.wait_ge(s["nv_kept"], i * 2 + (c + 1))
                for a in range(4):
                    pe.transpose(ps[:, 5, a * P:(a + 1) * P], nvf[:, META + a * P:META + (a + 1) * P], ident[:])
                pe.transpose(ps[0:META, 6, 0:P], nvf[:, 0:META], ident[:]).then_inc(s["nv_turned"], 1)

            def pair(i, c, more=True):
                for t in range(4):
                    if more:
                        if t == 0:
                            pe.wait_ge(s["nv_ready"], i * 4 + (2 * c + 2))
                        elif t == 1:
                            pe.wait_ge(s["g_done"], i * 2 + (c + 1))
                        else:
                            pe.wait_ge(s["q_root"], i * 8 + (4 * c + 2 * t + 1))
                        project(i, c + 1, t, 0)
                    else:
                        if t < EARLY:
                            pe.wait_ge(low_made, N_ON + t + 1)
                        if t == 0:
                            pe.wait_ge(s["nv_ready"], 16)
                            pe.wait_ge(s["g_done"], 8)
                            pe.wait_ge(s["t_low"], 27)
                        m, cut = min(t, EARLY - 1), ON_CUT[t]
                        product(pe, ps[:, 5 + m, :], N_ON + m, 0, P, KT, yx, last=False, ks=cut[:2])
                    if t:
                        back(i, c, t - 1)
                    elif c:
                        back(i, c - 1, 3)
                    if more and t in (1, 2):
                        sums(i, c + 1, t - 1)
                    turn(i, c, t)
                    if more:
                        project(i, c + 1, t, 1)
                    else:
                        if t == 0:
                            pe.wait_ge(s["t_low"], 28)
                        product(pe, ps[:, 5 + m, :], N_ON + m, 0, P, KT, yx, last=False, ks=cut[1:])
                    if t < 3:
                        scores(i, c, t + 1)
                    elif more:
                        scores(i, c + 1, 0)
                    weigh(i, c, t)
                if more:
                    turn_v(i, c + 1)

            project(0, 0, 0)
            after(pe, "om")
            project(0, 0, 1)
            sums(0, 0, 0)
            pe.wait_ge(s["q_root"], 1)
            project(0, 0, 2)
            sums(0, 0, 1)
            pe.wait_ge(s["q_root"], 3)
            project(0, 0, 3)
            turn_v(0, 0)
            scores(0, 0, 0, first=True)
            pair(0, 0)
            with pe.Fori(0, 3) as i:
                pair(i, 1)
                pair(i, 2)
            pair(3, 1, more=False)
            back(3, 1, 3)

            after(pe, "na")
            def out_turn(half):
                pe.wait_ge(s["on_added"], 4 * half + 4)
                for t in range(4):
                    for k in range(4):
                        mm = pe.transpose(ps[:, OUT_BANK[half][t], k * P:(k + 1) * P],
                                          x_t[:, 4 * half + k, t * P:(t + 1) * P], ident[:])
                    mm.then_inc(s["out_turned"], 1)

            for m in range(8):
                pe.wait_ge(low_made, N_ON + m + 1)
                if m < EARLY:
                    product(pe, ps[:, 5 + m, :], N_ON + m, (KT - 1) * P, P, 1,
                            lambda k: yx(KT - 1), first=False).then_inc(strip_used, 1)
                else:
                    product(pe, ps[:, m - EARLY, :], N_ON + m, 0, P, KT, yx).then_inc(strip_used, 1)
                if m == 5:
                    out_turn(0)
            out_turn(1)

        @block.scalar
        def _(act):
            c = 0

            def const(dst, src):
                nonlocal c
                c += 1
                act.dma_start(dst, src).then_inc(s["consts_in"], 16)

            for r, k, v in ((V_MIX, 8, mix_norm), (V_FFN, 8, ffn_norm), (V_N2, 8, norm_w_2),
                            (V_QL, 2, q_lat_norm_w_2), (V_KL, 2, kv_lat_norm_w_2), (V_QN, 1, mla_qn_w_2),
                            (V_KN, 1, mla_kn_w_2), (V_SGU, 4, sgu_norm)):
                const(rows_v[r:r + k, :], v[0].rearrange("(c p) -> c p", p=P))
            for r, v in ((V_AQ, q_norm), (V_AK, k_norm), (V_NQ, na_q_norm_w_2), (V_NK, na_k_norm_w_2),
                         (V_QPE, mla_qpe_w_2), (V_KPE, mla_kpe_w_2)):
                for h in range(2):
                    const(rows_v[r:r + 1, h * 64:(h + 1) * 64], v)
            assert c == N_CONST, c

            act.preload_act_table_set("natural_log_exp_and_others")
            for k in range(KT):
                act.wait_ge(s["x_ready"], k + 1)
                norm_square(act, 0, k, xs(k))
            act.wait_ge(s["ones_set"], 2)
            norm_act(act, 0, ps[:, 3, :], S, hh)
            act.wait_ge(s["meta_turned"], 1)
            act.activation(meta_t[:], ps[:, 2, 0:P].rearrange("p (k m) -> p k m", m=META), ACT.Copy)\
                .then_inc(s["meta_ready"], 1)
            act.wait_ge(s["meta_ready"], 1)
            for k in range(KT):
                norm_square(act, 1, k, meta_t[:, k, :], META)
            norm_act(act, 1, ps[:, 4, 0:META], META, lambda k: h_high[:, k, 0:META])

            after(act, "setup")
            for n in range(8):
                act.wait_ge(strip_used, N_SGU + n + 1)
                act.activation(uv[:, n, :], ps[:, n % 4, :], ACT.Gelu_apprx_tanh).then_inc(s["gelu_done"], 1)

            act.preload_act_table_set("natural_log_exp_and_others")
            for k in range(4):
                act.wait_ge(s["gelu_done"], 5 + k)
                if k >= 2:
                    act.wait_ge(s["sv_sum"], k - 1)
                act.activation(sq[:, k % 2, 0:S], uv[:, 4 + k, :], ACT.Square).then_inc(s["sv_sq"], 1)
            act.wait_ge(s["sv_sum"], 4)
            act.activation(root[:, 1, 0:S], ps[:, 2, :], ACT.Ln, bias=eps[:, 0:1], scale=1.0 / SGU)\
                .then_inc(s["sv_root"], 1)
            act.wait_ge(s["sv_root"], 1)
            act.activation(root[:, 1, 0:S], root[:, 1, 0:S], ACT.Exp, scale=-0.5).then_inc(s["sv_root"], 1)
            banks = [4, 6, 7, 4, 5]
            strips = [0, 2, 3, 4, 5]

            def i1_root(j):
                act.wait_ge(s["i1_sum"], j + 1)
                if j >= 2:
                    act.wait_ge(s["i1_normed"], j - 1)
                if j == 1:
                    act.wait_ge(s["sv_normed"], 4)
                act.activation(root[:, j % 2, 0:S], ps[:, j % 2, :], ACT.Ln, bias=eps[:, 0:1], scale=1.0 / HD)\
                    .then_inc(s["i1_ln"], 1)
                act.wait_ge(s["i1_ln"], j + 1)
                act.activation(root[:, j % 2, 0:S], root[:, j % 2, 0:S], ACT.Exp, scale=-0.5)\
                    .then_inc(s["i1_root"], 1)

            for j in range(5):
                act.wait_ge(strip_used, N_QKV + strips[j] + 1)
                if j >= 2:
                    act.wait_ge(s["i1_sum"], j - 1)
                act.activation(sq[:, j % 2, 0:S], ps[:, banks[j], :], ACT.Square).then_inc(s["i1_sq"], 1)
                if j == 0:
                    i1_root(0)
                    act.wait_ge(strip_used, N_QKV + 2)
                    act.activation(v_f[:], ps[:, 5, :], ACT.Copy).then_inc(s["v_copied"], 1)
                elif j >= 2:
                    i1_root(j - 1)
            i1_root(4)

            after(act, "qkv")
            act.wait_ge(s["ws_turned"], 1)
            act.activation(ws_t[:].rearrange("p (b g) i -> p b (g i)", b=2), ps[:, 6:8, :], ACT.Copy)\
                .then_inc(s["ws_ready"], 1)
            for q in range(4):
                if q == 2:
                    act.wait_ge(s["mixed"], 4)
                    act.activation(q_st[:], q_t[:, 0, :], ACT.Copy).then_inc(s["j_staged"], 1)
                act.wait_ge(s["mix_gated"], 2 * (q + 1))
                act.activation(a_high[:, 4 + q, :], uv[:, q, :], ACT.Copy).then_inc(s["mix_high"], 1)


            def a_pair(j, more=True):
                for t in range(4):
                    w = 2 * P if t else P
                    act.wait_ge(s["a_part"], j * 20 + (5 * t + 2))
                    for h in range(2):
                        act.activation(att_e[:, h, 0:w], att_e[:, h, 0:w], ACT.Exp, bias=att_m[:, 1, h:h + 1],
                                       accum_out=att_m[:, 2, h:h + 1]).then_inc(s["a_exp"], 1)
                    act.wait_ge(s["a_part"], j * 20 + (5 * t + 3))
                    act.activation(att_m[:, 4, :], att_m[:, 3, :], ACT.Exp).then_inc(s["a_sink_exp"], 1)
                    if t == 3 and more:
                        act.activation(q_st[:], q_t[:, bass.ds(j + 1, 1), :], ACT.Copy).then_inc(s["j_staged"], 1)
                    act.wait_ge(s["a_turned"], j * 4 + (t + 1))
                    act.activation(att_p[:, 0:w // 64, :], ps[:, 2, 0:2 * w].rearrange("p (a q) -> p a q", q=P),
                                   ACT.Copy).then_inc(s["a_copied"], 1)
                    act.wait_ge(s["a_summed"], j * 4 + (t + 1))
                    for h in range(2):
                        r = slice(h * HD, (h + 1) * HD)
                        act.activation(att_y[r, t % 2, :], ps[r, 3, h * P:(h + 1) * P], ACT.Copy)\
                            .then_inc(s["a_y"], 1)

            with act.Fori(0, 3) as j:
                a_pair(j)
            a_pair(3, more=False)

            after(act, "att")
            with act.Fori(0, 2) as i:
                for u in range(2):
                    for m in range(2):
                        for b in range(2):
                            g = gates[:, bass.ds(i * 4 + (8 * b + 2 * u + m), 1), :]
                            act.activation(g, g, ACT.Sigmoid).then_inc(s["g_sig"], 1)
            with act.Fori(0, 2) as i:
                for m in range(4):
                    act.wait_ge(s["m_whole"], i * 4 + (m + 1))
                    act.activation(h_high[:, bass.ds(i * 4 + m, 1), META:L], scaled[:, m % 2, 0:S], ACT.Copy)\
                        .then_inc(s["m_high_"], 1)

            act.preload_act_table_set("natural_log_exp_and_others")
            for k in range(KT):
                act.wait_ge(s["o_added"], k + 1)
                norm_square(act, 2, k, xs(k))
            norm_act(act, 2, ps[:, 7, :], S, hh)

            after(act, "norm2")
            with act.Fori(0, 11) as i:
                for m in range(4):
                    ct = m % 2 + FT * (m // 2)
                    act.wait_ge(strip_used, i * 4 + (N_UP + m + 1))
                    act.activation(z[:, m, :], ps[:, m, :], ACT.Identity,
                                   scale=cv[:, bass.ds(i * 2 + (C_CONV + 2 * 2 * FT + ct), 1)],
                                   bias=cv[:, bass.ds(i * 2 + (C_CONVB + ct), 1)]).then_inc(s["z_first"], 1)
                    if m >= 2:
                        act.wait_ge(s["z_done"], i * 4 + (m - 1))
                        act.activation(z[:, m - 2, :], z[:, m - 2, :], ACT.Silu).then_inc(s["z_silu"], 1)
                for m in range(2):
                    act.wait_ge(s["z_gated"], i * 2 + (m + 1))
                    act.activation(m_high[:, bass.ds(i * 2 + m, 1), :], zg[:, m, :], ACT.Copy)\
                        .then_inc(s["z_high"], 1)

            act.preload_act_table_set("natural_log_exp_and_others")
            for k in range(KT):
                act.wait_ge(s["d_added"], k + 1)
                act.activation(x_t[:, k, :].rearrange("p (g r c) -> p r g c", g=CG, c=16),
                               z[:, k % 4, :].rearrange("p (r g c) -> p r g c", g=CG, c=16), ACT.Copy)\
                    .then_inc(s["d_placed"], 1)
                act.wait_ge(s["d_placed"], k + 1)
                norm_square(act, 3, k, xs(k))
            norm_act(act, 3, ps[:, 0, :], S, hh)

            after(act, "norm3")
            act.wait_ge(strip_used, N_LAT + 5)
            act.activation(halves(sq[:, 0, :]), wide(6), ACT.Square).then_inc(s["pe_root_part"], 1)
            act.wait_ge(s["pe_sum"], 1)
            act.activation(halves(root[:, 0, :]), wide(6), ACT.Ln, bias=eps[:, 0:1], scale=1.0 / 64)\
                .then_inc(s["pe_root_part"], 1)
            act.wait_ge(s["pe_root_part"], 2)
            act.activation(root[:, 0, :], root[:, 0, :], ACT.Exp, scale=-0.5).then_inc(s["pe_root_part"], 1)
            for m in range(2):
                src, n = ((lambda k: ps[:, k, :]), S) if m == 0 else ((lambda k: wide(2 + 2 * k)), L)
                for k in range(2):
                    if m:
                        act.wait_ge(s["lat_sum"], 2 * m + k - 1)
                    dst = sq[:, k, 0:n] if m == 0 else halves(sq[:, k, :])
                    act.activation(dst, src(k), ACT.Square).then_inc(s["lat_sq"], 1)
                act.wait_ge(s["lat_sum"], 2 * m + 2)
                if m == 0:
                    act.wait_ge(s["pe_part"], 2)
                else:
                    act.wait_ge(s["lat_scaled"], 2)
                dst, acc = (root[:, 0, 0:n], ps[:, 6, :]) if m == 0 else (halves(root[:, 0, :]), wide(6))
                act.activation(dst, acc, ACT.Ln, bias=eps[:, 0:1], scale=1.0 / 256).then_inc(s["lat_root"], 1)
                act.wait_ge(s["lat_root"], m * 2 + 1)
                act.activation(root[:, 0, 0:n], root[:, 0, 0:n], ACT.Exp, scale=-0.5).then_inc(s["lat_root"], 1)
                for k in range(2):
                    act.wait_ge(s["lat_scaled"], 2 * m + k + 1)
                    act.activation((ql_high if m == 0 else kl_high)[:, k, :], scaled[:, k, 0:n], ACT.Copy)\
                        .then_inc(s["lat_high"], 1)

            after(act, "lat")

            def m_expo(i, c, t):
                act.wait_ge(s["s_neg"], i * 8 + (4 * c + t + 1))
                act.activation(halves(me[:, t % 2, :]), wide(0), ACT.Exp, scale=MLA_SCALE,
                               bias=mm_[:, t % 2, 1:2], accum_out=mm_[:, t % 2, 2:3]).then_inc(s["s_exp"], 1)

            def m_copy(i, c, t):
                act.wait_ge(s["s_turned"], i * 8 + (4 * c + t + 1))
                act.activation(mp[:, 0:4 * P], ps[:, 4, :], ACT.Copy).then_inc(s["s_copied_a"], 1)

            def m_square(i, c, item):
                if item < 2:
                    act.wait_ge(s["p_made"], i * 6 + (3 * c + item + 1))
                else:
                    act.wait_ge(strip_used, i * 4 + (N_MLA + 2 * c + 1))
                src, dst = ((ps[0:64, 7, :], sq[0:64, 0, 0:S]), (wide(2), halves(sq[:, 1, :])),
                            (ps[:, 7, :], sq[:, 0, 0:S]))[item]
                act.activation(dst, src, ACT.Square).then_inc(s["p_sq"], 1)

            def m_root(i, c, item):
                act.wait_ge(s["p_sum"], i * 6 + (3 * c + item + 1))
                if item == 2:
                    act.wait_ge(s["p_normed"], i * 6 + (3 * c + 1))
                elif c:
                    act.wait_ge(s["p_normed"], i * 6 + (3 * c - 1 + (item == 0)))
                r, n, src, dst, d = ((slice(0, 64), S, ps[0:64, 7, :], root[0:64, 0, 0:S], 64),
                                     (slice(0, P), L, wide(2), halves(root[:, 1, :]), P),
                                     (slice(0, P), S, ps[:, 7, :], root[:, 0, 0:S], P))[item]
                act.activation(dst, src, ACT.Ln, bias=eps[r, 0:1], scale=1.0 / d).then_inc(s["p_root"], 1)
                act.wait_ge(s["p_root"], i * 12 + (6 * c + 2 * item + 1))
                act.activation(root[r, item % 2, 0:n], root[r, item % 2, 0:n], ACT.Exp, scale=-0.5)\
                    .then_inc(s["p_root"], 1)

            def m_keep_v(i, c):
                act.wait_ge(s["p_made"], i * 6 + (3 * c + 3))
                if c:
                    act.wait_ge(s["mv_turned"], i * 2 + c)
                act.activation(halves(mvf[:]), wide(2), ACT.Copy).then_inc(s["mv_kept"], 1)

            def m_place_v(i, c):
                act.wait_ge(s["mv_turned"], i * 2 + (c + 1))
                act.activation(mv[:, c % 2, 0:4, :], ps[:, 2, :].rearrange("p (a d) -> p a d", d=P), ACT.Copy)\
                    .then_inc(s["mv_ready"], 1)
                act.activation(mv[0:META, c % 2, 4, :], ps[0:META, 3, 0:P], ACT.Copy).then_inc(s["mv_ready"], 1)

            def m_sigmoid(i, c):
                act.wait_ge(strip_used, i * 4 + (N_MLA + 2 * c + 2))
                if c:
                    act.wait_ge(s["mg_done"], i * 2 + c)
                act.activation(m_sig[:], ps[:, 5, :], ACT.Exp, scale=-1.0).then_inc(s["mg_part"], 1)
                act.wait_ge(s["mg_part"], i * 6 + (3 * c + 1))
                act.activation(m_sig[:], m_sig[:], ACT.Ln, bias=1.0).then_inc(s["mg_part"], 1)
                act.wait_ge(s["mg_part"], i * 6 + (3 * c + 2))
                act.activation(m_sig[:], m_sig[:], ACT.Exp, scale=-1.0).then_inc(s["mg_part"], 1)

            def head(i, c, more=True):
                m_expo(i, c, 0)
                m_copy(i, c, 0)
                if more:
                    m_square(i, c + 1, 0)
                    m_square(i, c + 1, 1)
                m_expo(i, c, 1)
                if more:
                    m_root(i, c + 1, 0)
                m_copy(i, c, 1)
                if more:
                    m_root(i, c + 1, 1)
                m_expo(i, c, 2)
                if more:
                    m_keep_v(i, c + 1)
                m_copy(i, c, 2)
                if more:
                    m_square(i, c + 1, 2)
                m_expo(i, c, 3)
                if more:
                    m_root(i, c + 1, 2)
                m_copy(i, c, 3)
                if more:
                    m_place_v(i, c + 1)
                    m_sigmoid(i, c + 1)

            m_square(0, 0, 0)
            m_square(0, 0, 1)
            m_root(0, 0, 0)
            m_root(0, 0, 1)
            m_keep_v(0, 0)
            m_square(0, 0, 2)
            m_root(0, 0, 2)
            m_place_v(0, 0)
            m_sigmoid(0, 0)
            head(0, 0)
            with act.Fori(0, 3) as i:
                head(i, 1)
                head(i, 2)
            head(3, 1, more=False)

            after(act, "mla")

            def expo(i, c, t):
                w = META + NA_W[t]
                act.wait_ge(s["t_neg"], i * 8 + (4 * c + t + 1))
                for h in range(2):
                    act.activation(ne[:, t % 2, h, 0:w], ne[:, t % 2, h, 0:w], ACT.Exp, bias=nm[:, t % 2, 0, h:h + 1],
                                   accum_out=nm[:, t % 2, 1, h:h + 1]).then_inc(s["t_exp"], 1)

            def copy_a(i, c, t):
                act.wait_ge(s["t_turned"], i * 8 + (4 * c + t + 1))
                act.activation(npt[:, 0:2, :], ps[:, 2, :].rearrange("p (a q) -> p a q", a=2), ACT.Copy)\
                    .then_inc(s["t_copied_a"], 1)

            def square(i, c, m):
                act.wait_ge(strip_used, i * 8 + (N_NA + 4 * c + m + 1))
                src = wide(5) if m == 0 else ps[:, 7, :]
                dst = halves(sq[:, 0, :]) if m == 0 else sq[:, 1, 0:S]
                act.activation(dst, src, ACT.Square).then_inc(s["q_sq"], 1)

            def root_ln(i, c, m):
                act.wait_ge(s["q_sum"], i * 4 + (2 * c + m + 1))
                if c:
                    act.wait_ge(s["q_normed"], i * 4 + (2 * c + m - 1))
                src = wide(5) if m == 0 else ps[:, 7, :]
                dst = halves(root[:, 0, :]) if m == 0 else root[:, 1, 0:S]
                act.activation(dst, src, ACT.Ln, bias=eps[:, 0:1], scale=1.0 / HD).then_inc(s["q_root"], 1)

            def root_exp(i, c, m):
                n = L if m == 0 else S
                act.wait_ge(s["q_root"], i * 8 + (4 * c + 2 * m + 1))
                act.activation(root[:, m, 0:n], root[:, m, 0:n], ACT.Exp, scale=-0.5).then_inc(s["q_root"], 1)

            def keep_v(i, c):
                act.wait_ge(strip_used, i * 8 + (N_NA + 4 * c + 3))
                if c:
                    act.wait_ge(s["nv_turned"], i * 2 + c)
                act.activation(halves(nvf[:]), wide(5), ACT.Copy).then_inc(s["nv_kept"], 1)

            def gate(i, c):
                act.wait_ge(strip_used, i * 8 + (N_NA + 4 * c + 4))
                if c:
                    act.wait_ge(s["g_done"], i * 2 + c)
                act.activation(sig[:], ps[:, 7, :], ACT.Exp, scale=-1.0).then_inc(s["g_part"], 1)
                act.wait_ge(s["g_part"], i * 6 + (3 * c + 1))
                act.activation(sig[:], sig[:], ACT.Ln, bias=1.0).then_inc(s["g_part"], 1)
                act.wait_ge(s["g_part"], i * 6 + (3 * c + 2))
                act.activation(sig[:], sig[:], ACT.Exp, scale=-1.0).then_inc(s["g_part"], 1)

            def place_v(i, c):
                act.wait_ge(s["nv_turned"], i * 2 + (c + 1))
                act.activation(nv[:, c % 2, 0:4, :], ps[:, 5, :].rearrange("p (a d) -> p a d", d=P), ACT.Copy)\
                    .then_inc(s["nv_ready"], 1)
                act.activation(nv[0:META, c % 2, 4, :], ps[0:META, 6, 0:P], ACT.Copy).then_inc(s["nv_ready"], 1)

            def pair(i, c, more=True):
                for t in range(4):
                    expo(i, c, t)
                    copy_a(i, c, t)
                    if more and t == 0:
                        square(i, c + 1, 0)
                    elif more and t == 1:
                        root_ln(i, c + 1, 0)
                        square(i, c + 1, 1)
                        root_exp(i, c + 1, 0)
                    elif more and t == 2:
                        root_ln(i, c + 1, 1)
                        root_exp(i, c + 1, 1)
                        keep_v(i, c + 1)
                    elif more:
                        gate(i, c + 1)
                        place_v(i, c + 1)

            square(0, 0, 0)
            square(0, 0, 1)
            root_ln(0, 0, 0)
            root_exp(0, 0, 0)
            root_ln(0, 0, 1)
            root_exp(0, 0, 1)
            keep_v(0, 0)
            gate(0, 0)
            place_v(0, 0)
            pair(0, 0)
            with act.Fori(0, 3) as i:
                pair(i, 1)
                pair(i, 2)
            pair(3, 1, more=False)

            for t in range(4):
                act.wait_ge(s["out_turned"], t + 1)
                act.activation(y_tok[:, t, 0:512], ps[:, OUT_BANK[0][t], :], ACT.Copy).then_inc(s["out_left"], 1)
            for t in (0, 2):
                act.wait_ge(s["out_turned"], 4 + t + 1)
                act.activation(y_tok[:, t, 512:D], ps[:, OUT_BANK[1][t], :], ACT.Copy).then_inc(s["out_left"], 1)

        @block.vector
        def _(dve):
            make_high(dve, 0)
            for k in range(KT):
                dve.wait_ge(s["x_turned"], k + 1)
                dve.tensor_copy(x_t[:, k, :], ps[:, k % 2, :]).then_inc(s["x_ready"], 1)
            make_high(dve, 1)
            dve.wait_ge(s["rows_turned"], 1)
            dve.tensor_copy(cv[:], ps[:, 7, 0:C_V + V_ROWS]).then_inc(s["cols_ready"], 1)
            dve.wait_ge(s["cols_ready"], 1)
            dve.tensor_scalar(aq_gain[:], col(V_AQ), HD ** -0.5, None, ALU.mult).then_inc(s["gain_ready"], 1)
            dve.tensor_scalar(nq_gain[:], col(V_NQ), HD ** -0.5, None, ALU.mult).then_inc(s["gain_ready"], 1)
            norm_dve(dve, 0, xs, V_MIX, S, hh, hl)
            make_high(dve, 2)
            dve.wait_ge(s["meta_ready"], 1)
            norm_dve(dve, 1, lambda k: meta_t[:, k, :], V_N2, META,
                     lambda k: h_high[:, k, 0:META], lambda k: h_low[:, k, 0:META])

            for n in range(N_SGU, N_QKV):
                make_high(dve, n + 3)

            dve.wait_ge(s["gain_ready"], 2)

            def i1_norm(j):
                dve.wait_ge(s["i1_root"], j + 1)
                dst = k_t[:] if j == 0 else q_t[:, j - 1, :]
                gain = col(V_AK) if j == 0 else aq_gain[:, 0:1]
                dve.scalar_tensor_tensor(dst, ps[:, [4, 6, 7, 4, 5][j], :], gain, root[:, j % 2, 0:S],
                                         ALU.mult, ALU.mult).then_inc(s["i1_normed"], 1)

            make_high(dve, N_QKV + 3)
            dve.wait_ge(s["sv_root"], 2)
            for k in range(4):
                dve.scalar_tensor_tensor(uv[:, 4 + k, :], uv[:, 4 + k, :], col(V_SGU + k), root[:, 1, 0:S],
                                         ALU.mult, ALU.mult).then_inc(s["sv_normed"], 1)
            i1_norm(0)
            make_high(dve, N_QKV + 4)
            make_high(dve, N_QKV + 5)
            dve.wait_ge(s["v_turned"], 1)
            dve.tensor_copy(v_tok[:], ps[:, 3, :].rearrange("p (a d) -> p a d", d=P)).then_inc(s["v_ready"], 1)
            for m in range(3, 6):
                i1_norm(m - 2)
                make_high(dve, N_QKV + m + 3)
            i1_norm(4)

            after(dve, "qkv")
            for c in range(4):
                dve.wait_ge(s["sv_turned"], c + 1)
                dve.tensor_copy(uv_tok[:, c, :], ps[:, c % 2, :]).then_inc(s["sv_tok_ready"], 1)
            for q in range(4):
                dve.wait_ge(s["mixed"], q + 1)
                b = 2 + 2 * (q % 2)
                for h in range(2):
                    r = slice(h * 64, (h + 1) * 64)
                    src = ps[r, b:b + 2, :].rearrange("p b (c g i) -> p b c g i", c=2, g=2)[:, :, :, h, :]
                    for c in range(2):
                        ins = dve.tensor_tensor(scaled[r, 0, 256 * c:256 * c + 256].rearrange("p (c i) -> p c i", c=2),
                                                src[:, c], bias_s[r, q:q + 1, :].broadcast_to([64, 2, P]), ALU.add)
                    ins.then_inc(s["mix_biased"], 1)
                    dve.wait_ge(s["mix_biased"], 2 * q + h + 1)
                    dve.tensor_tensor(uv[r, q, :], uv[r, q, :], scaled[r, 0, 0:S], ALU.mult)\
                        .then_inc(s["mix_gated"], 1)
                dve.wait_ge(s["mix_high"], q + 1)
                dve.tensor_tensor(a_low[:, 4 + q, :], uv[:, q, :], a_high[:, 4 + q, :].bitcast(F32),
                                  ALU.subtract).then_inc(s["mix_low"], 1)


            def a_bias(j):
                for h in range(2):
                    dve.tensor_scalar(bias_h[:, h, :], dist[:], slope[:, bass.ds(j + 4 * h, 1)], None, ALU.mult)\
                        .then_inc(s["j_bias"], 1)

            def a_masked(j, t, n):
                w = 2 * P if t else P
                sinks_j = sink[:].rearrange("p (h j) -> p h j", h=2)[:, :, bass.ds(j, 1)]
                dve.wait_ge(s["j_bias"], j * 2 + 2)
                dve.wait_ge(s["a_scored"], j * 4 + (t + 1))
                make_high(dve, n, j * 4)
                for h in range(2):
                    dve.tensor_tensor_reduce(att_e[:, h, 0:w], ps[:, h, 0:w], bias_h[:, h, 2 * P - w:2 * P],
                                             1.0, -3e38, ALU.add, ALU.max, att_m[:, 0, h:h + 1])\
                        .then_inc(s["a_masked"], 1)
                dve.wait_ge(s["a_masked"], j * 8 + (2 * t + 2))
                dve.tensor_tensor(att_m[:, 5, :], att_m[:, 0, :], sinks_j, ALU.max).then_inc(s["a_part"], 1)
                dve.wait_ge(s["a_part"], j * 20 + (5 * t + 1))
                dve.tensor_scalar(att_m[:, 1, :], att_m[:, 5, :], -1.0, None, ALU.mult).then_inc(s["a_part"], 1)
                dve.tensor_tensor(att_m[:, 3, :], sinks_j, att_m[:, 5, :], ALU.subtract).then_inc(s["a_part"], 1)

            def a_scale(j, t):
                w = 2 * P if t else P
                dve.wait_ge(s["a_exp"], j * 8 + (2 * t + 2))
                dve.wait_ge(s["a_sink_exp"], j * 4 + (t + 1))
                dve.tensor_tensor(att_m[:, 3, :], att_m[:, 2, :], att_m[:, 4, :], ALU.add).then_inc(s["a_part"], 1)
                dve.wait_ge(s["a_part"], j * 20 + (5 * t + 4))
                dve.reciprocal(att_m[:, 5, :], att_m[:, 3, :]).then_inc(s["a_part"], 1)
                dve.wait_ge(s["a_part"], j * 20 + (5 * t + 5))
                for h in range(2):
                    dve.tensor_scalar(att_e[:, h, 0:w], att_e[:, h, 0:w], att_m[:, 5, h:h + 1], None, ALU.mult)\
                        .then_inc(s["a_probs"], 1)

            def a_keep(j, t):
                dve.wait_ge(strip_used, j * 4 + (N_GATE + t + 1))
                dve.tensor_copy(gates[:, bass.ds(j * 4 + t, 1), :], ps[:, GATE_BANK[t], :]).then_inc(s["gate_kept"], 1)

            def a_parts(j, t):
                q = slice(t * P, (t + 1) * P)
                hi, y = a_high[:, bass.ds(j, 1), q], att_y[:, t % 2:t % 2 + 1, :]
                dve.wait_ge(s["a_y"], j * 8 + (2 * t + 2))
                dve.tensor_copy(hi, y).then_inc(s["a_high"], 1)
                dve.wait_ge(s["a_high"], j * 4 + (t + 1))
                dve.tensor_tensor(a_low[:, bass.ds(j, 1), q], y, hi.bitcast(F32), ALU.subtract)\
                    .then_inc(s["a_low"], 1)

            def a_pair(j, more=True):
                for t in range(4):
                    a_scale(j, t)
                    a_keep(j, t)
                    if t < 3:
                        a_masked(j, t + 1, N_GATE + t + 4)
                    elif more:
                        a_bias(j + 1)
                        a_masked(j + 1, 0, N_GATE + 3)
                    else:
                        make_high(dve, N_GATE + 16 + 3)
                    a_parts(j, t)

            a_bias(0)
            a_masked(0, 0, N_GATE + 3)
            with dve.Fori(0, 3) as j:
                a_pair(j)
            a_pair(3, more=False)

            after(dve, "att")
            for u in range(4):
                for m in range(2):
                    o = 2 * u + m
                    if o:
                        make_high(dve, N_MERGE + o + 3)
                    dve.wait_ge(strip_used, N_MERGE + 2 * u + 2)
                    for b in range(2):
                        dve.wait_ge(s["g_sig"], 2 * o + b + 1)
                        g = gates[:, 8 * b + o, :]
                        dve.tensor_tensor(g, g, ps[:, 4 * b + 2 * (u % 2) + m, :], ALU.mult).then_inc(s["m_part"], 1)
                    dve.wait_ge(s["m_part"], 2 * o + 2)
                    dve.tensor_tensor(scaled[:, m, 0:S], gates[:, o, :], gates[:, 8 + o, :], ALU.add)\
                        .then_inc(s["m_whole"], 1)
                    dve.wait_ge(s["m_high_"], o + 1)
                    dve.tensor_tensor(h_low[:, o, META:L], scaled[:, m, 0:S], h_high[:, o, META:L].bitcast(F32),
                                      ALU.subtract).then_inc(s["m_low_"], 1)

            def add_out(n0, banks, done, i, lag):
                for m in range(4):
                    dve.wait_ge(strip_used, i * 4 + (n0 + m + 1))
                    xm = x_t[:, bass.ds(i * 4 + m, 1), :]
                    dve.tensor_tensor(xm, xm, ps[:, banks[m], :], ALU.add).then_inc(s[done], 1)
                    make_high(dve, n0 + m + lag, i * 4)

            with dve.Fori(0, 2) as i:
                add_out(N_OUT, [0, 1, 2, 3], "o_added", i, 3)

            after(dve, "out")
            norm_dve(dve, 2, xs, V_FFN, S, hh, hl)

            after(dve, "norm2")
            with dve.Fori(0, 11) as i:
                for m in range(4):
                    ct = m % 2 + FT * (m // 2)
                    dve.wait_ge(s["z_first"], i * 4 + (m + 1))
                    dve.scalar_tensor_tensor(z[:, m, 1:S], ps[:, m, 0:S - 1],
                                             cv[:, bass.ds(i * 2 + (C_CONV + 2 * FT + ct), 1)], z[:, m, 1:S],
                                             ALU.mult, ALU.add).then_inc(s["z_mid"], 1)
                    dve.wait_ge(s["z_mid"], i * 4 + (m + 1))
                    dve.scalar_tensor_tensor(z[:, m, 2:S], ps[:, m, 0:S - 2],
                                             cv[:, bass.ds(i * 2 + (C_CONV + ct), 1)], z[:, m, 2:S],
                                             ALU.mult, ALU.add).then_inc(s["z_done"], 1)
                    make_high(dve, N_UP + m + 3, i * 4)
                    if m >= 2:
                        g = m - 2
                        dve.wait_ge(s["z_done"], i * 4 + (m + 1))
                        dve.wait_ge(s["z_silu"], i * 2 + (g + 1))
                        dve.tensor_tensor(zg[:, g, :], z[:, g, :], z[:, m, :], ALU.mult).then_inc(s["z_gated"], 1)
                for g in range(2):
                    dve.wait_ge(s["z_high"], i * 2 + (g + 1))
                    dve.tensor_tensor(m_low[:, bass.ds(i * 2 + g, 1), :], zg[:, g, :],
                                      m_high[:, bass.ds(i * 2 + g, 1), :].bitcast(F32), ALU.subtract)\
                        .then_inc(s["z_low"], 1)

            after(dve, "up")
            with dve.Fori(0, 2) as i:
                for m in range(4):
                    for part in range(3):
                        make_high(dve, N_DOWN + 3 * m + part + 3, i * 12)
                    dve.wait_ge(strip_used, i * 12 + (N_DOWN + 3 * m + 3))
                    dve.tensor_tensor(z[:, m, :], x_t[:, bass.ds(i * 4 + m, 1), :], ps[:, 4 + m, :], ALU.add)\
                        .then_inc(s["d_added"], 1)
                dve.wait_ge(s["d_placed"], i * 4 + 4)

            after(dve, "down")
            norm_dve(dve, 3, xs, V_N2, S, hh, hl)
            after(dve, "norm3")
            for m in range(5):
                make_high(dve, N_LAT + m + 3)
            dve.wait_ge(s["pe_root_part"], 1)
            dve.tensor_copy(halves(k_pe[:]), wide(6)).then_inc(s["pe_part"], 1)
            dve.wait_ge(s["pe_part"], 1)
            dve.wait_ge(s["pe_root_part"], 3)
            dve.scalar_tensor_tensor(k_pe[:], k_pe[:], col(V_KPE), root[:, 0, :],
                                     ALU.mult, ALU.mult).then_inc(s["pe_part"], 1)
            for m in range(2):
                dve.wait_ge(s["lat_root"], m * 2 + 2)
                n = S if m == 0 else L
                for k in range(2):
                    if m:
                        dve.wait_ge(s["lat_low"], 2)
                    else:
                        dve.wait_ge(s["pe_part"], 2)
                    src = ps[:, k, :] if m == 0 else wide(2 + 2 * k)
                    dst = scaled[:, k, 0:n] if m == 0 else halves(scaled[:, k, :])
                    r = root[:, 0, 0:n] if m == 0 else halves(root[:, 0, :])
                    dve.scalar_tensor_tensor(dst, src, col((V_QL, V_KL)[m] + k), r, ALU.mult, ALU.mult)\
                        .then_inc(s["lat_scaled"], 1)
                for k in range(2):
                    dve.wait_ge(s["lat_high"], 2 * m + k + 1)
                    hi, lo = (ql_high, ql_low) if m == 0 else (kl_high, kl_low)
                    dve.tensor_tensor(lo[:, k, :], scaled[:, k, 0:n], hi[:, k, :].bitcast(F32), ALU.subtract)\
                        .then_inc(s["lat_low"], 1)
            dve.wait_ge(s["tables_in"], 32)
            dve.wait_ge(s["pe_turned"], 1)
            dve.wait_ge(s["lat_low"], 4)
            dve.tensor_tensor(k_pe[:], k_pe[:], cos[:], ALU.mult).then_inc(s["pe_part"], 1)
            dve.tensor_tensor(halves(scaled[:, 0, :]), wide(0), halves(sin[:]), ALU.mult).then_inc(s["pe_part"], 1)
            dve.wait_ge(s["pe_part"], 3)
            dve.wait_ge(s["pe_part"], 4)
            dve.tensor_tensor(k_pe[:], k_pe[:], scaled[:, 0, :], ALU.add).then_inc(s["pe_part"], 1)

            after(dve, "lat")

            def m_top(i, c, t):
                dve.wait_ge(s["s_scored"], i * 8 + (4 * c + t + 1))
                dve.tensor_reduce(mm_[:, t % 2, 0:1], wide(0), AX.XY, ALU.max).then_inc(s["s_top"], 1)
                dve.wait_ge(s["s_top"], i * 8 + (4 * c + t + 1))
                dve.tensor_scalar(mm_[:, t % 2, 1:2], mm_[:, t % 2, 0:1], -MLA_SCALE, None, ALU.mult)\
                    .then_inc(s["s_neg"], 1)

            def m_scale(i, c, t):
                dve.wait_ge(s["s_exp"], i * 8 + (4 * c + t + 1))
                dve.reciprocal(mm_[:, t % 2, 3:4], mm_[:, t % 2, 2:3]).then_inc(s["s_inv"], 1)
                dve.wait_ge(s["s_inv"], i * 8 + (4 * c + t + 1))
                dve.tensor_scalar(me[:, t % 2, :], me[:, t % 2, :], mm_[:, t % 2, 3:4], None, ALU.mult)\
                    .then_inc(s["s_probs"], 1)

            def m_copy(i, c, t):
                dve.wait_ge(s["s_turned"], i * 8 + (4 * c + t + 1))
                dve.tensor_copy(mp[0:META, 4 * P:5 * P], ps[0:META, 1, 3 * P:4 * P]).then_inc(s["s_copied_b"], 1)

            def m_keep(i, c, item):
                dve.wait_ge(s["p_sq"], i * 6 + (3 * c + item + 1))
                dst, src = ((q_pe[:, c % 2, :], ps[0:64, 7, :]), (halves(kn[:, c % 2, :]), wide(2)),
                            (qn[:, c % 2, :], ps[:, 7, :]))[item]
                dve.tensor_copy(dst, src).then_inc(s["p_kept"], 1)

            def m_normed(i, c, item):
                dve.wait_ge(s["p_root"], i * 12 + (6 * c + 2 * item + 2))
                dst, gain, r = ((q_pe[:, c % 2, :], cv[0:64, C_V + V_QPE:C_V + V_QPE + 1], root[0:64, 0, 0:S]),
                                (kn[:, c % 2, :], col(V_KN), root[:, 1, :]),
                                (qn[:, c % 2, :], col(V_QN), root[:, 0, 0:S]))[item]
                dve.scalar_tensor_tensor(dst, dst, gain, r, ALU.mult, ALU.mult).then_inc(s["p_normed"], 1)

            def m_rope(i, c):
                q = q_pe[:, c % 2, :]
                turned = scaled[0:64, 1, 0:S]
                dve.wait_ge(s["qr_turned"], i * 2 + (c + 1))
                dve.tensor_tensor(turned, ps[0:64, 7, :], sin[0:64, META:L], ALU.mult).then_inc(s["qr_part"], 1)
                dve.tensor_tensor(q, q, cos[0:64, META:L], ALU.mult).then_inc(s["qr_part"], 1)
                dve.wait_ge(s["qr_part"], i * 6 + (3 * c + 2))
                dve.tensor_tensor(q, q, turned, ALU.add).then_inc(s["qr_part"], 1)

            def m_gate(i, c):
                dve.wait_ge(s["mg_part"], i * 6 + (3 * c + 3))
                dve.tensor_tensor(gm[:, c % 2, :], ps[:, 5, :], m_sig[:], ALU.mult).then_inc(s["mg_done"], 1)

            def m_gated(i, c):
                dve.wait_ge(s["s_summed"], i * 8 + (4 * c + 4))
                dve.wait_ge(s["mg_done"], i * 2 + (c + 1))
                dve.tensor_tensor(y_f[:], ps[:, 6, :], gm[:, c % 2, :], ALU.mult).then_inc(s["s_y"], 1)

            def m_parts(i, c):
                hi = y_high[:, bass.ds(i * 2 + c, 1), :]
                dve.wait_ge(s["s_y"], i * 2 + (c + 1))
                dve.tensor_copy(hi, y_f[:]).then_inc(s["s_high"], 1)
                dve.wait_ge(s["s_high"], i * 2 + (c + 1))
                dve.tensor_tensor(y_low[:, bass.ds(i * 2 + c, 1), :], y_f[:], hi.bitcast(F32), ALU.subtract)\
                    .then_inc(s["s_low"], 1)

            def head(i, c, more=True):
                ahead = N_MLA + 2 * (c + 1) + 3
                m_top(i, c, 0)
                m_gate(i, c)
                m_scale(i, c, 0)
                if c:
                    m_parts(i, c - 1)
                m_copy(i, c, 0)
                make_high(dve, ahead if more else N_OM + 3, i * 4 if more else 0)
                if more:
                    m_keep(i, c + 1, 0)
                    m_keep(i, c + 1, 1)
                m_top(i, c, 1)
                m_scale(i, c, 1)
                if more:
                    m_normed(i, c + 1, 0)
                m_copy(i, c, 1)
                if more:
                    m_rope(i, c + 1)
                m_top(i, c, 2)
                if more:
                    m_normed(i, c + 1, 1)
                m_scale(i, c, 2)
                m_copy(i, c, 2)
                if more:
                    m_keep(i, c + 1, 2)
                m_top(i, c, 3)
                if more:
                    make_high(dve, ahead + 1, i * 4)
                m_scale(i, c, 3)
                if more:
                    m_normed(i, c + 1, 2)
                m_copy(i, c, 3)
                m_gated(i, c)

            m_keep(0, 0, 0)
            m_keep(0, 0, 1)
            m_normed(0, 0, 0)
            m_rope(0, 0)
            m_normed(0, 0, 1)
            make_high(dve, N_MLA + 3)
            m_keep(0, 0, 2)
            m_normed(0, 0, 2)
            make_high(dve, N_MLA + 4)
            head(0, 0)
            with dve.Fori(0, 3) as i:
                head(i, 1)
                head(i, 2)
            head(3, 1, more=False)
            m_parts(3, 1)

            for m in range(8):
                dve.wait_ge(strip_used, N_OM + m + 1)
                dve.tensor_tensor(x_t[:, m, :], x_t[:, m, :], ps[:, OM_BANK[m], :], ALU.add)\
                    .then_inc(s["om_added"], 1)
                make_high(dve, N_OM + m + 4)

            after(dve, "om")

            def masked(i, c, t, n):
                w, z_ = META + NA_W[t], c % 2
                if t == 0:
                    dve.wait_ge(s["nb_ready"], i * 18 + (9 * c + 9))
                if n:
                    dve.wait_ge(s["t_scored"], i * 8 + (4 * c + t + 1))
                    make_high(dve, n, i * 8)
                for h in range(2):
                    dve.tensor_tensor_reduce(ne[:, t % 2, h, 0:w], ps[:, h, 0:w],
                                             nb[:, z_, h, NA_OFF[t]:NA_OFF[t] + w], 1.0, -3e38, ALU.add, ALU.max,
                                             nm[:, t % 2, 2, h:h + 1]).then_inc(s["t_masked"], 1)
                dve.wait_ge(s["t_masked"], i * 16 + (8 * c + 2 * t + 2))
                dve.tensor_scalar(nm[:, t % 2, 0, :], nm[:, t % 2, 2, :], -1.0, None, ALU.mult)\
                    .then_inc(s["t_neg"], 1)

            def copy_b(i, c, t):
                dve.wait_ge(s["t_turned"], i * 8 + (4 * c + t + 1))
                if NA_W[t] == 3 * P:
                    dve.tensor_copy(npt[:, 2, :], ps[:, 3, 0:2 * P])
                dve.tensor_copy(npt[0:META, 3, :], ps[0:META, 3, 2 * P:4 * P]).then_inc(s["t_copied_b"], 1)

            def inverse(i, c, t):
                dve.wait_ge(s["t_exp"], i * 16 + (8 * c + 2 * t + 2))
                dve.reciprocal(nm[:, t % 2, 3, :], nm[:, t % 2, 1, :]).then_inc(s["t_inv"], 1)

            def scale(i, c, t):
                dve.wait_ge(s["t_inv"], i * 8 + (4 * c + t + 1))
                dve.wait_ge(s["t_summed"], i * 8 + (4 * c + t + 1))
                for h in range(2):
                    d = slice(h * HD, (h + 1) * HD)
                    dve.tensor_scalar(no[:, t % 2, d], ps[:, 4, d], nm[:, t % 2, 3, h:h + 1], None, ALU.mult)\
                        .then_inc(s["t_out"], 1)

            def gated(i, c, t):
                q = slice(t * P, (t + 1) * P)
                dve.wait_ge(s["t_back"], i * 8 + (4 * c + t + 1))
                dve.tensor_tensor(ny[:, t % 2, :], ps[:, 4, 0:P], ng[:, c % 2, q], ALU.mult).then_inc(s["t_y"], 1)
                dve.wait_ge(s["t_y"], i * 8 + (4 * c + t + 1))
                hi = y_high[:, bass.ds(i * 2 + c, 1), q]
                y = ny[:, t % 2:t % 2 + 1, :]
                dve.tensor_copy(hi, y).then_inc(s["t_high"], 1)
                dve.wait_ge(s["t_high"], i * 8 + (4 * c + t + 1))
                dve.tensor_tensor(y_low[:, bass.ds(i * 2 + c, 1), q], y, hi.bitcast(F32), ALU.subtract)\
                    .then_inc(s["t_low"], 1)

            def keep(i, c, m):
                dve.wait_ge(s["q_sq"], i * 4 + (2 * c + m + 1))
                if m == 0:
                    dve.tensor_copy(halves(nk[:, c % 2, :]), wide(5)).then_inc(s["q_kept"], 1)
                else:
                    dve.tensor_copy(nq[:, c % 2, :], ps[:, 7, :]).then_inc(s["q_kept"], 1)

            def normed(i, c, m):
                dst = (nk, nq)[m][:, c % 2, :]
                dve.wait_ge(s["q_root"], i * 8 + (4 * c + 2 * m + 2))
                dve.scalar_tensor_tensor(dst, dst, (col(V_NK), nq_gain[:, 0:1])[m], root[:, m, 0:(L, S)[m]],
                                         ALU.mult, ALU.mult).then_inc(s["q_normed"], 1)

            def gate(i, c):
                dve.wait_ge(s["g_part"], i * 6 + (3 * c + 3))
                dve.tensor_tensor(ng[:, c % 2, :], ps[:, 7, :], sig[:], ALU.mult).then_inc(s["g_done"], 1)

            def pair(i, c, more=True):
                if c:
                    inverse(i, c - 1, 3)
                    scale(i, c - 1, 3)
                    gate(i, c)
                for t in range(4):
                    if more and t >= 2:
                        normed(i, c + 1, t - 2)
                    if not more and t == 0:
                        gated(i, c - 1, 3)
                    copy_b(i, c, t)
                    if more:
                        if t:
                            gated(i, c, t - 1)
                        elif c:
                            gated(i, c - 1, 3)
                        if t < 2:
                            keep(i, c + 1, t)
                        if t < 3:
                            masked(i, c, t + 1, N_NA + 4 * (c + 1) + t + 4)
                            inverse(i, c, t)
                            scale(i, c, t)
                        else:
                            masked(i, c + 1, 0, N_NA + 4 * (c + 1) + t + 4)
                    else:
                        if t < 3:
                            dve.wait_ge(s["t_scored"], i * 8 + (4 * c + t + 2))
                        inverse(i, c, t)
                        if t < 3:
                            masked(i, c, t + 1, None)
                        if t:
                            gated(i, c, t - 1)
                        if t < 3:
                            scale(i, c, t)

            keep(0, 0, 0)
            keep(0, 0, 1)
            make_high(dve, N_NA + 4)
            normed(0, 0, 0)
            normed(0, 0, 1)
            make_high(dve, N_NA + 5)
            make_high(dve, N_NA + 6)
            gate(0, 0)
            masked(0, 0, 0, N_NA + 7)
            pair(0, 0)
            with dve.Fori(0, 3) as i:
                pair(i, 1)
                pair(i, 2)
            pair(3, 1, more=False)
            scale(3, 1, 3)
            gated(3, 1, 3)
            for m in range(8):
                dve.wait_ge(strip_used, N_ON + m + 1)
                dve.tensor_tensor(x_t[:, m, :], x_t[:, m, :], ps[:, (m - EARLY) % 8, :], ALU.add)\
                    .then_inc(s["on_added"], 1)
                make_high(dve, N_ON + m + 4)

            for t in (1, 3):
                dve.wait_ge(s["out_turned"], 4 + t + 1)
                dve.tensor_copy(y_tok[:, t, 512:D], ps[:, OUT_BANK[1][t], :]).then_inc(s["out_right"], 1)


_INS = ["x", "mix_norm", "w_in", "q_norm", "k_norm", "sinks", "sgu_norm", "w_s", "b_s", "w_oa", "w_ob", "w_out",
        "ffn_norm", "w_up", "conv_w", "conv_b", "w_down", "meta_tokens_2", "norm_w_2", "w_in_2",
        "q_lat_norm_w_2", "kv_lat_norm_w_2", "w_uq_2", "w_ukv_2", "mla_qn_w_2", "mla_qpe_w_2", "mla_kn_w_2",
        "mla_kpe_w_2", "na_q_norm_w_2", "na_k_norm_w_2", "na_meta_bias_2", "w_out_2"]


def _grouped():
    g, r, c = np.meshgrid(np.arange(CG), np.arange(8), np.arange(16), indexing="ij")
    return (r * GW + g * 16 + c).ravel()


def _constants():
    f = np.float32
    i = np.arange(P)
    rot = np.zeros((P, P), f)
    for b in (0, 64):
        for d in range(32):
            rot[b + d + 32, b + d] = -1
            rot[b + d, b + d + 32] = 1
    pos = np.concatenate([np.arange(META), META + _grouped()]).astype(f)
    inv = (f(10000.0) ** (-(np.arange(0, 64, 2, dtype=f) / f(64)))).astype(f)
    ang = (pos[None, :] * np.tile(inv, 4)[:, None]).astype(f)
    gap = i[:, None] + P - np.arange(2 * P)[None, :]
    dist = np.where((gap >= 0) & (gap < 128), -gap, -1e33).astype(f)
    slope = np.broadcast_to(np.exp2(-(np.arange(ATT_H) + 1.0)).astype(f), (P, ATT_H))
    cq = i % 16
    ck = np.arange(3 * P) % 16 + np.arange(3 * P) // P * 16

    def window(first, at, n):
        c0 = np.clip(at + cq - 8, 0, GW - 16)
        k = first + ck[:n]
        return np.where((k[None, :] >= c0[:, None]) & (k[None, :] < c0[:, None] + 16), 0, -1e30)

    mask = np.concatenate([window(0, 16, 3 * P), window(0, 0, 2 * P), window(32, 48, 2 * P)], 1).astype(f)
    return {"c_ident": np.eye(P, dtype=f), "c_blocks": np.kron(np.eye(2), np.ones((64, 64))).astype(f),
            "c_rot": rot, "c_cos": np.cos(ang).astype(f), "c_sin": np.sin(ang).astype(f), "c_dist": dist,
            "c_slope": slope, "c_mask": mask}


def _relative():
    q, k = np.arange(P), np.arange(3 * P)
    dr = (k % P // 16)[None, :] - (q // 16)[:, None] + 7
    dc = (k // P * 16 - 16 + k % 16)[None, :] - (q % 16)[:, None] + 15
    return dr, np.clip(dc, 0, 30)


def kernel(**inputs):
    import concourse.bacc as _bacc
    from concourse.bass_utils import run_bass_kernel_spmd as _run

    nc = _bacc.Bacc("TRN2", target_bir_lowering=False, num_devices=1)
    feeds = {n: inputs[n] for n in _INS}
    dr, dc = _relative()
    feeds["rel_bias"] = np.asarray(inputs["na_rel_bias_2"])[0][:, dr, dc]
    feeds.update(_constants())
    arrays, args = {}, []
    for name, a in feeds.items():
        a = np.ascontiguousarray(a)
        arrays[f"in_{name}_dram"] = a
        args.append(nc.dram_tensor(f"in_{name}_dram", a.shape, mybir.dt.from_np(a.dtype), kind="ExternalInput").ap())
    args.append(nc.dram_tensor("out_0_dram", (1, S, D), F32, kind="ExternalOutput").ap())
    program(nc, *args)
    r = _run(nc, [arrays], core_ids=[0])
    return r.results[0]["out_0_dram"]
```
